# Optimizing a Trainium2 kernel written in Bass

```python
import math
import jax, jax.numpy as jnp
from jax import lax
import numpy as np

D_MODEL = 1024
BATCH = 1
SEQ = 512
DEPTH = 1

N_META = 16
EPS = 1e-6
D_FF = 2816
MLA_HEADS = 8
MLA_Q_RANK = 256
MLA_KV_RANK = 128
MLA_NOPE = 64
MLA_ROPE = 32
MLA_V = 64
ROPE_THETA = 10000.0
Q_BLOCK = 128
GDN_HEADS = 8
GDN_DK = 64
GDN_DV = 64
CONV_K = 4
CHUNK = 64
SPLITS = (MLA_Q_RANK, MLA_KV_RANK, MLA_ROPE,
          GDN_HEADS * GDN_DK, GDN_HEADS * GDN_DK, GDN_HEADS * GDN_DV,
          GDN_HEADS, GDN_HEADS, GDN_HEADS * GDN_DV,
          D_MODEL, D_MODEL)
D_IN = sum(SPLITS)
GDN_CONV_CH = 2 * GDN_HEADS * GDN_DK + GDN_HEADS * GDN_DV


def rmsnorm(x, w):
    x32 = x.astype(jnp.float32)
    y = x32 * lax.rsqrt(jnp.mean(x32 * x32, axis=-1, keepdims=True) + EPS)
    return (y * w.astype(jnp.float32)).astype(x.dtype)

def swiglu(x, w_gate, w_up, w_down):
    return (jax.nn.silu(x @ w_gate) * (x @ w_up)) @ w_down

def rope_tables(length):
    pos = jnp.arange(length, dtype=jnp.float32)
    inv = ROPE_THETA ** (-jnp.arange(0, MLA_ROPE, 2, dtype=jnp.float32) / MLA_ROPE)
    ang = pos[:, None] * inv[None, :]
    return jnp.cos(ang), jnp.sin(ang)

def apply_rope(x, cos, sin):
    half = x.shape[-1] // 2
    x1 = x[..., :half].astype(jnp.float32)
    x2 = x[..., half:].astype(jnp.float32)
    out = jnp.concatenate([x1 * cos - x2 * sin, x2 * cos + x1 * sin], axis=-1)
    return out.astype(x.dtype)

def mla(c_q_raw, c_kv_raw, k_rope_raw, q_norm, w_uq, kv_norm, w_ukv):
    b, length, _ = c_q_raw.shape
    q = (rmsnorm(c_q_raw, q_norm) @ w_uq).reshape(b, length, MLA_HEADS, MLA_NOPE + MLA_ROPE)
    kv = (rmsnorm(c_kv_raw, kv_norm) @ w_ukv).reshape(b, length, MLA_HEADS, MLA_NOPE + MLA_V)
    q_nope, q_rope = q[..., :MLA_NOPE], q[..., MLA_NOPE:]
    k_nope, v = kv[..., :MLA_NOPE], kv[..., MLA_NOPE:]
    cos, sin = rope_tables(length)
    q_rope = apply_rope(q_rope, cos[:, None, :], sin[:, None, :])
    k_rope = apply_rope(k_rope_raw, cos, sin)
    scale = (MLA_NOPE + MLA_ROPE) ** -0.5
    n_blk = -(-length // Q_BLOCK)
    l_pad = n_blk * Q_BLOCK

    def to_blocks(t):
        t = jnp.pad(t, ((0, 0), (0, l_pad - length), (0, 0), (0, 0)))
        return t.reshape(b, n_blk, Q_BLOCK, MLA_HEADS, t.shape[-1]).transpose(1, 0, 2, 3, 4)

    qn_blocks = to_blocks(q_nope)
    qr_blocks = to_blocks(q_rope)
    starts = jnp.arange(n_blk, dtype=jnp.int32) * Q_BLOCK
    k_pos = jnp.arange(length, dtype=jnp.int32)

    def attend_block(args):
        qn_b, qr_b, start = args
        s = (jnp.einsum('bqhd,bkhd->bhqk', qn_b, k_nope)
             + jnp.einsum('bqhd,bkd->bhqk', qr_b, k_rope)).astype(jnp.float32) * scale
        q_pos = start + jnp.arange(Q_BLOCK, dtype=jnp.int32)
        causal = k_pos[None, :] <= q_pos[:, None]
        s = jnp.where(causal, s, -jnp.inf)
        p = jax.nn.softmax(s, axis=-1).astype(v.dtype)
        return jnp.einsum('bhqk,bkhd->bqhd', p, v)

    o = lax.map(attend_block, (qn_blocks, qr_blocks, starts))
    o = o.transpose(1, 0, 2, 3, 4).reshape(b, l_pad, MLA_HEADS * MLA_V)
    return o[:, :length]

def short_conv(x, w):
    ch = x.shape[-1]
    return lax.conv_general_dilated(
        x, w[:, None, :].astype(x.dtype), window_strides=(1,),
        padding=[(CONV_K - 1, 0)], dimension_numbers=('NWC', 'WIO', 'NWC'),
        feature_group_count=ch)

def l2norm(x):
    return x * lax.rsqrt(jnp.sum(x * x, axis=-1, keepdims=True) + EPS)

def gated_deltanet(q_raw, k_raw, v_raw, b_raw, a_raw, z_raw, conv_w, a_log, dt_bias, gdn_norm):
    b, length, _ = q_raw.shape
    dtype = q_raw.dtype
    qkv = jax.nn.silu(short_conv(jnp.concatenate([q_raw, k_raw, v_raw], axis=-1), conv_w))
    nq = GDN_HEADS * GDN_DK
    q = qkv[..., :nq].reshape(b, length, GDN_HEADS, GDN_DK).astype(jnp.float32)
    k = qkv[..., nq:2 * nq].reshape(b, length, GDN_HEADS, GDN_DK).astype(jnp.float32)
    v = qkv[..., 2 * nq:].reshape(b, length, GDN_HEADS, GDN_DV).astype(jnp.float32)
    q = l2norm(q) * (GDN_DK ** -0.5)
    k = l2norm(k)
    beta = jax.nn.sigmoid(b_raw.astype(jnp.float32))
    g = -jnp.exp(a_log.astype(jnp.float32)) * jax.nn.softplus(
        a_raw.astype(jnp.float32) + dt_bias.astype(jnp.float32))

    pad_front = (-N_META) % CHUNK
    lc = pad_front + length
    n_chunk = lc // CHUNK

    def to_chunks(t):
        t = jnp.pad(t, ((0, 0), (pad_front, 0)) + ((0, 0),) * (t.ndim - 2))
        t = t.reshape((b, n_chunk, CHUNK) + t.shape[2:])
        return jnp.moveaxis(t, 3, 1)

    qc, kc, vc = to_chunks(q), to_chunks(k), to_chunks(v)
    bc = to_chunks(beta)
    gc = jnp.cumsum(to_chunks(g), axis=-1)
    tri_incl = jnp.tril(jnp.ones((CHUNK, CHUNK), dtype=bool))
    tri_strict = jnp.tril(jnp.ones((CHUNK, CHUNK), dtype=bool), -1)
    diff = gc[..., :, None] - gc[..., None, :]
    decay = jnp.exp(jnp.where(tri_incl, diff, -jnp.inf))
    kb = kc * bc[..., None]
    lmat = jnp.where(tri_strict, jnp.einsum('bhncd,bhnsd->bhncs', kb, kc) * decay, 0.0)
    eye = jnp.eye(CHUNK, dtype=jnp.float32)
    tmat = lax.linalg.triangular_solve(eye + lmat, jnp.broadcast_to(eye, lmat.shape),
                                       left_side=True, lower=True)
    u_c = tmat @ (vc * bc[..., None])
    w_c = tmat @ (kb * jnp.exp(gc)[..., None])
    intra = jnp.einsum('bhncd,bhnsd->bhncs', qc, kc) * decay

    def step(state, inp):
        q_i, k_i, u_i, w_i, g_i, a_i = inp
        v_new = u_i - w_i @ state
        o_i = (q_i * jnp.exp(g_i)[..., None]) @ state + a_i @ v_new
        g_last = g_i[..., -1]
        k_dec = k_i * jnp.exp(g_last[..., None] - g_i)[..., None]
        state = state * jnp.exp(g_last)[..., None, None] + jnp.einsum('bhcd,bhce->bhde', k_dec, v_new)
        return state, o_i

    xs = tuple(jnp.moveaxis(t, 2, 0) for t in (qc, kc, u_c, w_c, gc, intra))
    s0 = jnp.zeros((b, GDN_HEADS, GDN_DK, GDN_DV), jnp.float32)
    _, o = lax.scan(step, s0, xs)
    o = o.transpose(1, 0, 3, 2, 4).reshape(b, lc, GDN_HEADS, GDN_DV)[:, pad_front:]
    z = z_raw.reshape(b, length, GDN_HEADS, GDN_DV).astype(jnp.float32)
    o = rmsnorm(o, gdn_norm) * jax.nn.silu(z)
    return o.reshape(b, length, GDN_HEADS * GDN_DV).astype(dtype)

def _w(k, shape, fan_in):
    return jax.random.normal(k, shape, jnp.float32) * (fan_in ** -0.5)

def _gain(k, shape):
    return 1.0 + 0.02 * jax.random.normal(k, shape, jnp.float32)

def first_inputs(seed: int = 0) -> dict:
    key = jax.random.key(seed)
    ks = jax.random.split(key, 32)
    d = D_MODEL
    dt = jnp.exp(jax.random.uniform(ks[15], (DEPTH, GDN_HEADS), jnp.float32,
                                    minval=math.log(1e-3), maxval=math.log(1e-1)))
    return {
        'x': jax.random.normal(ks[0], (BATCH, SEQ, d), jnp.float32),
        'meta_tokens': jax.random.normal(ks[1], (N_META, d), jnp.float32),
        'ffn1_norm': _gain(ks[2], (DEPTH, d)),
        'ffn1_w_gate': _w(ks[3], (DEPTH, d, D_FF), d),
        'ffn1_w_up': _w(ks[4], (DEPTH, d, D_FF), d),
        'ffn1_w_down': _w(ks[5], (DEPTH, D_FF, d), D_FF),
        'mix_norm': _gain(ks[6], (DEPTH, d)),
        'w_in': _w(ks[7], (DEPTH, d, D_IN), d),
        'q_norm': _gain(ks[8], (DEPTH, MLA_Q_RANK)),
        'w_uq': _w(ks[9], (DEPTH, MLA_Q_RANK, MLA_HEADS * (MLA_NOPE + MLA_ROPE)), MLA_Q_RANK),
        'kv_norm': _gain(ks[10], (DEPTH, MLA_KV_RANK)),
        'w_ukv': _w(ks[11], (DEPTH, MLA_KV_RANK, MLA_HEADS * (MLA_NOPE + MLA_V)), MLA_KV_RANK),
        'w_mla_o': _w(ks[12], (DEPTH, MLA_HEADS * MLA_V, d), MLA_HEADS * MLA_V),
        'conv_w': _w(ks[13], (DEPTH, CONV_K, GDN_CONV_CH), CONV_K),
        'a_log': jnp.log(jax.random.uniform(ks[14], (DEPTH, GDN_HEADS), jnp.float32, minval=1.0, maxval=16.0)),
        'dt_bias': dt + jnp.log(-jnp.expm1(-dt)),
        'gdn_norm': _gain(ks[16], (DEPTH, GDN_DV)),
        'w_gdn_o': _w(ks[17], (DEPTH, GDN_HEADS * GDN_DV, d), GDN_HEADS * GDN_DV),
        'w_out': _w(ks[18], (DEPTH, d, d), d),
        'ffn2_norm': _gain(ks[19], (DEPTH, d)),
        'ffn2_w_gate': _w(ks[20], (DEPTH, d, D_FF), d),
        'ffn2_w_up': _w(ks[21], (DEPTH, d, D_FF), d),
        'ffn2_w_down': _w(ks[22], (DEPTH, D_FF, d), D_FF),
        'final_norm': _gain(ks[23], (d,)),
    }

def first_block(x, meta_tokens, ffn1_norm, ffn1_w_gate, ffn1_w_up, ffn1_w_down, mix_norm, w_in,
              q_norm, w_uq, kv_norm, w_ukv, w_mla_o, conv_w, a_log, dt_bias, gdn_norm, w_gdn_o,
              w_out, ffn2_norm, ffn2_w_gate, ffn2_w_up, ffn2_w_down, final_norm):
    b = x.shape[0]
    meta = jnp.broadcast_to(meta_tokens[None].astype(x.dtype), (b, N_META, D_MODEL))
    h = jnp.concatenate([meta, x], axis=1)
    split_points = [int(p) for p in np.cumsum(SPLITS)[:-1]]
    for l in range(DEPTH):
        h = h + 0.5 * swiglu(rmsnorm(h, ffn1_norm[l]), ffn1_w_gate[l], ffn1_w_up[l], ffn1_w_down[l])
        u = rmsnorm(h, mix_norm[l])
        (c_q, c_kv, k_rope, g_q, g_k, g_v, g_b, g_a, g_z,
         gate_mla, gate_gdn) = jnp.split(u @ w_in[l], split_points, axis=-1)
        y_mla = mla(c_q, c_kv, k_rope, q_norm[l], w_uq[l], kv_norm[l], w_ukv[l]) @ w_mla_o[l]
        y_gdn = gated_deltanet(g_q, g_k, g_v, g_b, g_a, g_z, conv_w[l], a_log[l], dt_bias[l],
                               gdn_norm[l]) @ w_gdn_o[l]
        merged = jax.nn.sigmoid(gate_mla) * y_mla + jax.nn.sigmoid(gate_gdn) * y_gdn
        h = h + merged @ w_out[l]
        h = h + 0.5 * swiglu(rmsnorm(h, ffn2_norm[l]), ffn2_w_gate[l], ffn2_w_up[l], ffn2_w_down[l])
    return rmsnorm(h, final_norm)[:, N_META:]


HEAD_DIM = 64
D_MIX = D_MODEL
A_HEADS = D_MIX // 2 // HEAD_DIM
A_KV = A_HEADS // 4
B_HEADS = D_MIX // 2 // HEAD_DIM
B_KV = B_HEADS // 4
D_A = A_HEADS * HEAD_DIM
D_B = B_HEADS * HEAD_DIM
KV_A = A_KV * HEAD_DIM
KV_B = B_KV * HEAD_DIM
N_HEADS_TOTAL = A_HEADS + B_HEADS
SWA_WINDOW = 128
ATTN_BLOCK = 128
CMP_LEN = 32
CMP_STRIDE = 16
CMP_HIDDEN = 256
SEL_LEN = 64
SEL_TOPK = 16
NSA_WINDOW = 512
NSA_Q_CHUNK = 32
N_NSA_BRANCHES = 3
N_BUCKETS = 32
MAX_DISTANCE = 128
FORCE_BONUS = 1e4
PROJ_SIZES = (D_A, KV_A, KV_A, D_A,
              D_B, KV_B, KV_B, KV_B, KV_B, KV_B, KV_B, D_B, B_HEADS * N_NSA_BRANCHES)
D_PROJ = sum(PROJ_SIZES)


def _split_points():
    pts, acc = [], 0
    for s in PROJ_SIZES[:-1]:
        acc += s
        pts.append(acc)
    return pts

def rms_norm(x, gain):
    xf = x.astype(jnp.float32)
    y = xf * lax.rsqrt(jnp.mean(xf * xf, -1, keepdims=True) + EPS)
    return (y * gain.astype(jnp.float32)).astype(x.dtype)

def qk_norm(t, gain):
    tf = t.astype(jnp.float32)
    return tf * lax.rsqrt(jnp.mean(tf * tf, -1, keepdims=True) + EPS) * gain.astype(jnp.float32)

def t5_bucket(dist):
    n = jnp.maximum(dist, 0)
    max_exact = N_BUCKETS // 2
    nf = jnp.maximum(n, 1).astype(jnp.float32)
    large = max_exact + (jnp.log(nf / max_exact) / math.log(MAX_DISTANCE / max_exact)
                         * (N_BUCKETS - max_exact)).astype(jnp.int32)
    large = jnp.minimum(large, N_BUCKETS - 1)
    return jnp.where(n < max_exact, n, large)

def masked_softmax(logits, mask, sink=None):
    z = jnp.where(mask, logits, -jnp.inf)
    m = jnp.max(z, -1, keepdims=True)
    if sink is not None:
        m = jnp.maximum(m, sink)
    m = jnp.where(jnp.isfinite(m), m, 0.0)
    e = jnp.where(mask, jnp.exp(z - m), 0.0)
    denom = jnp.sum(e, -1, keepdims=True)
    if sink is not None:
        denom = denom + jnp.exp(sink - m)
    return e / jnp.maximum(denom, 1e-30)

def banded_gqa(q, k, v, window, head_bias, sinks):
    Bn, S, H, D = q.shape
    G = k.shape[2]
    R = H // G
    nblk = S // ATTN_BLOCK
    span = window + ATTN_BLOCK
    kp = jnp.pad(k.astype(jnp.float32), ((0, 0), (window, 0), (0, 0), (0, 0)))
    vp = jnp.pad(v.astype(jnp.float32), ((0, 0), (window, 0), (0, 0), (0, 0)))
    qb = q.reshape(Bn, nblk, ATTN_BLOCK, G, R, D).transpose(1, 0, 2, 3, 4, 5)
    hb = head_bias.astype(jnp.float32)
    sink = None if sinks is None else sinks.astype(jnp.float32).reshape(G, R, 1, 1)
    q_off = jnp.arange(ATTN_BLOCK)
    k_off = jnp.arange(span)

    def block(args):
        qi, i = args
        start = i * ATTN_BLOCK
        kb = lax.dynamic_slice_in_dim(kp, start, span, axis=1)
        vb = lax.dynamic_slice_in_dim(vp, start, span, axis=1)
        t = start + q_off
        s = start - window + k_off
        dist = t[:, None] - s[None, :]
        mask = (dist >= 0) & (dist < window) & (s[None, :] >= 0)
        bias = hb[t5_bucket(dist)].reshape(ATTN_BLOCK, span, G, R).transpose(2, 3, 0, 1)
        logits = jnp.einsum('btgrd,bsgd->bgrts', qi, kb) + bias
        p = masked_softmax(logits, mask, sink)
        return jnp.einsum('bgrts,bsgd->btgrd', p, vb)

    out = lax.map(block, (qb, jnp.arange(nblk)))
    return out.transpose(1, 0, 2, 3, 4, 5).reshape(Bn, S, H, D)

def compress_blocks(t, pos, w1, w2):
    Bn, S, G, D = t.shape
    nc = (S - CMP_LEN) // CMP_STRIDE + 1
    idx = jnp.arange(nc)[:, None] * CMP_STRIDE + jnp.arange(CMP_LEN)[None, :]
    blocks = t[:, idx] + pos[None, None, :, None, :]
    flat = blocks.transpose(0, 1, 3, 2, 4).reshape(Bn, nc, G, CMP_LEN * D)
    return jax.nn.silu(flat @ w1) @ w2

def nsa_cmp_sel(q, k_cmp, v_cmp, k_sel, v_sel, head_bias):
    Bn, S, H, D = q.shape
    G = k_sel.shape[2]
    R = H // G
    nc = k_cmp.shape[1]
    ns = S // SEL_LEN
    topk = min(SEL_TOPK, ns)
    qc_len = NSA_Q_CHUNK
    nch = S // qc_len
    kc = k_cmp.astype(jnp.float32)
    vc = v_cmp.astype(jnp.float32)
    ks_b = k_sel.astype(jnp.float32).reshape(Bn, ns, SEL_LEN, G, D).transpose(0, 3, 1, 2, 4)
    vs_b = v_sel.astype(jnp.float32).reshape(Bn, ns, SEL_LEN, G, D).transpose(0, 3, 1, 2, 4)
    c_lo = jnp.arange(nc) * CMP_STRIDE
    c_end = c_lo + CMP_LEN - 1
    s_lo = jnp.arange(ns) * SEL_LEN
    overlap = jnp.clip(jnp.minimum(c_lo[:, None] + CMP_LEN, s_lo[None, :] + SEL_LEN)
                       - jnp.maximum(c_lo[:, None], s_lo[None, :]), 0, None).astype(jnp.float32) / CMP_LEN
    tbl = head_bias.astype(jnp.float32).reshape(N_BUCKETS, G, R).transpose(1, 0, 2)
    g_idx = jnp.arange(G)[None, :, None, None]
    blk = jnp.arange(ns)
    gather = jax.vmap(jax.vmap(lambda kb, ix: kb[ix]))
    qch = q.reshape(Bn, nch, qc_len, G, R, D).transpose(1, 0, 2, 3, 4, 5)

    def chunk(args):
        qi, i = args
        t = i * qc_len + jnp.arange(qc_len)
        logits_c = jnp.einsum('btgrd,bngd->bgrtn', qi, kc)
        p_c = masked_softmax(logits_c, c_end[None, :] <= t[:, None])
        o_cmp = jnp.einsum('bgrtn,bngd->btgrd', p_c, vc)
        imp = jnp.einsum('bgrtn,nj->bgtj', p_c, overlap)
        cur = t // SEL_LEN
        valid = blk[None, :] <= cur[:, None]
        forced = (blk[None, :] == 0) | (blk[None, :] == cur[:, None]) | (blk[None, :] == cur[:, None] - 1)
        score = jnp.where(valid, imp + jnp.where(forced, FORCE_BONUS, 0.0), -jnp.inf)
        _, sel = lax.top_k(score, topk)
        kg = gather(ks_b, sel).reshape(Bn, G, qc_len, topk * SEL_LEN, D)
        vg = gather(vs_b, sel).reshape(Bn, G, qc_len, topk * SEL_LEN, D)
        spos = (sel[..., None] * SEL_LEN + jnp.arange(SEL_LEN)).reshape(Bn, G, qc_len, topk * SEL_LEN)
        dist = t[None, None, :, None] - spos
        bias = tbl[g_idx, t5_bucket(dist)].transpose(0, 1, 4, 2, 3)
        logits_s = jnp.einsum('btgrd,bgtld->bgrtl', qi, kg) + bias
        p_s = masked_softmax(logits_s, (dist >= 0)[:, :, None])
        o_sel = jnp.einsum('bgrtl,bgtld->btgrd', p_s, vg)
        return o_cmp, o_sel

    o_cmp, o_sel = lax.map(chunk, (qch, jnp.arange(nch)))
    o_cmp = o_cmp.transpose(1, 0, 2, 3, 4, 5).reshape(Bn, S, H, D)
    o_sel = o_sel.transpose(1, 0, 2, 3, 4, 5).reshape(Bn, S, H, D)
    return o_cmp, o_sel

def hybrid_layer(x, c, w_ada, b_ada, norm_gain, w_in, b_nsa_gate, q_gain_a, k_gain_a, sinks,
                 q_gain_b, k_gain_cmp, k_gain_sel, k_gain_win, cmp_pos_k, cmp_pos_v,
                 w_cmp_k1, w_cmp_k2, w_cmp_v1, w_cmp_v2, w_out, rel_bias):
    Bn, S, _ = x.shape
    qscale = HEAD_DIM ** -0.5
    mod = jax.nn.silu(c) @ w_ada + b_ada
    shift, scale, gate = jnp.split(mod, 3, axis=-1)
    h = rms_norm(x, norm_gain) * (1 + scale[:, None, :]) + shift[:, None, :]
    proj = h @ w_in
    (q_a, k_a, v_a, z_a, q_b, kc, vc, ks, vs, kw, vw, z_b, g_b) = jnp.split(proj, _split_points(), axis=-1)
    heads = lambda t, n: t.reshape(Bn, S, n, HEAD_DIM)

    qa = qk_norm(heads(q_a, A_HEADS), q_gain_a) * qscale
    ka = qk_norm(heads(k_a, A_KV), k_gain_a)
    o_a = banded_gqa(qa, ka, heads(v_a, A_KV), SWA_WINDOW, rel_bias[:, :A_HEADS], sinks)

    bias_b = rel_bias[:, A_HEADS:]
    qb = qk_norm(heads(q_b, B_HEADS), q_gain_b) * qscale
    k_cmp = qk_norm(compress_blocks(heads(kc, B_KV), cmp_pos_k, w_cmp_k1, w_cmp_k2), k_gain_cmp)
    v_cmp = compress_blocks(heads(vc, B_KV), cmp_pos_v, w_cmp_v1, w_cmp_v2)
    k_sel = qk_norm(heads(ks, B_KV), k_gain_sel)
    k_win = qk_norm(heads(kw, B_KV), k_gain_win)
    o_cmp, o_sel = nsa_cmp_sel(qb, k_cmp, v_cmp, k_sel, heads(vs, B_KV), bias_b)
    o_win = banded_gqa(qb, k_win, heads(vw, B_KV), NSA_WINDOW, bias_b, None)
    gb = jax.nn.sigmoid((g_b + b_nsa_gate).astype(jnp.float32)).reshape(Bn, S, B_HEADS, N_NSA_BRANCHES, 1)
    o_b = gb[..., 0, :] * o_cmp + gb[..., 1, :] * o_sel + gb[..., 2, :] * o_win

    y = jnp.concatenate([o_a.reshape(Bn, S, D_A) * jax.nn.silu(z_a.astype(jnp.float32)),
                         o_b.reshape(Bn, S, D_B) * jax.nn.silu(z_b.astype(jnp.float32))], axis=-1)
    out = y.astype(x.dtype) @ w_out
    return x + gate[:, None, :] * out

def second_inputs(seed: int = 0) -> dict:
    key = jax.random.key(seed)
    ks = jax.random.split(key, 24)
    nrm = lambda k, shape, s: jax.random.normal(k, shape, jnp.float32) * s
    gain = lambda k, shape: 1.0 + 0.1 * jax.random.normal(k, shape, jnp.float32)
    L = DEPTH
    return {
        "x": nrm(ks[0], (BATCH, SEQ, D_MODEL), 1.0),
        "c": nrm(ks[1], (BATCH, D_MODEL), 1.0),
        "w_ada": nrm(ks[2], (L, D_MODEL, 3 * D_MODEL), 0.5 * D_MODEL ** -0.5),
        "b_ada": nrm(ks[3], (L, 3 * D_MODEL), 0.01),
        "norm_gain": gain(ks[4], (L, D_MODEL)),
        "w_in": nrm(ks[5], (L, D_MODEL, D_PROJ), D_MODEL ** -0.5),
        "b_nsa_gate": nrm(ks[6], (L, B_HEADS * N_NSA_BRANCHES), 0.1),
        "q_gain_a": gain(ks[7], (L, HEAD_DIM)),
        "k_gain_a": gain(ks[8], (L, HEAD_DIM)),
        "sinks": nrm(ks[9], (L, A_HEADS), 1.0),
        "q_gain_b": gain(ks[10], (L, HEAD_DIM)),
        "k_gain_cmp": gain(ks[11], (L, HEAD_DIM)),
        "k_gain_sel": gain(ks[12], (L, HEAD_DIM)),
        "k_gain_win": gain(ks[13], (L, HEAD_DIM)),
        "cmp_pos_k": nrm(ks[14], (L, CMP_LEN, HEAD_DIM), 0.5),
        "cmp_pos_v": nrm(ks[15], (L, CMP_LEN, HEAD_DIM), 0.5),
        "w_cmp_k1": nrm(ks[16], (L, CMP_LEN * HEAD_DIM, CMP_HIDDEN), (CMP_LEN * HEAD_DIM) ** -0.5),
        "w_cmp_k2": nrm(ks[17], (L, CMP_HIDDEN, HEAD_DIM), CMP_HIDDEN ** -0.5),
        "w_cmp_v1": nrm(ks[18], (L, CMP_LEN * HEAD_DIM, CMP_HIDDEN), (CMP_LEN * HEAD_DIM) ** -0.5),
        "w_cmp_v2": nrm(ks[19], (L, CMP_HIDDEN, HEAD_DIM), CMP_HIDDEN ** -0.5),
        "w_out": nrm(ks[20], (L, D_MIX, D_MODEL), D_MIX ** -0.5),
        "rel_bias": nrm(ks[21], (N_BUCKETS, N_HEADS_TOTAL), 0.5),
    }

def second_block(x, c, w_ada, b_ada, norm_gain, w_in, b_nsa_gate, q_gain_a, k_gain_a, sinks,
              q_gain_b, k_gain_cmp, k_gain_sel, k_gain_win, cmp_pos_k, cmp_pos_v,
              w_cmp_k1, w_cmp_k2, w_cmp_v1, w_cmp_v2, w_out, rel_bias):
    for l in range(DEPTH):
        x = hybrid_layer(x, c, w_ada[l], b_ada[l], norm_gain[l], w_in[l], b_nsa_gate[l],
                         q_gain_a[l], k_gain_a[l], sinks[l], q_gain_b[l], k_gain_cmp[l],
                         k_gain_sel[l], k_gain_win[l], cmp_pos_k[l], cmp_pos_v[l],
                         w_cmp_k1[l], w_cmp_k2[l], w_cmp_v1[l], w_cmp_v2[l], w_out[l], rel_bias)
    return x


def setup_inputs(seed=0):
    out = dict(first_inputs(seed))
    for name, value in second_inputs(seed + 1).items():
        if name != "x":
            out[name + "_2"] = value
    return out


def reference(
    x, meta_tokens, ffn1_norm, ffn1_w_gate, ffn1_w_up, ffn1_w_down, mix_norm, w_in, q_norm,
    w_uq, kv_norm, w_ukv, w_mla_o, conv_w, a_log, dt_bias, gdn_norm, w_gdn_o, w_out, ffn2_norm,
    ffn2_w_gate, ffn2_w_up, ffn2_w_down, final_norm, c_2, w_ada_2, b_ada_2, norm_gain_2, w_in_2,
    b_nsa_gate_2, q_gain_a_2, k_gain_a_2, sinks_2, q_gain_b_2, k_gain_cmp_2, k_gain_sel_2,
    k_gain_win_2, cmp_pos_k_2, cmp_pos_v_2, w_cmp_k1_2, w_cmp_k2_2, w_cmp_v1_2, w_cmp_v2_2,
    w_out_2, rel_bias_2,
):
    x = first_block(
        x, meta_tokens, ffn1_norm, ffn1_w_gate, ffn1_w_up, ffn1_w_down, mix_norm, w_in, q_norm,
        w_uq, kv_norm, w_ukv, w_mla_o, conv_w, a_log, dt_bias, gdn_norm, w_gdn_o, w_out,
        ffn2_norm, ffn2_w_gate, ffn2_w_up, ffn2_w_down, final_norm,
    )
    return second_block(
        x, c_2, w_ada_2, b_ada_2, norm_gain_2, w_in_2, b_nsa_gate_2, q_gain_a_2, k_gain_a_2,
        sinks_2, q_gain_b_2, k_gain_cmp_2, k_gain_sel_2, k_gain_win_2, cmp_pos_k_2, cmp_pos_v_2,
        w_cmp_k1_2, w_cmp_k2_2, w_cmp_v1_2, w_cmp_v2_2, w_out_2, rel_bias_2,
    )


_drawn_inputs = setup_inputs


def setup_inputs(seed=0):
    import zlib

    import numpy as np

    out = dict(_drawn_inputs(seed))
    spreads = {}
    factors = {'ffn1_norm': 5.821,
     'mix_norm': 4.563,
     'q_norm': 8.0,
     'kv_norm': 8.0,
     'gdn_norm': 7.908,
     'ffn2_norm': 7.483,
     'final_norm': 2.902,
     'b_ada_2': 8.0,
     'norm_gain_2': 5.818,
     'b_nsa_gate_2': 8.0,
     'q_gain_a_2': 8.0,
     'k_gain_a_2': 8.0,
     'sinks_2': 49.783,
     'q_gain_b_2': 8.0,
     'k_gain_cmp_2': 8.0,
     'k_gain_sel_2': 8.0,
     'k_gain_win_2': 8.0,
     'cmp_pos_k_2': 8.0,
     'cmp_pos_v_2': 3.282,
     'w_cmp_k1_2': 5.766,
     'w_cmp_k2_2': 5.322,
     'rel_bias_2': 4.322}
    for name, (base, spread) in spreads.items():
        noise = np.random.default_rng([zlib.crc32(name.encode()), seed]).standard_normal(out[name].shape)
        drawn = base * np.exp(spread * noise) if base else spread * noise
        out[name] = __import__('jax').numpy.asarray(drawn.astype(out[name].dtype))
    for name, factor in factors.items():
        out[name] = (out[name] * factor).astype(out[name].dtype)
    return out
```

```python
from contextlib import ExitStack

import numpy as np

import concourse.bass as bass
from concourse import mybir

P = 128
D_MODEL, SEQ, N_META, D_FF = 1024, 512, 16, 2816
EPS = 1e-6
KD = D_MODEL // P
T1 = N_META + SEQ
HT = T1 // 2
NH = 8
FJ = D_FF // P
FH = FJ // 2
QT = SEQ // P
CH = 64
NCH = (T1 + 48) // CH
PAD = NCH * CH - T1
NU = 4 * NCH
UB = 6
NB = NU // UB
LEVELS = 6
NCMP = 31
NEG = -1.0e30
SLOT = 2048

STREAM = [("f1u0", FH, 16), ("f1d0", KD, FH), ("f1u1", FH, 16), ("f1d1", KD, FH),
          ("w1", 8, 16), ("uq", 1, 16), ("ukv", 1, 8), ("z", 2, 16), ("mg", 16, 16), ("wo", 4, 16),
          ("f2u0", FH, 16), ("f2d0", KD, FH), ("f2u1", FH, 16), ("f2d1", KD, FH),
          ("wi", 10, 16), ("wt", 1, 8), ("wv", 2, 0), ("wo2", 4, 16)]
TOKEN_COLS = 408
WIDTH = {n: t * P for n, _, t in STREAM}
WIDTH["wv"] = 4 * TOKEN_COLS
START = {}
_n = 0
for _name, _c, _ in STREAM:
    START[_name] = _n
    _n += _c
COUNT = {n: c for n, c, _ in STREAM}
ORDER = [n for n, _, _ in STREAM]

COLS = {}
_n = 0
for _name, _c in [("ffn1", 8), ("mix", 8), ("ffn2", 8), ("fin", 8), ("ng2", 8), ("qn", 2), ("kvn", 1),
                  ("gdn", 1), ("conv", 48), ("qa", 1), ("qb", 1), ("ka", 1), ("ks", 1), ("kw", 1),
                  ("kc", 1), ("bada", 24), ("dtb", 1), ("alog", 1), ("sink", 8), ("bg", 24),
                  ("posk", 16), ("posv", 16)]:
    COLS[_name] = _n
    _n += _c
NCOLS = _n
TABS = {}
_n = 0
for _name, _c in [("ident", 128), ("ones", 128), ("bones", 128), ("cos", T1), ("sin", T1),
                  ("mA", 256), ("mB", 256), ("cneg", 4 * NCMP), ("c01", 4 * NCMP), ("i64", CH),
                  ("mincl", CH), ("mstrict", CH), ("lvl", LEVELS * CH), ("sel", 4 * 128),
                  ("oh", 383)]:
    TABS[_name] = _n
    _n += _c
NTAB = _n
GROUPS = 4 + 3 * QT


def build(nc, io):
    f32, f32r = mybir.dt.float32, mybir.dt.float32r
    ALU, ACT, AX = mybir.AluOpType, mybir.ActivationFunctionType, mybir.AxisListType
    ctx = ExitStack()

    def sem(name):
        return ctx.enter_context(nc.semaphore(name))

    top = [16512]

    def at(name, shape, dtype, off):
        return nc.alloc_sbuf_tensor_at(name, shape, dtype, offset=off)

    def size(shape):
        n = 4
        for s in shape[1:]:
            n *= s
        return (n + 31) // 32 * 32

    def place(name, shape, dtype=f32):
        off = top[0]
        top[0] += size(shape)
        assert top[0] <= 229344, (name, top[0])
        return at(name, shape, dtype, off)

    H = place("H", [P, KD, T1])
    RAW = place("RAW", [P, 2, SLOT])
    WHI = place("WHI", [P, 2, SLOT], f32r)
    WLO = place("WLO", [P, 2, SLOT], f32r)
    TAB = place("TAB", [P, NTAB])
    COL = place("COL", [P, NCOLS])
    MOD = place("MOD", [P, 24])
    CST = place("CST", [P, 4])
    RELB = place("RELB", [32, 16])
    GATE = place("GATE", [P, QT, 24])
    B31 = place("B31", [P, 16])
    NSINK = place("NSINK", [P, NH])
    SNK = place("SNK", [P, 2 * NH])
    arena = top[0]
    SIZES = {}

    def region(start, *items):
        off, out = start, []
        for name, shape, dtype in items:
            out.append(at(name, shape, dtype, off))
            off += size(shape)
            assert off <= 229344, (name, off)
        return out + [off]

    U3 = [P, NU, CH]
    UH, UL, a_u = region(arena, ("UH", [P, KD, T1], f32r), ("UL", [P, KD, T1], f32r))
    RSTD, SQ, _ = region(a_u, ("RSTD", [P, T1], f32), ("SQ", [P, KD, T1], f32))
    _, GH, GL, TANH, SILU, GF, ADA, SILUC, JUNK, SILUT, _ = region(
        a_u, ("RSTDF", [P, T1], f32), ("GH", [P, FH, T1], f32r), ("GL", [P, FH, T1], f32r),
        ("TANH", [P, 2, T1], f32), ("SILU", [P, 2, T1], f32), ("GF", [P, 2, T1], f32),
        ("ADA", [P, 2, D_MODEL], f32), ("SILUC", [P, D_MODEL], f32), ("JUNK", [P, D_MODEL], f32),
        ("SILUT", [P, D_MODEL], f32))
    PR, a_pr = region(a_u, ("PR", [P, 16, T1], f32))
    OTH, OTL, a_ot = region(a_pr, ("OTH", [P, 4, SEQ], f32r), ("OTL", [P, 4, SEQ], f32r))
    QH, KH, a_qk = region(arena, ("QH", [96, NH, SEQ], f32), ("KH", [96, NH, T1], f32))
    assert a_qk <= a_u
    VM, a_vm = region(a_ot, ("VM", [P, 5, SEQ], f32))
    CF, CHI, CLO, RQ, RK, ROT, _ = region(
        a_vm, ("CF", [P, 3, T1], f32), ("CHI", [P, 3, T1], f32r), ("CLO", [P, 3, T1], f32r),
        ("RQ", [P, SEQ], f32), ("RK", [P, T1], f32), ("ROT", [P, 4, SEQ], f32))
    KROT, _ = region(a_vm, ("KROT", [P, 2, T1], f32))
    PB1, PTS1, PTM, OSB1, NM1, RS1, RI1, OTF1, _ = region(
        a_vm, ("PB1", [P, 2, 640], f32), ("PTS1", [P, 2, SEQ], f32), ("PTM", [N_META, 2, P], f32),
        ("OSB1", [P, 2, SEQ], f32), ("NM1", [P, 4 * NH], f32), ("RS1", [P, 4 * NH], f32),
        ("RI1", [P, 4 * NH], f32), ("OTF1", [P, SEQ], f32))
    CV, a_cv = region(arena, ("CV", [P, 12, NCH * CH], f32))
    assert a_cv <= a_u
    IT, EU, TTT, VB, SV, SE, a_sv = region(
        a_cv, ("IT", U3, f32), ("EU", U3, f32), ("TTT", U3, f32), ("VB", U3, f32),
        ("SV", [P, 2, 4, CH], f32), ("SE", [P, 4, CH], f32))
    assert a_sv <= a_pr
    KDEC, GB, KBG, a_kb = region(a_ot, ("KDEC", U3, f32), ("GB", U3, f32), ("KBG", U3, f32))
    CT, GSQ, GR, _ = region(a_ot, ("CT", [P, 2, T1], f32), ("GSQ", [P, 2, T1], f32),
                            ("GR", [P, 2, T1], f32))
    BT8, GT, _ = region(a_kb, ("BT8", [NH, NCH * CH], f32), ("GT", [32 + NH, 5, NCH * CH], f32))
    TB, UMB, AB, VN, GP, _ = region(
        a_kb, ("TB", [P, 2, UB, CH], f32), ("UMB", [P, 2, UB, CH], f32),
        ("AB", [P, 2, UB, CH], f32), ("VN", [P, 2, 4, CH], f32), ("GP", [P, 8, NU], f32))
    SQ2, _ = region(a_ot + 3 * size([P, 4, SEQ]), ("SQ2", [P, KD, T1], f32))
    GOH, GOL, a_go = region(a_cv + 2 * size(U3), ("GOH", [P, 4, SEQ], f32r),
                            ("GOL", [P, 4, SEQ], f32r))
    assert a_go <= a_pr
    OSQ, OR, ZT, _ = region(a_ot, ("OSQ", [P, 4, SEQ], f32), ("OR", [P, 4, SEQ], f32),
                            ("ZT", [P, 4, SEQ], f32))
    MH, ML, TG, MF, _ = region(a_ot, ("MH", [P, KD, SEQ], f32r), ("ML", [P, KD, SEQ], f32r),
                               ("TG", [P, 2, SEQ], f32), ("MF", [P, 2, SEQ], f32))
    P2, VT, DT, OC, a_oc = region(
        a_u, ("P2", [P, 21, SEQ], f32), ("VT", [P, QT, TOKEN_COLS], f32),
        ("DT", [P, 16, 256], f32), ("OC", [P, QT, SEQ], f32))
    W1C, _ = region(arena, ("W1C", [P, 2, 16, 256], f32))
    XC, HC, HTN, W2C, KCF, VCF, CPB, PSQ, CB, M8, a_pr2 = region(
        a_oc, ("XC", [P, 2, 2, SEQ], f32), ("HC", [P, 4, 64], f32), ("HTN", [P, 4, 64], f32),
        ("W2C", [P, 2, 2, CH], f32), ("KCF", [P, 32], f32), ("VCF", [NCMP, 2, CH], f32),
        ("CPB", [P, NH, NCMP], f32), ("PSQ", [P, 2, SEQ], f32), ("CB", [P, 4], f32),
        ("M8", [P, 4, NH], f32))
    PRS, _ = region(a_pr2, ("PRS", [P, 2, SEQ], f32))
    CPT, _ = region(a_pr2, ("CPT", [NCMP, NH, P], f32))
    YH, YL, _ = region(arena, ("YH", [P, KD, SEQ], f32r), ("YL", [P, KD, SEQ], f32r))
    PB2, PTS2, OSB2, OBT, OTF2, NM2, RS2, RI2, _ = region(
        a_oc, ("PB2", [P, 2, SEQ], f32), ("PTS2", [P, 2, SEQ], f32), ("OSB2", [P, 2, SEQ], f32),
        ("OBT", [P, SEQ], f32), ("OTF2", [P, SEQ], f32), ("NM2", [P, 12 * NH], f32), ("RS2", [P, 12 * NH], f32),
        ("RI2", [P, 12 * NH], f32))
    PS = ctx.enter_context(nc.psum_tensor("PS", [P, 8, 512], f32))

    def tab(name, a=0, b=None):
        b = b if b is not None else P
        return TAB[:, TABS[name] + a:TABS[name] + b]

    def col(name, k=0, n=1):
        return COL[:, COLS[name] + k:COLS[name] + k + n]

    IDENT, ONES, BONES = tab("ident"), tab("ones"), tab("bones")
    EPS_AP = CST[:, 0:1]

    def flat(t):
        return t.rearrange("p a b -> p (a b)")

    def units(t, b):
        return t[:, b * UB:(b + 1) * UB, :]

    def over(ap, n):
        return ap.unsqueeze(1).to_broadcast([P, n, CH])

    def along(ap, n, w=CH):
        return ap.unsqueeze(2).to_broadcast([P, n, w])

    def chunk_of(t, n):
        return t[:, :, :].rearrange("p (t n) c -> p t n c", n=NCH)[:, :, n, :]

    def pair_rows(t):
        return t[:, :, :].rearrange("p (t n) c -> p t (n c)", n=NCH)

    def halves(ap):
        return ap.rearrange("p (a b) -> p a b", a=2)

    h_ld, tab_ld, col_ld, rel_ld = sem("h_loaded"), sem("tables_loaded"), sem("cols_loaded"), sem("rel_loaded")
    raw_ld = [sem("raw_loaded_0"), sem("raw_loaded_1")]
    hi_rdy, lo_rdy = sem("weights_hi_ready"), sem("weights_lo_ready")
    mm_done, evac = sem("chunk_multiplied"), sem("chunk_evacuated")
    eps_rdy, dve_chain, act_chain = sem("eps_ready"), sem("vector_chain"), sem("scalar_chain")
    sq_rdy, ss_done, rstd_rdy = sem("squares_ready"), sem("square_sums_done"), sem("rstd_ready")
    uf_rdy, uh_rdy, ul_rdy = sem("normed_ready"), sem("normed_hi_ready"), sem("normed_lo_ready")
    tanh_rdy, silu_rdy = sem("tanh_ready"), sem("silu_ready")
    gh_rdy, gl_rdy = sem("hidden_hi_ready"), sem("hidden_lo_ready")
    ada_ld = [sem("ada_loaded_0"), sem("ada_loaded_1")]
    c_ld, ct_rdy, ada_used = sem("c_loaded"), sem("c_tanh_ready"), sem("ada_used")
    rev_ps, rev_rdy, rev_st, dt_ld = sem("rev_in_psum"), sem("rev_ready"), sem("rev_stored"), sem("bias_loaded")
    dt_rdy = sem("bias_ready")
    c_sq, c_ss, c_r, c_f, c_hi, c_lo = (sem("latent_" + x) for x in
                                        ("squared", "summed", "rstd", "normed", "hi", "lo"))
    uq_ps, q_act, kn_ps, k_act, kr_dve = (sem(x) for x in (
        "q_tile_in_psum", "q_nope_copied", "k_tile_in_psum", "k_nope_copied", "k_rope_ready"))
    s_ps, max_rdy, exp_rdy = sem("scores_in_psum"), sem("max_ready"), sem("exp_ready")
    pt_ps, pt_rdy, pv_done = sem("probs_t_in_psum"), sem("probs_t_ready"), sem("values_done")
    o_free, o_rdy, ot_ps = sem("o_psum_free"), sem("o_ready"), sem("o_t_in_psum")
    ot_f, ot_hi, ot_lo, sink_e = sem("o_t_ready"), sem("o_t_hi"), sem("o_t_lo"), sem("sink_exp_ready")
    cv_c, cv_t, cv_s = sem("conv_done"), sem("conv_tanh"), sem("conv_silu")
    l_sq, l_ss, l_r, l_n = sem("l2_squared"), sem("l2_summed"), sem("l2_rstd"), sem("l2_normed")
    gt_a, gt_d = sem("gate_scalar_steps"), sem("gate_vector_steps")
    bb_ps, bb_ev, gb_ps, gb_ev = (sem(x) for x in ("beta_bcast_psum", "beta_bcast_ready",
                                                   "decay_bcast_psum", "decay_bcast_ready"))
    dc_d, dc_a, un_rdy = sem("decay_vector_steps"), sem("decay_scalar_steps"), sem("unit_operands_ready")
    pr_ps, pr_rdy = sem("products_in_psum"), sem("products_ready")
    um_rdy, a_ps, ab_rdy, d_ps, t_rdy = (sem(x) for x in (
        "masked_ready", "a_in_psum", "a_ready", "update_in_psum", "inverse_updated"))
    uw_ps, u_rdy, w_rdy = sem("uw_in_psum"), sem("u_ready"), sem("w_ready")
    st_rdy, ws_ps, vn_rdy, sa_ps, o_ps, o_ev = (sem(x) for x in (
        "state_ready", "ws_in_psum", "v_new_ready", "state_add_in_psum", "delta_o_in_psum",
        "delta_o_ready"))
    osq_rdy, oss_ps, or_rdy, zt_rdy, gof_rdy, goh_rdy, gol_rdy = (sem(x) for x in (
        "delta_squared", "delta_summed", "delta_rstd", "z_tanh", "delta_gated", "delta_hi", "delta_lo"))
    tg_rdy, mf_rdy, mh_rdy, ml_rdy = (sem(x) for x in (
        "merge_gates_ready", "merged_ready", "merged_hi", "merged_lo"))
    x2_rdy = sem("second_input_ready")
    n_sq, n_ss, n_r, n_n = sem("qk_squared"), sem("qk_summed"), sem("qk_rstd"), sem("qk_normed")
    z_t, z_s, bg_d, bg_a = sem("z2_tanh"), sem("z2_silu"), sem("branch_gate_sum"), sem("branch_gate_tanh")
    w1_ld, xc_rdy, hc_ps, hc_x, hc_t, hc_rdy = (sem(x) for x in (
        "compress_loaded", "compress_input", "compress_psum", "compress_sum", "compress_tanh",
        "compress_hidden"))
    kc_ps, kc_f, kc_sq, kc_ss, kc_r, kc_rdy = (sem(x) for x in (
        "cmp_kv_psum", "cmp_kv_copied", "cmp_k_squared", "cmp_k_summed", "cmp_k_rstd", "cmp_k_ready"))
    cs_ps, cs_z, cs_e, cs_p, ct_ps, ct_ev, co_ps, co_rdy = (sem(x) for x in (
        "cmp_scores", "cmp_shifted", "cmp_exp", "cmp_probs", "cmp_probs_t", "cmp_probs_t_ready",
        "cmp_o_psum", "cmp_o_ready"))
    out_st = sem("out_stored")
    sink_s, tb_rdy, se_rdy = sem("sink_shifted"), sem("inverse_half_updated"), sem("state_decayed")

    class Chain:

        def __init__(self, eng, s):
            self.eng, self.s, self.n, self.add = eng, s, 0, 0

        def __call__(self, ins):
            self.n += 1
            ins.then_inc(self.s, 1)
            self.eng.wait_ge(self.s, self.n + self.add)

    def chunk_width(name, parity):
        if name == "mg":
            return SLOT if parity == 0 else SLOT // 2
        return WIDTH[name]

    def stream(eng, name, body):
        n0, count = START[name], COUNT[name]
        at_ = ORDER.index(name)
        after = chunk_width(ORDER[at_ + 1], 0) if at_ + 1 < len(ORDER) else 0
        head = 2 if n0 == 0 else 0

        def one(j):
            n = n0 + j
            body(n, j, n // 2, n % 2, chunk_width(name, (j + 1) % 2) if j + 1 < count else after)

        for j in range(head):
            one(j)
        trips = (count - head - 1) // 2
        if trips > 1:
            with eng.Fori(0, trips) as i:
                for s in range(2):
                    n = n0 + head + s
                    body(2 * i + n, 2 * i + head + s, i + n // 2, n % 2,
                         chunk_width(name, (head + s + 1) % 2))
            done = head + 2 * trips
        else:
            done = head
        for j in range(done, count):
            one(j)

    NORMS = [(0, T1), (0, T1), (N_META, SEQ), (N_META, SEQ), (N_META, SEQ), (N_META, SEQ)]

    def spans(c0, w):
        return [(c0, w)] if w <= 512 else [(c0, w // 2), (c0 + w // 2, w // 2)]

    def attention_units(part):
        out = []
        if part == 0:
            for qi in range(QT):
                for h in range(NH):
                    w = P * (qi + 1)
                    out.append(dict(
                        u=len(out), g=qi, h=h, last=h == NH - 1, kind="mla", qi=qi, w=w, total=w + N_META,
                        q=QH[0:96, h, P * qi:P * (qi + 1)],
                        keys=[(0, w, KH[0:96, h, N_META:N_META + w]), (w, N_META, KH[0:96, h, 0:N_META])],
                        bias=(w - P, P, tab("mB", P, 2 * P)),
                        v=[VM[:, 1 + j, CH * h:CH * (h + 1)] for j in range(qi + 1)],
                        vm=VM[0:N_META, 0, CH * h:CH * (h + 1)], tg=qi, sink=False))
            return out
        for qi in range(QT):
            for b, kind in enumerate(("A", "sel", "win")):
                for h in range(NH):
                    j, g = h % 4, h // 4
                    rows = slice(CH * g, CH * (g + 1))
                    first = max(qi - 1, 0) if kind == "A" else 0
                    w = P * (qi + 1 - first)
                    near = min(w, 2 * P)
                    out.append(dict(
                        u=4 * NH + len(out), g=QT + 3 * qi + b, h=h, last=h == NH - 1, kind=kind, qi=qi,
                        w=w, total=w, q=P2[rows, (j if kind == "A" else 4 + j), P * qi:P * (qi + 1)],
                        keys=[(0, w, P2[rows, 8 + b, P * first:P * (qi + 1)])],
                        bias=(w - near, near, DT[:, (h if kind == "A" else 8 + h), 2 * P - near:2 * P]),
                        v=[VT[:, t, P * b + CH * g:P * b + CH * (g + 1)] for t in range(first, qi + 1)],
                        vm=None, tg=(QT + 2 * qi if kind == "A" else QT + 2 * qi + 1 if kind == "win" else None),
                        sink=kind == "A"))
        return out

    PARTS = [attention_units(0), attention_units(1)]

    def bufs(part):
        return (PB1, PTS1, OSB1, OTF1, NM1, RS1, RI1) if part == 0 else (PB2, PTS2, OSB2, OTF2, NM2, RS2, RI2)

    def scores(s, a, b):
        return PS[:, 2 * s:2 * s + 2, :].rearrange("p a b -> p (a b)")[:, a:b]

    block = ctx.enter_context(nc.Block())

    @block.sync
    def _(sp):
        sp.dma_start(COL[:, :], io["cols"]).then_inc(col_ld, 16)
        sp.dma_start(TAB[:, :], io["tabs"]).then_inc(tab_ld, 16)
        sp.dma_start(H[:, :, :], io["h"].rearrange("k p t -> p k t")).then_inc(h_ld, 16)
        sp.dma_start(RELB[:, :], io["rel"]).then_inc(rel_ld, 16)

        def load(name):
            def body(n, j, turn, slot, nxt):
                if not isinstance(n, int) or n >= 2:
                    sp.wait_ge(lo_rdy, n - 1)
                w = chunk_width(name, (n - START[name]) % 2 if isinstance(n, int) else
                                (slot - START[name]) % 2)
                src = io[name][j] if name != "mg" else io["mg"][j, :, 0:w]
                sp.dma_start(RAW[:, slot, 0:w], src).then_inc(raw_ld[slot], 16)
            return body

        for name in ORDER[:-1]:
            stream(sp, name, load(name))
        n0 = START["wo2"]
        for j in range(2):
            load("wo2")(n0 + j, j, 0, (n0 + j) % 2, 0)
        sp.wait_ge(mm_done, n0)
        sp.dma_start(W1C[:, 0, :, :], io["w1k"]).then_inc(w1_ld, 16)
        sp.dma_start(W1C[:, 1, :, :], io["w1v"]).then_inc(w1_ld, 16)
        sp.dma_start(W2C[:, :, :, :], io["w2"]).then_inc(w1_ld, 16)
        for j in range(2, 4):
            load("wo2")(n0 + j, j, 0, (n0 + j) % 2, 0)
        for j in range(4):
            sp.wait_ge(evac, n0 + j + 1)
            sp.dma_start(io["out"][2 * j:2 * j + 2].rearrange("k p t -> p k t"),
                         H[:, 2 * j:2 * j + 2, N_META:T1]).then_inc(out_st, 16)
        sp.wait_ge(out_st, 64)

    @block.gpsimd
    def _(pool):
        pool.dma_start(SILUC[:, :], io["c"].partition_broadcast(P)).then_inc(c_ld, 16)
        for s in range(2):
            pool.dma_start(ADA[:, s, :], io["ada"][s]).then_inc(ada_ld[s], 16)
        pool.wait_ge(rev_rdy, 1)
        pool.dma_start(io["rev"][:, :, 0:383], JUNK[0:16, 0:383].unsqueeze(1).to_broadcast([16, P, 383]))\
            .then_inc(rev_st, 16)
        pool.dma_start(io["rev0"].unsqueeze(1), JUNK[0:16, 0:1]).then_inc(rev_st, 16)
        with pool.Fori(1, 12) as i:
            for s in range(2):
                pool.wait_ge(ada_used, 2 * i + s - 1)
                pool.dma_start(ADA[:, s, :], io["ada"][2 * i + s]).then_inc(ada_ld[s], 16)
        pool.wait_ge(rev_st, 32)
        pool.wait_ge(evac, START["wi"])
        pool.dma_start(DT[:, :, :], bass.AP(io["rev"].tensor, 127, [[383, P], [P * 384, 16], [1, 256]]))\
            .then_inc(dt_ld, 16)
        pool.dma_start(B31[:, :], io["rev0"].partition_broadcast(P)).then_inc(dt_ld, 16)
        pool.wait_ge(dt_ld, 32)

    @block.tensor
    def _(pe):
        mm = nc.tensor.matmul

        def mm3(out, slot, c, hi, lo, first, last, w=P):
            mm(out, WHI[:, slot, c:c + w], hi, start=first, stop=False)
            mm(out, WLO[:, slot, c:c + w], hi, start=False, stop=False)
            return mm(out, WHI[:, slot, c:c + w], lo, start=False, stop=last)

        def norm(v):
            c0, w = NORMS[v]
            sq = SQ2 if v == 2 else SQ
            for k in range(KD):
                pe.wait_ge(sq_rdy, KD * v + k + 1)
                for b, (a, n) in enumerate(spans(c0, w)):
                    last = mm(PS[:, 6 + b, 0:n], ONES, sq[:, k, a:a + n], start=k == 0, stop=k == KD - 1)
            last.then_inc(ss_done, 1)

        def ffn(f, c0, w):
            sp_ = spans(c0, w)
            for half in range(2):
                def up(n, j, turn, slot, nxt):
                    pe.wait_ge(lo_rdy, n + 1)
                    if not isinstance(n, int) or n >= 2:
                        pe.wait_ge(evac, n - 1)
                    for which in range(2):
                        for b, (a, m) in enumerate(sp_):
                            for k in range(KD):
                                last = mm3(PS[:, 4 * slot + 2 * which + b, 0:m], slot,
                                           (which * KD + k) * P, UH[:, k, a:a + m], UL[:, k, a:a + m],
                                           k == 0, k == KD - 1)
                    last.then_inc(mm_done, 1)

                def down(n, j, turn, slot, nxt):
                    pe.wait_ge(lo_rdy, n + 1)
                    pe.wait_ge(evac, n - 1)
                    for b, (a, m) in enumerate(sp_):
                        for k in range(FH):
                            last = mm3(PS[:, 4 * slot + b, 0:m], slot, k * P, GH[:, k, a:a + m],
                                       GL[:, k, a:a + m], k == 0, k == FH - 1)
                    last.then_inc(mm_done, 1)

                stream(pe, f"f{f + 1}u{half}", up)
                pe.wait_ge(gl_rdy, (2 * f + half + 1) * FH)
                stream(pe, f"f{f + 1}d{half}", down)

        pe.wait_ge(rel_ld, 16)
        pe.wait_ge(tab_ld, 16)
        mm(PS[0:16, 0, 0:383], RELB[:, :], TAB[0:32, TABS["oh"]:TABS["oh"] + 383], start=True,
           stop=True).then_inc(rev_ps, 1)
        norm(0)
        pe.wait_ge(ul_rdy, KD)
        pe.wait_ge(rev_rdy, 1)
        ffn(0, 0, T1)
        norm(1)
        pe.wait_ge(ul_rdy, 2 * KD)

        def project(c0, w):
            def body(n, j, turn, slot, nxt):
                pe.wait_ge(lo_rdy, n + 1)
                pe.wait_ge(evac, n - 1)
                for t in range(2):
                    for b, (a, m) in enumerate(spans(c0, w)):
                        for k in range(KD):
                            last = mm3(PS[:, 4 * slot + (2 if w > 512 else 1) * t + b, 0:m], slot,
                                       (t * KD + k) * P, UH[:, k, a:a + m], UL[:, k, a:a + m],
                                       k == 0, k == KD - 1)
                last.then_inc(mm_done, 1)
            return body

        stream(pe, "w1", project(0, T1))
        pe.wait_ge(c_sq, 3)
        pe.wait_ge(evac, START["uq"])
        for k in range(2):
            last = mm(PS[:, 0, 0:SEQ], ONES, CF[:, k, N_META:T1], start=k == 0, stop=k == 1)
        for b, (a, m) in enumerate(spans(0, T1)):
            last = mm(PS[:, 1 + b, 0:m], ONES, CF[:, 2, a:a + m], start=True, stop=True)
        last.then_inc(c_ss, 1)
        pe.wait_ge(lo_rdy, START["uq"] + 1)
        pe.wait_ge(c_lo, 1)
        for t in range(8):
            for k in range(2):
                last = mm3(PS[:, t, 0:SEQ], 0, (2 * t + k) * P, CHI[:, k, N_META:T1],
                           CLO[:, k, N_META:T1], k == 0, k == 1)
            last.then_inc(uq_ps, 1)
            if t == 7:
                mm_last = last
        pe.wait_ge(uq_ps, 8)
        pe.sem_inc(mm_done, 1)
        pe.wait_ge(lo_rdy, START["ukv"] + 1)
        pe.wait_ge(evac, START["ukv"])
        for t in range(4):
            for b, (a, m) in enumerate(spans(0, T1)):
                last = mm3(PS[:, 2 * t + b, 0:m], 1, t * P, CHI[:, 2, a:a + m], CLO[:, 2, a:a + m],
                           True, True)
            last.then_inc(kn_ps, 1)
        pe.wait_ge(k_act, NH)
        for t in range(5):
            a = 0 if t == 0 else N_META + P * (t - 1)
            mm(PS[:, t, 0:SEQ], CHI[:, 2, a:a + P], WHI[:, 1, SEQ:2 * SEQ], start=True, stop=False)
            mm(PS[:, t, 0:SEQ], CLO[:, 2, a:a + P], WHI[:, 1, SEQ:2 * SEQ], start=False, stop=False)
            last = mm(PS[:, t, 0:SEQ], CHI[:, 2, a:a + P], WLO[:, 1, SEQ:2 * SEQ], start=False, stop=True)
        last.then_inc(mm_done, 1)

        def attention(part):
            U = PARTS[part]
            PB, PTS, OSB = bufs(part)[:3]
            base = U[0]["u"]
            ends = {x["u"] - base: x for x in U if x["last"]}
            for i in range(len(U) + 5):
                if i < len(U):
                    x = U[i]
                    s = x["u"] % 2
                    if i >= 2:
                        pe.wait_ge(pt_rdy, x["u"] - 1)
                    for c, n, k in x["keys"]:
                        for c1 in range(c, c + n, 512):
                            n1 = min(n, 512)
                            last = mm(scores(s, c1, c1 + n1), x["q"], k, start=True, stop=True)
                    last.then_inc(s_ps, 1)
                if 1 <= i <= len(U):
                    x = U[i - 1]
                    s = x["u"] % 2
                    pe.wait_ge(exp_rdy, x["u"] + 1)
                    for t in range(x["w"] // P):
                        last = nc.tensor.transpose(PS[:, 4 + s, t * P:(t + 1) * P],
                                                   PB[:, s, t * P:(t + 1) * P], IDENT)
                    if x["vm"] is not None:
                        last = nc.tensor.transpose(PS[0:N_META, 2 * s + 1, P:2 * P],
                                                   PB[:, s, x["w"]:x["w"] + N_META], IDENT)
                    last.then_inc(pt_ps, 1)
                if 2 <= i <= len(U) + 1:
                    x = U[i - 2]
                    s = x["u"] % 2
                    o = PS[:, 6, CH * x["h"]:CH * (x["h"] + 1)]
                    pe.wait_ge(pt_rdy, x["u"] + 1)
                    if x["h"] == 0 and x["g"] > 0:
                        pe.wait_ge(o_free, x["g"])
                    n = len(x["v"])
                    for t, v in enumerate(x["v"]):
                        last = mm(o, PTS[:, s, t * P:(t + 1) * P], v, start=t == 0,
                                  stop=t == n - 1 and x["vm"] is None)
                    if x["vm"] is not None:
                        last = mm(o, PTM[:, s, :], x["vm"], start=False, stop=True)
                    last.then_inc(pv_done, 1)
                x = ends.get(i - 4)
                if x is not None and x["tg"] is not None:
                    pe.wait_ge(o_rdy, x["tg"] + 1)
                    if x["tg"] > 0:
                        pe.wait_ge(ot_f, x["tg"])
                    for f in range(4):
                        last = nc.tensor.transpose(PS[:, 7, f * P:(f + 1) * P],
                                                   OSB[:, x["tg"] % 2, f * P:(f + 1) * P], IDENT)
                    last.then_inc(ot_ps, 1)

        pe.wait_ge(evac, START["z"])
        pe.wait_ge(kr_dve, 1)
        attention(0)
        pe.wait_ge(ot_f, QT)
        for t in range(8):
            pe.wait_ge(l_sq, t + 1)
            if t >= 4:
                pe.wait_ge(l_r, t - 3)
            for b, (a, m) in enumerate(spans(0, T1)):
                last = mm(PS[:, 2 * (t % 4) + b, 0:m], BONES, GSQ[:, t % 2, a:a + m], start=True, stop=True)
            last.then_inc(l_ss, 1)
        W2 = NCH * CH // 2
        pe.wait_ge(l_r, 8)
        pe.wait_ge(gt_d, 9)
        for t in range(4):
            for b in range(2):
                last = mm(PS[:, 2 * t + b, 0:W2], TAB[0:NH, TABS["sel"] + t * P:TABS["sel"] + (t + 1) * P],
                          BT8[:, b * W2:(b + 1) * W2], start=True, stop=True)
        last.then_inc(bb_ps, 1)
        pe.wait_ge(bb_ev, 1)
        for t in range(4):
            for b in range(2):
                last = mm(PS[:, 2 * t + b, 0:W2],
                          TAB[32:32 + NH, TABS["sel"] + t * P:TABS["sel"] + (t + 1) * P],
                          GT[32:32 + NH, 2, b * W2:(b + 1) * W2], start=True, stop=True)
        last.then_inc(gb_ps, 1)
        pe.wait_ge(un_rdy, 1)

        def cvu(group, u, p):
            t, n = divmod(u, NCH)
            return CV[CH * p:CH * (p + 1), 4 * group + t, n * CH:(n + 1) * CH]

        def un(t, u, p):
            return t[CH * p:CH * (p + 1), u, :]

        for b in range(NB):
            if b >= 2:
                pe.wait_ge(pr_rdy, b - 1)
            for r in range(UB):
                u = b * UB + r
                for p in range(2):
                    rows = slice(CH * p, CH * (p + 1))

                    def bank(i):
                        return PS[rows, 4 * (b % 2) + i, r * CH:(r + 1) * CH]

                    i64 = TAB[rows, TABS["i64"]:TABS["i64"] + CH]
                    mm(bank(0), cvu(1, u, p), un(TTT, u, p), start=True, stop=True)
                    mm(bank(1), cvu(1, u, p), cvu(0, u, p), start=True, stop=True)
                    mm(bank(2), cvu(1, u, p), i64, start=True, stop=True)
                    last = mm(bank(3), cvu(2, u, p), i64, start=True, stop=True)
            last.then_inc(pr_ps, 1)
        pe.wait_ge(pr_rdy, NB)
        for bp in range(NB // 2):
            for lv in range(LEVELS):
                for x in range(2):
                    b = 2 * bp + x
                    i = 2 * (LEVELS * bp + lv) + x
                    pe.wait_ge(um_rdy, i + 1)
                    pe.wait_ge(t_rdy, i + 2 * bp + 1)
                    for r in range(UB):
                        for p in range(2):
                            rows = slice(CH * p, CH * (p + 1))
                            last = mm(PS[rows, 4 * x, r * CH:(r + 1) * CH], UMB[rows, x, r, :],
                                      TB[rows, x, r, :], start=True, stop=True)
                    last.then_inc(a_ps, 1)
                for x in range(2):
                    b = 2 * bp + x
                    i = 2 * (LEVELS * bp + lv) + x
                    pe.wait_ge(ab_rdy, i + 1)
                    for r in range(UB):
                        u = b * UB + r
                        for p in range(2):
                            rows = slice(CH * p, CH * (p + 1))
                            mm(PS[rows, 4 * x + 1, r * CH:(r + 1) * CH], un(TTT, u, p),
                               AB[rows, x, r, :], start=True, stop=True)
                            last = mm(PS[rows, 4 * x + 2, r * CH:(r + 1) * CH], AB[rows, x, r, :],
                                      un(TTT, u, p), start=True, stop=True)
                    last.then_inc(d_ps, 1)
            for x in range(2):
                b = 2 * bp + x
                pe.wait_ge(t_rdy, 2 * (LEVELS + 1) * (bp + 1) - 1 + x)
                for r in range(UB):
                    u = b * UB + r
                    for p in range(2):
                        rows = slice(CH * p, CH * (p + 1))
                        mm(PS[rows, 4 * x, r * CH:(r + 1) * CH], un(TTT, u, p), un(VB, u, p),
                           start=True, stop=True)
                        last = mm(PS[rows, 4 * x + 3, r * CH:(r + 1) * CH], un(KBG, u, p),
                                  un(TTT, u, p), start=True, stop=True)
                last.then_inc(uw_ps, 1)
        pe.wait_ge(u_rdy, NB)
        pe.wait_ge(w_rdy, NB)
        for n in range(NCH):
            pe.wait_ge(st_rdy, n + 1)

            def tiles(t, p, a):
                return slice(CH * p, CH * (p + 1)), t * NCH + n, slice(CH * a, CH * (a + 1))

            for t in range(4):
                for p in range(2):
                    rows, u, _ = tiles(t, p, 0)
                    last = mm(PS[rows, 0, t * CH:(t + 1) * CH], KBG[rows, u, :],
                              SV[rows, n % 2, t, :], start=True, stop=True)
            last.then_inc(ws_ps, 1)
            pe.wait_ge(vn_rdy, n + 1)
            if n < NCH - 1:
                for t in range(4):
                    for p in range(2):
                        rows, u, _ = tiles(t, p, 0)
                        last = mm(PS[rows, 1, t * CH:(t + 1) * CH], KDEC[rows, u, :],
                                  VN[rows, n % 2, t, :], start=True, stop=True)
                last.then_inc(sa_ps, 1)
            if n >= 2:
                pe.wait_ge(o_ev, n - 1)
            for t in range(4):
                for p in range(2):
                    rows, u, _ = tiles(t, p, 0)
                    o = PS[rows, 2 + n % 2, t * CH:(t + 1) * CH]
                    mm(o, SV[rows, n % 2, t, :], GB[rows, u, :], start=True, stop=False)
                    last = mm(o, VN[rows, n % 2, t, :], IT[rows, u, :], start=False, stop=True)
            last.then_inc(o_ps, 1)
        norm(2)
        pe.wait_ge(rstd_rdy, 3)
        pe.wait_ge(osq_rdy, 1)
        for t in range(4):
            last = mm(PS[:, (2, 3, 6, 7)[t], 0:SEQ], BONES, OSQ[:, t, :], start=True, stop=True)
        last.then_inc(oss_ps, 1)
        pe.wait_ge(ul_rdy, 3 * KD)
        stream(pe, "z", project(N_META, SEQ))
        pe.wait_ge(or_rdy, 1)
        pe.wait_ge(gol_rdy, 1)

        def merge(n, j, turn, slot, nxt):
            pe.wait_ge(lo_rdy, n + 1)
            if slot == 0:
                pe.wait_ge(tg_rdy, turn - (START["mg"] // 2 - 1))
                for t in range(2):
                    for k in range(KD):
                        last = mm3(PS[:, t, 0:SEQ], slot, (t * KD + k) * P, UH[:, k, N_META:T1],
                                   UL[:, k, N_META:T1], k == 0, k == KD - 1)
            else:
                pe.wait_ge(evac, n - 1)
                for t, (hi, lo) in enumerate(((OTH, OTL), (GOH, GOL))):
                    for k in range(4):
                        last = mm3(PS[:, 4 + t, 0:SEQ], slot, (t * 4 + k) * P, hi[:, k, :], lo[:, k, :],
                                   k == 0, k == 3)
            last.then_inc(mm_done, 1)

        stream(pe, "mg", merge)

        def outward(hi, lo):
            def body(n, j, turn, slot, nxt):
                pe.wait_ge(lo_rdy, n + 1)
                pe.wait_ge(evac, n - 1)
                for t in range(2):
                    for k in range(KD):
                        last = mm3(PS[:, 4 * slot + t, 0:SEQ], slot, (t * KD + k) * P, hi[:, k, :],
                                   lo[:, k, :], k == 0, k == KD - 1)
                last.then_inc(mm_done, 1)
            return body

        pe.wait_ge(ml_rdy, KD + 1)
        pe.wait_ge(evac, START["wo"])
        stream(pe, "wo", outward(MH, ML))
        norm(3)
        pe.wait_ge(ul_rdy, 4 * KD)
        ffn(1, N_META, SEQ)
        norm(4)
        norm(5)
        pe.wait_ge(ul_rdy, 5 * KD)
        stream(pe, "wi", project(N_META, SEQ))
        n = START["wt"]
        pe.wait_ge(lo_rdy, n + 1)
        pe.wait_ge(evac, n - 1)
        for k in range(KD):
            last = mm3(PS[:, 4 * (n % 2), 0:SEQ], n % 2, k * P, UH[:, k, N_META:T1], UL[:, k, N_META:T1],
                       k == 0, k == KD - 1)
        last.then_inc(mm_done, 1)
        n = START["wv"]
        pe.wait_ge(evac, n - 1)
        for c in range(2):
            s = (n + c) % 2
            pe.wait_ge(lo_rdy, n + c + 1)
            for qi in range(QT):
                for kk in range(4):
                    k = 4 * c + kk
                    a = N_META + P * qi
                    out = PS[:, 4 + qi, 0:TOKEN_COLS]
                    wc = slice(kk * TOKEN_COLS, (kk + 1) * TOKEN_COLS)
                    mm(out, UH[:, k, a:a + P], WHI[:, s, wc], start=k == 0, stop=False)
                    mm(out, UL[:, k, a:a + P], WHI[:, s, wc], start=False, stop=False)
                    last = mm(out, UH[:, k, a:a + P], WLO[:, s, wc], start=False, stop=k == KD - 1)
            last.then_inc(mm_done, 1)
        for t in range(11):
            pe.wait_ge(n_sq, t + 1)
            if t >= 4:
                pe.wait_ge(n_r, t - 3)
            mm(PS[:, t % 4, 0:SEQ], BONES, PSQ[:, t % 2, :], start=True, stop=True).then_inc(n_ss, 1)
        pe.wait_ge(n_r, 11)
        pe.wait_ge(w1_ld, 48)
        pe.wait_ge(xc_rdy, 2)
        pe.wait_ge(evac, START["wo2"])
        for kv, pos in enumerate(("posk", "posv")):
            for m in range(2):
                for lp in range(16):
                    wt = W1C[:, kv, lp, m * P:(m + 1) * P]
                    mm(PS[:, 2 * kv + m, 0:2 * NCMP].rearrange("p (g n) -> p g n", g=2), wt,
                       XC[:, kv, :, 2 * lp:2 * lp + 16 * (NCMP - 1) + 1:16], start=lp == 0, stop=lp == 15)
                for lp in range(16):
                    wt = W1C[:, kv, lp, m * P:(m + 1) * P]
                    last = mm(PS[:, 4 + 2 * kv + m, 0:1], wt, col(pos, lp), start=lp == 0, stop=lp == 15)
        last.then_inc(hc_ps, 1)
        pe.wait_ge(hc_rdy, 1)
        for g in range(2):
            for m in range(2):
                mm(PS[CH * g:CH * (g + 1), 0, 0:NCMP], W2C[:, 0, m, :],
                   HC[:, m, g * NCMP:(g + 1) * NCMP], start=m == 0, stop=m == 1)
            for m in range(2):
                last = mm(PS[0:NCMP, 1, CH * g:CH * (g + 1)], HC[:, 2 + m, g * NCMP:(g + 1) * NCMP],
                          W2C[:, 1, m, :], start=m == 0, stop=m == 1)
        last.then_inc(kc_ps, 1)
        pe.wait_ge(kc_sq, 1)
        mm(PS[:, 2, 0:NCMP], BONES, PSQ[:, 0, 0:NCMP], start=True, stop=True).then_inc(kc_ss, 1)
        pe.wait_ge(kc_rdy, 1)
        pe.wait_ge(n_n, 11)
        for qi in range(QT):
            for h in range(NH):
                rows = slice(CH * (h // 4), CH * (h // 4) + CH)
                last = mm(PS[:, h // 4, NCMP * (h % 4):NCMP * (h % 4 + 1)], P2[rows, 4 + h % 4, P * qi:P * (qi + 1)],
                          KCF[rows, 0:NCMP], start=True, stop=True)
            last.then_inc(cs_ps, 1)
            pe.wait_ge(cs_p, qi + 1)
            for h in range(NH):
                last = nc.tensor.transpose(PS[0:NCMP, 4 + h // 4, P * (h % 4):P * (h % 4 + 1)],
                                           CPB[:, h, :], IDENT)
            last.then_inc(ct_ps, 1)
            pe.wait_ge(ct_ev, qi + 1)
            if qi >= 1:
                pe.wait_ge(co_rdy, qi)
            for h in range(NH):
                last = mm(PS[:, 6, CH * h:CH * (h + 1)], CPT[:, h, :], VCF[:, h // 4, :], start=True, stop=True)
            last.then_inc(co_ps, 1)
        pe.wait_ge(co_rdy, QT)
        pe.wait_ge(dt_rdy, 1)
        attention(1)
        pe.wait_ge(ot_lo, 3 * QT)
        stream(pe, "wo2", outward(YH, YL))

    @block.scalar
    def _(act):
        A = nc.scalar.activation
        chain = Chain(act, act_chain)

        def hi_part(n, slot, turn, w):
            if w:
                act.wait_ge(raw_ld[slot], 16 * turn + 16)
                if not isinstance(n, int) or n >= 2:
                    act.wait_ge(mm_done, n - 1)
                A(WHI[:, slot, 0:w], RAW[:, slot, 0:w], ACT.Copy).then_inc(hi_rdy, 1)

        def next_hi(n, turn, slot, nxt):
            hi_part(n + 1, 1 - slot, turn + slot, nxt)

        def rstd(out, sums, d, scale=1.0):
            chain(A(out, sums, ACT.Ln, bias=CST[0:out.shape[0], 0:1], scale=scale / d))
            return A(out, out, ACT.Exp, scale=-0.5)

        def norm(v):
            c0, w = NORMS[v]
            sq = SQ2 if v == 2 else SQ
            for k in range(KD):
                A(sq[:, k, c0:c0 + w], H[:, k, c0:c0 + w], ACT.Square).then_inc(sq_rdy, 1)
            act.wait_ge(ss_done, v + 1)
            b = len(spans(c0, w))
            out = RSTD[:, c0:c0 + w].rearrange("p (b n) -> p b n", b=b)
            rstd(out, PS[:, 6:6 + b, 0:w // b], D_MODEL).then_inc(rstd_rdy, 1)
            if v == 4:
                return
            done = v if v < 4 else 4
            for k in range(KD):
                act.wait_ge(uf_rdy, KD * done + k + 1)
                A(UH[:, k, c0:c0 + w], sq[:, k, c0:c0 + w], ACT.Copy).then_inc(uh_rdy, 1)

        def ffn(f, c0, w):
            b = len(spans(c0, w))
            m = w // b
            for half in range(2):
                m0 = f * FJ + half * FH - START[f"f{f + 1}u{half}"]

                def up(n, j, turn, slot, nxt):
                    next_hi(n, turn, slot, nxt)
                    q = n + m0
                    act.wait_ge(mm_done, n + 1)
                    if not isinstance(q, int) or q >= 2:
                        act.wait_ge(silu_rdy, q - 1)
                    A(TANH[:, slot, 0:w].rearrange("p (b n) -> p b n", b=b),
                      PS[:, 4 * slot:4 * slot + b, 0:m], ACT.Tanh, scale=0.5).then_inc(tanh_rdy, 1)
                    act.wait_ge(evac, n + 1)
                    A(GH[:, j, c0:c0 + w], GF[:, slot, 0:w], ACT.Copy).then_inc(gh_rdy, 1)

                def down(n, j, turn, slot, nxt):
                    next_hi(n, turn, slot, nxt)

                stream(act, f"f{f + 1}u{half}", up)
                stream(act, f"f{f + 1}d{half}", down)

        def only_weights(n, j, turn, slot, nxt):
            next_hi(n, turn, slot, nxt)

        act.wait_ge(eps_rdy, 1)
        act.wait_ge(h_ld, 16)
        norm(0)
        hi_part(0, 0, 0, SLOT)
        act.wait_ge(c_ld, 16)
        A(SILUT[:, :], SILUC[:, :], ACT.Tanh, scale=0.5).then_inc(ct_rdy, 1)
        ffn(0, 0, T1)
        act.wait_ge(evac, START["w1"])
        norm(1)
        stream(act, "w1", only_weights)
        act.wait_ge(evac, START["uq"])
        for k in range(3):
            A(CF[:, k, :], PR[:, k, :], ACT.Square).then_inc(c_sq, 1)
        act.wait_ge(c_ss, 1)
        rstd(RQ[:, :], PS[:, 0, 0:SEQ], 2 * P).then_inc(c_r, 1)
        rstd(halves(RK[:, :]), PS[:, 1:3, 0:HT], P).then_inc(c_r, 1)
        act.wait_ge(c_f, 1)
        A(CHI[:, 0:2, N_META:T1], CF[:, 0:2, N_META:T1], ACT.Copy).then_inc(c_hi, 1)
        A(CHI[:, 2, :], CF[:, 2, :], ACT.Copy).then_inc(c_hi, 1)
        n = START["uq"]
        hi_part(n + 1, 1, (n + 1) // 2, WIDTH["ukv"])
        scale = float(96) ** -0.5
        for t in range(4):
            act.wait_ge(uq_ps, t + 1)
            for p in range(2):
                A(QH[0:CH, 2 * t + p, :], PS[CH * p:CH * (p + 1), t, 0:SEQ], ACT.Copy,
                  scale=scale).then_inc(q_act, 1)
        hi_part(n + 2, 0, (n + 2) // 2, WIDTH["z"])
        for t in range(4):
            act.wait_ge(kn_ps, t + 1)
            for p in range(2):
                A(halves(KH[0:CH, 2 * t + p, :]), PS[CH * p:CH * (p + 1), 2 * t:2 * t + 2, 0:HT],
                  ACT.Copy).then_inc(k_act, 1)

        def attention(part):
            U = PARTS[part]
            PB, PTS, OSB, OTF, NM, RS, RI = bufs(part)
            base = U[0]["u"]
            ends = {x["u"] - base: x for x in U if x["last"]}
            for i in range(len(U) + 7):
                if i < len(U):
                    x = U[i]
                    s, c = x["u"] % 2, x["u"] - base
                    act.wait_ge(max_rdy, x["u"] + 1)
                    if i >= 2:
                        act.wait_ge(pt_ps, x["u"] - 1)
                    A(PB[:, s, 0:x["total"]], scores(s, 0, x["total"]), ACT.Exp, bias=NM[:, c:c + 1],
                      accum_out=RS[:, c:c + 1]).then_inc(exp_rdy, 1)
                if 1 <= i <= len(U):
                    x = U[i - 1]
                    s = x["u"] % 2
                    act.wait_ge(pt_ps, x["u"] + 1)
                    if i >= 3:
                        act.wait_ge(pv_done, x["u"] - 1)
                    if x["vm"] is not None:
                        A(PTM[:, s, :], PS[0:N_META, 2 * s + 1, P:2 * P], ACT.Copy)
                    A(PTS[:, s, 0:x["w"]], PS[:, 4 + s, 0:x["w"]], ACT.Copy).then_inc(pt_rdy, 1)
                x = ends.get(i - 1)
                if x is not None and x["sink"]:
                    act.wait_ge(sink_s, x["qi"] + 1)
                    A(SNK[:, 8:16], SNK[:, 0:8], ACT.Exp).then_inc(sink_e, 1)
                x = ends.get(i - 6)
                if x is not None and x["tg"] is not None:
                    act.wait_ge(ot_f, x["tg"] + 1)
                    hi, f0 = (OTH, 0) if part == 0 else (YH, 0 if x["kind"] == "A" else 4)
                    A(hi[:, f0:f0 + 4, P * x["qi"]:P * (x["qi"] + 1)],
                      OTF[:, :].rearrange("p (f q) -> p f q", f=4), ACT.Copy).then_inc(ot_hi, 1)

        attention(0)
        for t in range(12):
            act.wait_ge(cv_c, t + 1)
            if t >= 2:
                act.wait_ge(cv_s, t - 1)
            A(GSQ[:, t % 2, :], CT[:, t % 2, :], ACT.Tanh, scale=0.5).then_inc(cv_t, 1)
        act.wait_ge(cv_s, 12)

        def l2_rstd(t):
            act.wait_ge(l_ss, t + 1)
            if t >= 2:
                act.wait_ge(l_n, t - 1)
            s = 2 * (t % 4)
            rstd(halves(GR[:, t % 2, :]), PS[:, s:s + 2, 0:HT], 1.0, scale=0.25).then_inc(l_r, 1)

        for t in range(8):
            if t >= 2:
                act.wait_ge(l_ss, t - 1)
            A(GSQ[:, t % 2, :], CV[:, t, PAD:], ACT.Square).then_inc(l_sq, 1)
            if t >= 1:
                l2_rstd(t - 1)
        l2_rstd(7)
        R8 = slice(32, 32 + NH)
        act.wait_ge(gt_d, 1)
        A(BT8[:, PAD:], PR[0:NH, 3, :], ACT.Tanh, scale=0.5).then_inc(gt_a, 1)
        A(CST[R8, 2:3], COL[R8, COLS["alog"]:COLS["alog"] + 1], ACT.Exp).then_inc(gt_a, 1)
        act.wait_ge(gt_d, 3)
        chain(A(GT[R8, 1, PAD:], GT[R8, 1, PAD:], ACT.Exp, scale=-1.0))
        A(GT[R8, 1, PAD:], GT[R8, 1, PAD:], ACT.Ln, bias=1.0).then_inc(gt_a, 1)
        act.wait_ge(gb_ps, 1)
        A(pair_rows(GB).rearrange("p t (b n) -> p (t b) n", b=2), PS[:, :, 0:NCH * CH // 2],
          ACT.Copy).then_inc(gb_ev, 1)
        act.wait_ge(dc_d, 2)
        A(EU[:, :, :], EU[:, :, :], ACT.Exp).then_inc(dc_a, 1)
        A(GP[:, 3:6, :], GP[:, 3:6, :], ACT.Exp).then_inc(dc_a, 1)
        A(GB[:, :, :], GB[:, :, :], ACT.Exp).then_inc(dc_a, 1)
        for bp in range(NB // 2):
            with act.Fori(0, LEVELS) as lv:
                for x in range(2):
                    i = 2 * lv + (2 * LEVELS * bp + x)
                    act.wait_ge(a_ps, i + 1)
                    A(AB[:, x, :, :], PS[:, 4 * x, 0:UB * CH].rearrange("p (r c) -> p r c", c=CH),
                      ACT.Copy).then_inc(ab_rdy, 1)
            for x in range(2):
                act.wait_ge(uw_ps, 2 * bp + x + 1)
                A(units(KBG, 2 * bp + x), PS[:, 4 * x + 3, 0:UB * CH].rearrange("p (r c) -> p r c", c=CH),
                  ACT.Copy).then_inc(w_rdy, 1)
        for n in range(NCH):
            act.wait_ge(o_ps, n + 1)
            A(chunk_of(EU, n), PS[:, 2 + n % 2, 0:4 * CH].rearrange("p (t c) -> p t c", c=CH),
              ACT.Copy).then_inc(o_ev, 1)
        norm(2)
        act.wait_ge(o_ev, NCH)
        A(OSQ[:, :, :], pair_rows(EU)[:, :, PAD + N_META:], ACT.Square).then_inc(osq_rdy, 1)
        act.wait_ge(oss_ps, 1)
        for i, (t, b) in enumerate(((0, 2), (2, 6))):
            ins = rstd(OR[:, t:t + 2, :], PS[:, b:b + 2, 0:SEQ], CH)
        ins.then_inc(or_rdy, 1)
        stream(act, "z", only_weights)
        act.wait_ge(evac, START["mg"])
        A(OSQ[:, :, :], ZT[:, :, :], ACT.Tanh, scale=0.5).then_inc(zt_rdy, 1)
        act.wait_ge(gof_rdy, 1)
        A(GOH[:, :, :], OR[:, :, :], ACT.Copy).then_inc(goh_rdy, 1)
        act.wait_ge(gol_rdy, 1)
        act.sem_inc(tg_rdy, 1)

        def merge(n, j, turn, slot, nxt):
            next_hi(n, turn, slot, nxt)
            d1 = turn - (START["mg"] // 2 - 1)
            if slot == 0:
                act.wait_ge(mm_done, n + 1)
                act.wait_ge(evac, n)
                A(TG[:, :, :], PS[:, 0:2, 0:SEQ], ACT.Tanh, scale=0.5).then_inc(tg_rdy, 1)
            else:
                act.wait_ge(mf_rdy, d1)
                k = d1 - 1
                A(MH[:, k, :], MF[:, 1, :], ACT.Copy).then_inc(mh_rdy, 1)

        stream(act, "mg", merge)
        stream(act, "wo", only_weights)
        act.wait_ge(evac, START["f2u0"])
        norm(3)
        ffn(1, N_META, SEQ)
        act.wait_ge(evac, START["wi"])
        norm(4)
        act.wait_ge(x2_rdy, 1)
        norm(5)
        stream(act, "wi", only_weights)
        stream(act, "wt", only_weights)
        stream(act, "wv", only_weights)
        act.wait_ge(evac, START["wo2"])

        def qk_rstd(t):
            act.wait_ge(n_ss, t + 1)
            if t >= 2:
                act.wait_ge(n_n, t - 1)
            rstd(PRS[:, t % 2, :], PS[:, t % 4, 0:SEQ], CH).then_inc(n_r, 1)

        for t in range(11):
            if t >= 2:
                act.wait_ge(n_ss, t - 1)
            A(PSQ[:, t % 2, :], P2[:, t, :], ACT.Square).then_inc(n_sq, 1)
            if t >= 1:
                qk_rstd(t - 1)
        qk_rstd(10)
        act.wait_ge(n_n, 11)
        for t in range(8):
            if t >= 2:
                act.wait_ge(z_s, t - 1)
            A(PRS[:, t % 2, :], P2[:, 13 + t, :], ACT.Tanh, scale=0.5).then_inc(z_t, 1)
        act.wait_ge(bg_d, 1)
        A(GATE[:, :, :], GATE[:, :, :], ACT.Tanh, scale=0.5).then_inc(bg_a, 1)
        act.wait_ge(hc_x, 1)
        A(HTN[:, :, 0:2 * NCMP], HC[:, :, 0:2 * NCMP], ACT.Tanh, scale=0.5).then_inc(hc_t, 1)
        act.wait_ge(kc_f, 1)
        A(PSQ[:, 0, 0:NCMP], KCF[:, 0:NCMP], ACT.Square).then_inc(kc_sq, 1)
        act.wait_ge(kc_ss, 1)
        rstd(PRS[:, 0, 0:NCMP], PS[:, 2, 0:NCMP], CH).then_inc(kc_r, 1)
        for qi in range(QT):
            act.wait_ge(cs_z, qi + 1)
            A(CPB[:, :, :], CPB[:, :, :], ACT.Exp).then_inc(cs_e, 1)
            act.wait_ge(ct_ps, qi + 1)
            A(CPT[:, :, :].rearrange("p (a h) q -> p a (h q)", a=2), PS[0:NCMP, 4:6, 0:512],
              ACT.Copy).then_inc(ct_ev, 1)
        attention(1)
        stream(act, "wo2", only_weights)

    @block.vector
    def _(dve):
        V = nc.vector
        chain = Chain(dve, dve_chain)
        TT, STT, TS = V.tensor_tensor, V.scalar_tensor_tensor, V.tensor_scalar

        def lo_part(n, slot, w):
            if w:
                dve.wait_ge(hi_rdy, n + 1)
                if not isinstance(n, int) or n >= 2:
                    dve.wait_ge(mm_done, n - 1)
                TT(WLO[:, slot, 0:w], RAW[:, slot, 0:w], WHI[:, slot, 0:w].bitcast(f32),
                   ALU.subtract).then_inc(lo_rdy, 1)

        def next_lo(n, slot, nxt):
            lo_part(n + 1, 1 - slot, nxt)

        def norm(v, gain, gain_of=None):
            c0, w = NORMS[v]
            cs = slice(c0, c0 + w)
            sq = SQ2 if v == 2 else SQ
            dve.wait_ge(rstd_rdy, v + 1)
            if v == 4:
                for k in range(KD):
                    last = STT(H[:, k, cs], H[:, k, cs], col(gain, k), RSTD[:, cs], ALU.mult, ALU.mult)
                last.then_inc(x2_rdy, 1)
                return
            done = v if v < 4 else 4
            if v < 5:
                for k in range(KD):
                    STT(sq[:, k, cs], H[:, k, cs], col(gain, k), RSTD[:, cs], ALU.mult,
                        ALU.mult).then_inc(uf_rdy, 1)
            else:
                for k in range(KD):
                    last = STT(sq[:, k, cs], H[:, k, cs], col("ng2", k), RSTD[:, cs], ALU.mult, ALU.mult)
                chain(last)
                for k in range(KD):
                    TS(sq[:, k, cs], sq[:, k, cs], MOD[:, k:k + 1], None, ALU.add).then_inc(uf_rdy, 1)
            for k in range(KD):
                dve.wait_ge(uh_rdy, KD * done + k + 1)
                TT(UL[:, k, cs], sq[:, k, cs], UH[:, k, cs].bitcast(f32), ALU.subtract)\
                    .then_inc(ul_rdy, 1)

        def ada(m, slot, turn):
            dve.wait_ge(ada_ld[slot], 16 * turn + 16)
            if not isinstance(m, int) or m >= 1:
                dve.wait_ge(ada_used, m)
            STT(JUNK[:, :], ADA[:, slot, :], 0.5, SILUC[:, :], ALU.mult, ALU.mult,
                accum_out=MOD[:, bass.ds(m, 1)] if not isinstance(m, int) else MOD[:, m:m + 1])\
                .then_inc(ada_used, 1)

        def ffn(f, c0, w):
            b = len(spans(c0, w))
            m = w // b
            wide = lambda t: t.rearrange("p (b n) -> p b n", b=b)
            for half in range(2):
                n0 = START[f"f{f + 1}u{half}"]
                m0 = f * FJ + half * FH - n0

                def up(n, j, turn, slot, nxt):
                    next_lo(n, slot, nxt)
                    q = n + m0
                    if f == 0:
                        ada(q, (slot + m0) % 2, turn + (slot + m0) // 2)
                    ps = PS[:, 4 * slot:4 * slot + 4, 0:m]
                    dve.wait_ge(tanh_rdy, q + 1)
                    STT(wide(SILU[:, slot, 0:w]), wide(TANH[:, slot, 0:w]), 1.0, ps[:, 0:b, :], ALU.add,
                        ALU.mult).then_inc(silu_rdy, 1)
                    dve.wait_ge(silu_rdy, q + 1)
                    if not isinstance(q, int) or q >= 2:
                        dve.wait_ge(gl_rdy, q - 1)
                    TT(wide(GF[:, slot, 0:w]), wide(SILU[:, slot, 0:w]), ps[:, 2:2 + b, :],
                       ALU.mult).then_inc(evac, 1)
                    dve.wait_ge(gh_rdy, q + 1)
                    TT(GL[:, j, c0:c0 + w], GF[:, slot, 0:w], GH[:, j, c0:c0 + w].bitcast(f32),
                       ALU.subtract).then_inc(gl_rdy, 1)

                def down(n, j, turn, slot, nxt):
                    next_lo(n, slot, nxt)
                    dve.wait_ge(mm_done, n + 1)
                    h = wide(H[:, j, c0:c0 + w])
                    STT(h, PS[:, 4 * slot:4 * slot + b, 0:m], 0.25, h, ALU.mult, ALU.add)\
                        .then_inc(evac, 1)

                stream(dve, f"f{f + 1}u{half}", up)
                stream(dve, f"f{f + 1}d{half}", down)

        V.memset(CST[:, 0:1], EPS).then_inc(eps_rdy, 1)
        dve.wait_ge(rev_ps, 1)
        V.tensor_copy(JUNK[0:16, 0:383], PS[0:16, 0, 0:383]).then_inc(rev_rdy, 1)
        dve.wait_ge(col_ld, 16)
        norm(0, "ffn1")
        lo_part(0, 0, SLOT)
        dve.wait_ge(ct_rdy, 1)
        dve.wait_ge(rev_st, 32)
        chain(STT(SILUC[:, :], SILUT[:, :], 1.0, SILUC[:, :], ALU.add, ALU.mult))
        ffn(0, 0, T1)
        for m in range(FJ, 24):
            ada(m, m % 2, m // 2)
        dve.wait_ge(ada_used, 24)
        chain(TT(MOD[:, :], MOD[:, :], col("bada", 0, 24), ALU.add))
        chain(STT(col("ng2", 0, 8), MOD[:, 8:16], 1.0, col("ng2", 0, 8), ALU.add, ALU.mult))
        chain(TS(col("qa", 0, 2), col("qa", 0, 2), 0.125, None, ALU.mult))
        norm(1, "mix")

        def project(dst, w, per):
            def body(n, j, turn, slot, nxt):
                next_lo(n, slot, nxt)
                dve.wait_ge(mm_done, n + 1)
                if w > 512:
                    for t in range(2):
                        last = V.tensor_copy(halves(dst[:, 2 * j + t, :]),
                                             PS[:, 4 * slot + 2 * t:4 * slot + 2 * t + 2, 0:HT])
                        if t == 0:
                            last.then_inc(dve_chain, 1)
                else:
                    last = V.tensor_copy(dst[:, bass.ds(2 * j, 2), :], PS[:, 4 * slot:4 * slot + 2, 0:SEQ])
                last.then_inc(evac, 1)
            return body

        stream(dve, "w1", project(PR, T1, 2))
        chain.n += COUNT["w1"]
        dve.wait_ge(dve_chain, chain.n)
        dve.wait_ge(c_ss, 1)
        dve.wait_ge(c_r, 2)
        for k in range(2):
            last = STT(CF[:, k, N_META:T1], PR[:, k, N_META:T1], col("qn", k), RQ[:, :], ALU.mult, ALU.mult)
        last = STT(CF[:, 2, :], PR[:, 2, :], col("kvn"), RK[:, :], ALU.mult, ALU.mult)
        last.then_inc(c_f, 1)
        dve.wait_ge(c_hi, 2)
        TT(CLO[:, 0:2, N_META:T1], CF[:, 0:2, N_META:T1], CHI[:, 0:2, N_META:T1].bitcast(f32), ALU.subtract)
        TT(CLO[:, 2, :], CF[:, 2, :], CHI[:, 2, :].bitcast(f32), ALU.subtract).then_inc(c_lo, 1)
        n = START["uq"]
        lo_part(n + 1, 1, WIDTH["ukv"])
        scale = float(96) ** -0.5
        cos, sin = tab("cos", 0, T1), tab("sin", 0, T1)
        dve.wait_ge(uq_ps, 8)
        for r in range(2):
            STT(ROT[:, r, :], PS[:, 4 + r, 0:SEQ], scale, cos[:, N_META:T1], ALU.mult, ALU.mult)
            last = STT(ROT[:, 2 + r, :], PS[:, 6 + r, 0:SEQ], scale, sin[:, N_META:T1], ALU.mult, ALU.mult)
        chain(last)
        for h in range(NH):
            rows = slice(32 * (h % 4), 32 * (h % 4) + 32)
            last = TT(QH[CH:96, h, :], ROT[rows, h // 4, :], ROT[rows, 2 + h // 4, :], ALU.add)
        chain(last)
        dve.wait_ge(q_act, NH)
        dve.sem_inc(evac, 1)
        lo_part(n + 2, 0, WIDTH["z"])
        dve.wait_ge(mm_done, n + 2)
        TT(KROT[CH:96, 0, :], PR[CH:96, 3, :], cos[CH:96, :], ALU.mult)
        chain(TT(KROT[CH:96, 1, :], PR[96:128, 3, :], sin[96:128, :], ALU.mult))
        for h in range(NH):
            last = TT(KH[CH:96, h, :], KROT[CH:96, 0, :], KROT[CH:96, 1, :], ALU.add)
        last.then_inc(kr_dve, 1)
        chain(V.tensor_copy(VM[0:N_META, 0, :], PS[0:N_META, 0, 0:SEQ]))
        for t in range(1, 5):
            last = V.tensor_copy(VM[:, t, :], PS[:, t, 0:SEQ])
        chain(last)
        dve.wait_ge(kr_dve, 1)
        dve.sem_inc(evac, 1)

        def attention(part):
            U = PARTS[part]
            PB, PTS, OSB, OTF, NM, RS, RI = bufs(part)
            base, gbase = U[0]["u"], U[0]["g"]
            ends = {x["u"] - base: x for x in U if x["last"]}
            for i in range(len(U) + 8):
                if i < len(U):
                    x = U[i]
                    s, c = x["u"] % 2, x["u"] - base
                    a, n, bias = x["bias"]
                    dve.wait_ge(s_ps, x["u"] + 1)
                    chain(TT(scores(s, a, a + n), scores(s, a, a + n), bias, ALU.add))
                    red = V.tensor_reduce(NM[:, c:c + 1], scores(s, 0, x["total"]), AX.X, ALU.max,
                                          negate=True)
                    if x["sink"]:
                        chain(red)
                        red = TT(NM[:, c:c + 1], NM[:, c:c + 1], NSINK[:, x["h"]:x["h"] + 1], ALU.min)
                    red.then_inc(max_rdy, 1)
                x = ends.get(i - 1)
                if x is not None and x["sink"]:
                    c = x["u"] - base
                    dve.wait_ge(max_rdy, x["u"] + 1)
                    if x["qi"] > 0:
                        dve.wait_ge(sink_e, x["qi"])
                    TT(SNK[:, 0:8], NM[:, c - 7:c + 1], col("sink", 0, 8), ALU.add).then_inc(sink_s, 1)
                x = ends.get(i - 2)
                if x is not None:
                    c, g, qi = x["u"] - base, x["g"], x["qi"]
                    rs, ri = RS[:, c - 7:c + 1], RI[:, c - 7:c + 1]
                    dve.wait_ge(pv_done, x["u"] + 1)
                    if x["sink"]:
                        dve.wait_ge(sink_e, qi + 1)
                        chain(TT(rs, rs, SNK[:, 8:16], ALU.add))
                    chain(V.reciprocal(ri, rs))
                    o = PS[:, 6, :].rearrange("p (h d) -> p h d", h=NH)
                    if x["kind"] in ("sel", "win"):
                        g_col = GATE[:, qi, :].rearrange("p (h b) -> p b h", b=3)[:, 1 if x["kind"] == "sel" else 2, :]
                        chain(TT(ri, ri, g_col, ALU.mult))
                    tg = x["tg"] if x["tg"] is not None else U[c + NH]["tg"]
                    osb = OSB[:, tg % 2, :]
                    wide = lambda t: t.rearrange("p (h d) -> p h d", h=NH)
                    norm8 = ri.unsqueeze(2).to_broadcast([P, NH, CH])
                    if x["kind"] == "win":
                        TT(wide(OBT[:, :]), o, norm8, ALU.mult).then_inc(o_free, 1)
                        dve.wait_ge(o_free, g + 1)
                        chain(TT(osb, osb, OBT[:, :], ALU.add))
                        TT(osb, osb, OC[:, qi, :], ALU.add).then_inc(o_rdy, 1)
                    else:
                        if tg >= 2:
                            dve.wait_ge(ot_ps, tg - 1)
                        TT(wide(osb), o, norm8, ALU.mult).then_inc(o_free, 1)
                        dve.wait_ge(o_free, g + 1)
                        if x["kind"] != "sel":
                            dve.sem_inc(o_rdy, 1)
                x = ends.get(i - 5)
                if x is not None and x["tg"] is not None:
                    dve.wait_ge(ot_ps, x["tg"] + 1)
                    if x["tg"] > 0:
                        dve.wait_ge(ot_lo, x["tg"])
                    ps = PS[:, 7, :].rearrange("p (f q) -> p f q", f=4)
                    otf = OTF[:, :].rearrange("p (f q) -> p f q", f=4)
                    if part == 0:
                        V.tensor_copy(otf, ps).then_inc(ot_f, 1)
                    else:
                        f0 = 13 if x["kind"] == "A" else 17
                        STT(otf, ps, 0.5, P2[:, f0:f0 + 4, P * x["qi"]:P * (x["qi"] + 1)], ALU.mult,
                            ALU.mult).then_inc(ot_f, 1)
                x = ends.get(i - 7)
                if x is not None and x["tg"] is not None:
                    dve.wait_ge(ot_hi, x["tg"] + 1)
                    hi, lo, f0 = (OTH, OTL, 0) if part == 0 else (YH, YL, 0 if x["kind"] == "A" else 4)
                    sl = slice(P * x["qi"], P * (x["qi"] + 1))
                    TT(lo[:, f0:f0 + 4, sl], OTF[:, :].rearrange("p (f q) -> p f q", f=4),
                       hi[:, f0:f0 + 4, sl].bitcast(f32), ALU.subtract).then_inc(ot_lo, 1)

        attention(0)
        dve.wait_ge(ot_lo, QT)
        V.memset(CV[:, :, 0:PAD], 0.0).then_inc(dve_chain, 1)
        chain.n += 1

        def conv_silu(t):
            dve.wait_ge(cv_t, t + 1)
            STT(CV[:, t, PAD:], GSQ[:, t % 2, :], 1.0, CT[:, t % 2, :], ALU.add, ALU.mult)\
                .then_inc(cv_s, 1)

        for t in range(12):
            y, x = CT[:, t % 2, :], PR[:, 4 + t, :]
            if t >= 2:
                dve.wait_ge(cv_s, t - 1)
            chain(TS(y, x, col("conv", 4 * t + 3), None, ALU.mult))
            for d in (1, 2, 3):
                ins = STT(y[:, d:T1], x[:, 0:T1 - d], col("conv", 4 * t + 3 - d), y[:, d:T1], ALU.mult,
                          ALU.add)
                if d < 3:
                    chain(ins)
            ins.then_inc(cv_c, 1)
            if t >= 1:
                conv_silu(t - 1)
        conv_silu(11)
        dve.wait_ge(cv_s, 12)
        for t in range(8):
            dve.wait_ge(l_r, t + 1)
            STT(CV[:, t, PAD:], CV[:, t, PAD:], 0.0625 if t < 4 else 0.5, GR[:, t % 2, :], ALU.mult,
                ALU.mult).then_inc(l_n, 1)
        R8 = slice(32, 32 + NH)
        V.memset(GT[R8, 3, 0:PAD], 0.0)
        V.memset(GT[R8, 4, :], 1.0).then_inc(dve_chain, 1)
        chain.n += 1
        V.memset(BT8[:, 0:PAD], 0.0).then_inc(gt_d, 1)
        dve.wait_ge(dve_chain, chain.n)
        chain(V.memset(GT[R8, 4, :].rearrange("p (n c) -> p n c", c=CH)[:, :, 0:1], 0.0))
        x = GT[R8, 0, PAD:]
        TS(x, PR[R8, 3, :], COL[R8, COLS["dtb"]:COLS["dtb"] + 1], None, ALU.add).then_inc(gt_d, 1)
        dve.wait_ge(gt_d, 2)
        chain(TS(GT[R8, 1, PAD:], x, -1.0, None, ALU.mult))
        TT(GT[R8, 1, PAD:], x, GT[R8, 1, PAD:], ALU.max).then_inc(gt_d, 1)
        dve.wait_ge(gt_a, 1)
        TS(BT8[:, PAD:], BT8[:, PAD:], 1.0, 0.5, ALU.add, ALU.mult).then_inc(gt_d, 1)
        dve.wait_ge(gt_a, 3)
        STT(GT[R8, 3, PAD:], x, 0.0, GT[R8, 1, PAD:], ALU.max, ALU.add).then_inc(gt_d, 1)
        dve.wait_ge(gt_d, 5)
        TS(GT[R8, 3, PAD:], GT[R8, 3, PAD:], CST[R8, 2:3], -1.0, ALU.mult, ALU.mult).then_inc(gt_d, 1)
        dve.wait_ge(gt_d, 6)
        V.tensor_tensor_scan(GT[R8, 2, :], GT[R8, 4, :], GT[R8, 3, :], 0.0, ALU.mult, ALU.add)\
            .then_inc(gt_d, 3)
        dve.wait_ge(bb_ps, 1)
        dve.wait_ge(l_n, 8)
        W2 = NCH * CH // 2
        V.tensor_copy(pair_rows(TTT).rearrange("p t (b n) -> p (t b) n", b=2), PS[:, :, 0:W2])\
            .then_inc(bb_ev, 1)
        dve.wait_ge(bb_ev, 1)
        i64 = over(tab("i64", 0, CH), NU)
        chain(TT(IT[:, :, :], TTT[:, :, :], i64, ALU.mult))
        chain(V.tensor_reduce(GP[:, 0, :], IT[:, :, :], AX.X, ALU.add))
        dve.wait_ge(gb_ev, 1)
        chain(TT(IT[:, :, :], GB[:, :, :], i64, ALU.mult))
        chain(V.tensor_reduce(GP[:, 1, :], IT[:, :, :], AX.X, ALU.add))
        chain(TT(EU[:, :, :], GB[:, :, :], along(GP[:, 1, :], NU), ALU.subtract))
        TS(EU[:, :, :], EU[:, :, :], 0.0, None, ALU.min).then_inc(dc_d, 1)
        chain(V.tensor_copy(GP[:, 2, :], GB[:, :, CH - 1]))
        V.tensor_copy(GP[:, 3, :], GP[:, 1, :])
        V.tensor_copy(GP[:, 4, :], GP[:, 2, :])
        chain(TT(GP[:, 5, :], GP[:, 2, :], GP[:, 1, :], ALU.subtract))
        chain(TS(GP[:, 6, :], GP[:, 0, :], 0.5, None, ALU.mult))
        dve.sem_inc(dc_d, 1)
        chain(TT(pair_rows(TTT), CV[:, 4:8, :], pair_rows(TTT), ALU.mult))
        dve.wait_ge(dc_a, 2)
        TT(GP[:, 7, :], GP[:, 0, :], GP[:, 3, :], ALU.mult)
        chain(TT(EU[:, :, :], EU[:, :, :], over(tab("mincl", 0, CH), NU), ALU.mult))
        dve.wait_ge(dc_a, 3)
        chain(TT(pair_rows(GB), CV[:, 0:4, :], pair_rows(GB), ALU.mult))
        dve.sem_inc(un_rdy, 1)
        for b in range(NB):
            dve.wait_ge(pr_ps, b + 1)

            def bank(i):
                return PS[:, 4 * (b % 2) + i, 0:UB * CH].rearrange("p (r c) -> p r c", c=CH)

            def value(i):
                return along(GP[:, i, b * UB:(b + 1) * UB], UB)

            chain(TT(units(IT, b), bank(1), units(EU, b), ALU.mult))
            chain(TT(units(EU, b), bank(0), units(EU, b), ALU.mult))
            TT(units(EU, b), units(EU, b), over(tab("mstrict", 0, CH), UB), ALU.mult)
            TT(units(KBG, b), bank(2), value(7), ALU.mult)
            TT(units(KDEC, b), bank(2), value(5), ALU.mult)
            chain(TT(units(VB, b), bank(3), value(6), ALU.mult))
            dve.sem_inc(pr_rdy, 1)
        LVL = TAB[:, TABS["lvl"]:TABS["lvl"] + LEVELS * CH].rearrange("p (l c) -> p l c", c=CH)
        dve.wait_ge(gt_d, 9)
        for bp in range(NB // 2):
            if bp:
                dve.wait_ge(uw_ps, 2 * bp)
            for x in range(2):
                chain(V.tensor_copy(TB[:, x, :, :], over(tab("i64", 0, CH), UB)))
                V.tensor_copy(units(TTT, 2 * bp + x), over(tab("i64", 0, CH), UB)).then_inc(t_rdy, 1)
            with dve.Fori(0, LEVELS) as lv:
                for x in range(2):
                    b = 2 * bp + x
                    mask = LVL[:, bass.ds(lv, 1), :].to_broadcast([P, UB, CH])
                    TT(UMB[:, x, :, :], units(EU, b), mask, ALU.mult).then_inc(um_rdy, 1)
                for x in range(2):
                    b = 2 * bp + x
                    i = 2 * lv + (2 * LEVELS * bp + x)
                    dve.wait_ge(d_ps, i + 1)

                    def bank(k):
                        return PS[:, 4 * x + k, 0:UB * CH].rearrange("p (r c) -> p r c", c=CH)

                    TT(TB[:, x, :, :], TB[:, x, :, :], bank(1), ALU.subtract).then_inc(tb_rdy, 1)
                    dve.wait_ge(tb_rdy, i + 1)
                    TT(units(TTT, b), units(TTT, b), bank(2), ALU.subtract).then_inc(t_rdy, 1)
            for x in range(2):
                b = 2 * bp + x
                dve.wait_ge(uw_ps, b + 1)
                V.tensor_copy(units(VB, b), PS[:, 4 * x, 0:UB * CH].rearrange("p (r c) -> p r c", c=CH))\
                    .then_inc(u_rdy, 1)
        chain(V.memset(SV[:, 0, :, :], 0.0))
        dve.sem_inc(st_rdy, 1)
        for n in range(NCH):
            ws = PS[:, 0, 0:4 * CH].rearrange("p (t c) -> p t c", c=CH)
            sa = PS[:, 1, 0:4 * CH].rearrange("p (t c) -> p t c", c=CH)
            if n < NCH - 1:
                egl = GP[:, 4, :].rearrange("p (t n) -> p t n", n=NCH)[:, :, n:n + 1].to_broadcast([P, 4, CH])
                TT(SE[:, :, :], SV[:, n % 2, :, :], egl, ALU.mult).then_inc(se_rdy, 1)
            if n >= 2:
                dve.wait_ge(o_ps, n - 1)
            dve.wait_ge(ws_ps, n + 1)
            TT(VN[:, n % 2, :, :], chunk_of(VB, n), ws, ALU.subtract).then_inc(vn_rdy, 1)
            if n < NCH - 1:
                dve.wait_ge(se_rdy, n + 1)
                dve.wait_ge(sa_ps, n + 1)
                if n >= 1:
                    dve.wait_ge(o_ps, n)
                TT(SV[:, (n + 1) % 2, :, :], SE[:, :, :], sa, ALU.add).then_inc(st_rdy, 1)
                dve.wait_ge(st_rdy, n + 2)
        dve.wait_ge(o_ev, NCH)
        norm(2, "mix")
        dve.wait_ge(or_rdy, 1)
        STT(OR[:, :, :], pair_rows(EU)[:, :, PAD + N_META:], col("gdn"), OR[:, :, :], ALU.mult, ALU.mult)\
            .then_inc(dve_chain, 1)
        chain.n += 1
        stream(dve, "z", project(ZT, SEQ, 2))
        dve.wait_ge(dve_chain, chain.n)
        dve.wait_ge(zt_rdy, 1)
        chain(STT(ZT[:, :, :], OSQ[:, :, :], 1.0, ZT[:, :, :], ALU.add, ALU.mult))
        STT(OR[:, :, :], OR[:, :, :], 0.5, ZT[:, :, :], ALU.mult, ALU.mult).then_inc(gof_rdy, 1)
        dve.wait_ge(goh_rdy, 1)
        TT(GOL[:, :, :], OR[:, :, :], GOH[:, :, :].bitcast(f32), ALU.subtract).then_inc(gol_rdy, 1)

        def merge(n, j, turn, slot, nxt):
            next_lo(n, slot, nxt)
            if slot == 0:
                return
            d1 = turn - (START["mg"] // 2 - 1)
            dve.wait_ge(mm_done, n + 1)
            dve.wait_ge(tg_rdy, d1 + 1)
            dve.wait_ge(ml_rdy, d1)
            TT_ = STT(MF[:, 0, :], TG[:, 0, :], 1.0, PS[:, 4, 0:SEQ], ALU.add, ALU.mult)
            STT(MF[:, 1, :], TG[:, 1, :], 1.0, PS[:, 5, 0:SEQ], ALU.add, ALU.mult).then_inc(evac, 2)
            dve.wait_ge(evac, n + 1)
            TT(MF[:, 1, :], MF[:, 0, :], MF[:, 1, :], ALU.add).then_inc(mf_rdy, 1)
            dve.wait_ge(mh_rdy, d1)
            TT(ML[:, d1 - 1, :], MF[:, 1, :], MH[:, d1 - 1, :].bitcast(f32), ALU.subtract)\
                .then_inc(ml_rdy, 1)

        dve.sem_inc(ml_rdy, 1)
        stream(dve, "mg", merge)

        def outward(n, j, turn, slot, nxt):
            next_lo(n, slot, nxt)
            dve.wait_ge(mm_done, n + 1)
            h = H[:, bass.ds(2 * j, 2), N_META:T1]
            STT(h, PS[:, 4 * slot:4 * slot + 2, 0:SEQ], 0.5, h, ALU.mult, ALU.add).then_inc(evac, 1)

        stream(dve, "wo", outward)
        norm(3, "ffn2")
        ffn(1, N_META, SEQ)
        norm(4, "fin")
        dve.wait_ge(x2_rdy, 1)
        norm(5, "ng2")
        stream(dve, "wi", project(P2, SEQ, 2))
        n = START["wt"]
        next_lo(n, n % 2, WIDTH["wv"])
        dve.wait_ge(mm_done, n + 1)
        V.tensor_copy(P2[:, 20, :], PS[:, 4 * (n % 2), 0:SEQ]).then_inc(evac, 1)
        n = START["wv"]
        next_lo(n, n % 2, WIDTH["wv"])
        next_lo(n + 1, (n + 1) % 2, WIDTH["wo2"])
        dve.wait_ge(mm_done, n + 2)
        V.tensor_copy(VT[:, :, :], PS[:, 4:8, 0:TOKEN_COLS]).then_inc(evac, 2)
        dve.wait_ge(evac, START["wo2"])
        TT(GATE[:, :, :], VT[:, :, 384:408], col("bg", 0, 24).unsqueeze(1).to_broadcast([P, QT, 24]),
           ALU.add).then_inc(bg_d, 1)
        for kv in range(2):
            src = P2[:, 11 + kv, :]
            for g in range(2):
                rows = slice(CH * g, CH * (g + 1))
                V.tensor_copy(XC[0:CH, kv, g, :], src[rows, :])
                last = V.tensor_copy(XC[CH:P, kv, g, 0:SEQ - 1], src[rows, 1:SEQ])
            last.then_inc(xc_rdy, 1)
        gains = ["qa"] * 4 + ["qb"] * 4 + ["ka", "ks", "kw"]
        for t in range(11):
            dve.wait_ge(n_r, t + 1)
            STT(P2[:, t, :], P2[:, t, :], col(gains[t]), PRS[:, t % 2, :], ALU.mult, ALU.mult)\
                .then_inc(n_n, 1)
        for t in range(8):
            dve.wait_ge(z_t, t + 1)
            STT(P2[:, 13 + t, :], PRS[:, t % 2, :], 1.0, P2[:, 13 + t, :], ALU.add, ALU.mult)\
                .then_inc(z_s, 1)
        dve.wait_ge(bg_a, 1)
        chain(TS(GATE[:, :, :], GATE[:, :, :], 1.0, 0.5, ALU.add, ALU.mult))
        dve.wait_ge(dt_ld, 32)
        for h in range(NH):
            TT(DT[:, h, :], DT[:, h, :], tab("mA", 0, 256), ALU.add)
            last = STT(DT[:, 8 + h, :], DT[:, 8 + h, :], B31[:, 8 + h:9 + h], tab("mB", 0, 256),
                       ALU.subtract, ALU.add)
        chain(last)
        chain(TS(NSINK[:, :], col("sink", 0, 8), -1.0, None, ALU.mult))
        dve.sem_inc(dt_rdy, 1)
        dve.wait_ge(hc_ps, 1)
        chain(V.tensor_copy(CB[:, :], PS[:, 4:8, 0]))
        for i in range(4):
            last = TS(HC[:, i, 0:2 * NCMP], PS[:, i, 0:2 * NCMP], CB[:, i:i + 1], None, ALU.add)
        last.then_inc(hc_x, 1)
        dve.wait_ge(hc_t, 1)
        STT(HC[:, :, 0:2 * NCMP], HTN[:, :, 0:2 * NCMP], 1.0, HC[:, :, 0:2 * NCMP], ALU.add, ALU.mult)\
            .then_inc(hc_rdy, 1)
        dve.wait_ge(kc_ps, 1)
        TS(KCF[:, 0:NCMP], PS[:, 0, 0:NCMP], 0.5, None, ALU.mult).then_inc(kc_f, 1)
        TS(VCF[:, :, :], PS[0:NCMP, 1, 0:P].rearrange("p (g d) -> p g d", g=2), 0.5, None, ALU.mult)\
            .then_inc(dve_chain, 1)
        chain.n += 1
        dve.wait_ge(dve_chain, chain.n)
        dve.wait_ge(kc_r, 1)
        dve.wait_ge(kc_f, 1)
        STT(KCF[:, 0:NCMP], KCF[:, 0:NCMP], col("kc"), PRS[:, 0, 0:NCMP], ALU.mult, ALU.mult)\
            .then_inc(kc_rdy, 1)
        for qi in range(QT):
            def masks(name, n=NH):
                m = tab(name, qi * NCMP, (qi + 1) * NCMP)
                return m.unsqueeze(1).to_broadcast([P, n, NCMP])

            def heads(ap):
                return ap.unsqueeze(2).to_broadcast([P, NH, NCMP])

            dve.wait_ge(cs_ps, qi + 1)
            if qi >= 1:
                dve.wait_ge(ct_ps, qi)
            for g in range(2):
                last = TT(CPB[:, 4 * g:4 * g + 4, :],
                          PS[:, g, 0:4 * NCMP].rearrange("p (h n) -> p h n", h=4),
                          masks("cneg", 4), ALU.add)
            chain(last)
            chain(V.tensor_reduce(M8[:, 0, :], CPB[:, :, :], AX.X, ALU.max))
            TT(CPB[:, :, :], CPB[:, :, :], heads(M8[:, 0, :]), ALU.subtract).then_inc(cs_z, 1)
            dve.wait_ge(cs_e, qi + 1)
            TT(CPB[:, :, :], CPB[:, :, :], masks("c01"), ALU.mult).then_inc(cs_p, 1)
            dve.wait_ge(cs_p, qi + 1)
            chain(V.tensor_reduce(M8[:, 1, :], CPB[:, :, :], AX.X, ALU.add))
            chain(TS(M8[:, 1, :], M8[:, 1, :], 1e-30, None, ALU.max))
            chain(V.reciprocal(M8[:, 2, :], M8[:, 1, :]))
            chain(TT(M8[:, 3, :], M8[:, 2, :], GATE[:, qi, :].rearrange("p (h b) -> p b h", b=3)[:, 0, :],
                     ALU.mult))
            dve.wait_ge(co_ps, qi + 1)
            TT(OC[:, qi, :].rearrange("p (h d) -> p h d", h=NH), PS[:, 6, :].rearrange("p (h d) -> p h d", h=NH),
               M8[:, 3, :].unsqueeze(2).to_broadcast([P, NH, CH]), ALU.mult).then_inc(co_rdy, 1)
        dve.wait_ge(co_rdy, QT)
        attention(1)

        def last_product(n, j, turn, slot, nxt):
            next_lo(n, slot, nxt)
            dve.wait_ge(mm_done, n + 1)
            for t in range(2):
                h = H[:, bass.ds(2 * j + t, 1), N_META:T1] if not isinstance(j, int) else \
                    H[:, 2 * j + t:2 * j + t + 1, N_META:T1]
                m = MOD[:, bass.ds(2 * j + 16 + t, 1)] if not isinstance(j, int) else \
                    MOD[:, 2 * j + 16 + t:2 * j + 17 + t]
                last = STT(h, PS[:, 4 * slot + t:4 * slot + t + 1, 0:SEQ], m, h, ALU.mult, ALU.add)
                if t == 0:
                    last.then_inc(dve_chain, 1)
            last.then_inc(evac, 1)

        stream(dve, "wo2", last_product)

    ctx.close()


def tables():
    t = np.zeros((P, NTAB), np.float32)

    def put(name, a):
        t[:a.shape[0], TABS[name]:TABS[name] + a.shape[1]] = a

    p = np.arange(P)
    put("ident", np.eye(P))
    put("ones", np.ones((P, P)))
    put("bones", (p[:, None] // CH == p[None] // CH).astype(np.float32))
    pos = np.arange(T1, dtype=np.float32)
    inv = np.float32(10000.0) ** (-np.arange(0, 32, 2, dtype=np.float32) / np.float32(32))
    ang = (pos[:, None] * inv[None, :]).astype(np.float32)
    put("cos", np.cos(ang).T[p % 16])
    put("sin", np.sin(ang).T[p % 16] * np.where(p % 32 < 16, -1, 1)[:, None])
    k = np.arange(256)
    dist = P + p[:, None] - k[None]
    put("mA", np.where((dist >= 0) & (dist < P), 0, NEG))
    put("mB", np.where(dist >= 0, 0, NEG))
    n = np.arange(NCMP)
    ok = np.stack([(16 * n[None] + 31) <= (P * q + p[:, None]) for q in range(QT)], 1).reshape(P, -1)
    put("cneg", np.where(ok, 0, NEG))
    put("c01", ok.astype(np.float32))
    s, c = (p % CH)[:, None], np.arange(CH)[None]
    put("i64", (s == c).astype(np.float32))
    put("mincl", (c >= s).astype(np.float32))
    put("mstrict", (c > s).astype(np.float32))
    put("lvl", np.concatenate([((s // (2 << l) == c // (2 << l)) & (s // (1 << l) % 2 == 0)
                                & (c // (1 << l) % 2 == 1)).astype(np.float32) for l in range(LEVELS)], 1))
    sel = np.zeros((40, 4 * P), np.float32)
    for h in range(NH):
        sel[h, P * (h // 2) + CH * (h % 2):P * (h // 2) + CH * (h % 2 + 1)] = 1
    sel[32:40] = sel[0:8]
    put("sel", sel)
    d = 255 - np.arange(383)
    nn = np.maximum(d, 0)
    nf = np.maximum(nn, 1).astype(np.float32)
    large = 16 + (np.log(nf / np.float32(16)) / np.float32(np.log(8.0)) * np.float32(16)).astype(np.int32)
    bucket = np.where(nn < 16, nn, np.minimum(large, 31))
    put("oh", (np.arange(32)[:, None] == bucket[None]).astype(np.float32))
    return t


def tiled(w):
    k, n = w.shape
    return np.ascontiguousarray(w.reshape(k // P, P, n // P, P).transpose(2, 1, 0, 3).reshape(n // P, P, k))


def pairs(t):
    n, p, k = t.shape
    return np.ascontiguousarray(t.reshape(n // 2, 2, p, k).transpose(0, 2, 1, 3).reshape(n // 2, p, 2 * k))


def lay_out(x):
    a = {}
    h = np.concatenate([x["meta_tokens"], x["x"][0]], axis=0)
    a["h"] = np.ascontiguousarray(h.T.reshape(KD, P, T1))
    a["tabs"] = tables()
    for f in (1, 2):
        g, u, d = (tiled(x[f"ffn{f}_w_{n}"][0]) for n in ("gate", "up", "down"))
        for half in range(2):
            js = slice(half * FH, (half + 1) * FH)
            a[f"f{f}u{half}"] = np.ascontiguousarray(np.concatenate([g[js], u[js]], axis=2))
            a[f"f{f}d{half}"] = np.ascontiguousarray(d[:, :, half * FH * P:(half + 1) * FH * P])
    w = x["w_in"][0]
    misc = np.zeros((D_MODEL, P), np.float32)
    kr = w[:, 384:416]
    misc[:, 0:8], misc[:, 32:40], misc[:, 64:96] = w[:, 1952:1960], w[:, 1960:1968], kr
    misc[:, 96:112], misc[:, 112:128] = kr[:, 16:32], kr[:, 0:16]
    a["w1"] = pairs(tiled(np.concatenate([w[:, 0:384], misc, w[:, 416:1952]], axis=1)))
    a["z"] = pairs(tiled(w[:, 1968:2480]))
    gm, gg = tiled(w[:, 2480:3504]), tiled(w[:, 3504:4528])
    mo, go = tiled(x["w_mla_o"][0]), tiled(x["w_gdn_o"][0])
    mg = np.zeros((16, P, SLOT), np.float32)
    mg[0::2] = np.concatenate([gm, gg], axis=2)
    mg[1::2, :, 0:SLOT // 2] = np.concatenate([mo, go], axis=2)
    a["mg"] = mg
    uq = x["w_uq"][0].reshape(256, NH, 96)
    rope = uq[:, :, 64:96]
    swap = np.concatenate([rope[:, :, 16:32], rope[:, :, 0:16]], axis=2)
    a["uq"] = tiled(np.concatenate([uq[:, :, 0:64].reshape(256, 512), rope.reshape(256, 256),
                                    swap.reshape(256, 256)], axis=1)).transpose(1, 0, 2).reshape(1, P, SLOT)
    ukv = x["w_ukv"][0].reshape(P, NH, 128)
    a["ukv"] = np.concatenate([ukv[:, :, 0:64].reshape(P, 512), ukv[:, :, 64:128].reshape(P, 512)], axis=1)[None]
    a["wo"] = pairs(tiled(x["w_out"][0]))
    w = x["w_in_2"][0]
    at = np.cumsum([0, 512, 128, 128, 512, 512, 128, 128, 128, 128, 128, 128, 512, 24])
    qa, ka, va, za, qb, kc, vc, ks, vs, kw, vw, zb, gb = (w[:, at[i]:at[i + 1]] for i in range(13))

    def heads(q):
        return q.reshape(D_MODEL, 2, 4, CH).transpose(0, 2, 1, 3).reshape(D_MODEL, 512)

    t = tiled(np.concatenate([heads(qa), heads(qb), ka, ks, kw, kc, vc, za, zb], axis=1))
    a["wi"], a["wt"] = pairs(t[:20]), t[20:21]
    wv = np.concatenate([va, vs, vw, gb], axis=1)
    a["wv"] = wv.reshape(2, 4, P, TOKEN_COLS).transpose(0, 2, 1, 3).reshape(2, P, 4 * TOKEN_COLS)
    a["wo2"] = pairs(tiled(x["w_out_2"][0]))
    for n in ("k", "v"):
        a["w1" + n] = x[f"w_cmp_{n}1_2"][0].reshape(16, P, 256).transpose(1, 0, 2)
    a["w2"] = np.stack([x[f"w_cmp_{n}2_2"][0].reshape(2, P, CH).transpose(1, 0, 2) for n in ("k", "v")], axis=1)
    a["ada"] = x["w_ada_2"][0].T.reshape(24, P, D_MODEL)
    a["c"] = x["c_2"][0]
    a["rel"] = x["rel_bias_2"]
    c = np.zeros((P, NCOLS), np.float32)

    def put(name, v):
        c[:, COLS[name]:COLS[name] + v.shape[1]] = v

    for name, key in (("ffn1", "ffn1_norm"), ("mix", "mix_norm"), ("ffn2", "ffn2_norm"),
                      ("fin", "final_norm"), ("ng2", "norm_gain_2"), ("qn", "q_norm"),
                      ("kvn", "kv_norm"), ("bada", "b_ada_2")):
        put(name, x[key].reshape(-1, P).T)
    for name, key in (("gdn", "gdn_norm"), ("qa", "q_gain_a_2"), ("qb", "q_gain_b_2"), ("ka", "k_gain_a_2"),
                      ("ks", "k_gain_sel_2"), ("kw", "k_gain_win_2"), ("kc", "k_gain_cmp_2")):
        put(name, np.tile(x[key][0], 2)[:, None])
    put("conv", x["conv_w"][0].reshape(4, 12, P).transpose(2, 1, 0).reshape(P, 48))
    c[32:40, COLS["dtb"]], c[32:40, COLS["alog"]] = x["dt_bias"][0], x["a_log"][0]
    put("sink", np.broadcast_to(x["sinks_2"][0], (P, 8)))
    put("bg", np.broadcast_to(x["b_nsa_gate_2"][0], (P, 24)))
    put("posk", x["cmp_pos_k_2"][0].reshape(16, P).T)
    put("posv", x["cmp_pos_v_2"][0].reshape(16, P).T)
    a["cols"] = c
    return {k: np.ascontiguousarray(v) for k, v in a.items()}


def program(nc, shapes):
    io = {n: nc.dram_tensor("in_" + n, s, mybir.dt.float32, kind="ExternalInput").ap()
          for n, s in shapes.items()}
    io["rev"] = nc.dram_tensor("rev", [16, P, 384], mybir.dt.float32).ap()
    io["rev0"] = nc.dram_tensor("rev0", [16], mybir.dt.float32).ap()
    io["out"] = nc.dram_tensor("out", [KD, P, SEQ], mybir.dt.float32, kind="ExternalOutput").ap()
    build(nc, io)


def kernel(**inputs):
    import concourse.bacc as bacc
    from concourse.bass_utils import run_bass_kernel_spmd

    arrays = lay_out({k: np.asarray(v) for k, v in inputs.items()})
    nc = bacc.Bacc("TRN2", target_bir_lowering=False, num_devices=1)
    program(nc, {k: list(v.shape) for k, v in arrays.items()})
    r = run_bass_kernel_spmd(nc, [{"in_" + k: v for k, v in arrays.items()}], core_ids=[0])
    out = r.results[0]["out"]
    return np.ascontiguousarray(out.reshape(D_MODEL, SEQ).T)[None]
```

```python
from contextlib import ExitStack

import numpy as np

import concourse.bass as bass
from concourse import mybir

P = 128
D_MODEL, SEQ, N_META, D_FF = 1024, 512, 16, 2816
EPS = 1e-6
KD = D_MODEL // P
T1 = N_META + SEQ
HT = T1 // 2
NH = 8
FJ = D_FF // P
FH = FJ // 2
QT = SEQ // P
CH = 64
NCH = (T1 + 48) // CH
PAD = NCH * CH - T1
NU = 4 * NCH
UB = 6
NB = NU // UB
SIDE = 3
LEVELS = 6
NCMP = 31
NEG = -1.0e30
SLOT = 2048

STREAM = [("f1u0", FH, 16), ("f1d0", KD, FH), ("f1u1", FH, 16), ("f1d1", KD, FH),
          ("w1", 8, 16), ("uq", 1, 16), ("ukv", 1, 8), ("z", 2, 16), ("mg", 16, 16), ("wo", 4, 16),
          ("f2u0", FH, 16), ("f2d0", KD, FH), ("f2u1", FH, 16), ("f2d1", KD, FH),
          ("wi", 10, 16), ("wt", 1, 8), ("wv", 2, 0), ("wo2", 4, 16)]
TOKEN_COLS = 408
WIDTH = {n: t * P for n, _, t in STREAM}
WIDTH["wv"] = 4 * TOKEN_COLS
START = {}
_n = 0
for _name, _c, _ in STREAM:
    START[_name] = _n
    _n += _c
COUNT = {n: c for n, c, _ in STREAM}
ORDER = [n for n, _, _ in STREAM]

COLS = {}
_n = 0
for _name, _c in [("ffn1", 8), ("mix", 8), ("ffn2", 8), ("fin", 8), ("ng2", 8), ("qn", 2), ("kvn", 1),
                  ("gdn", 1), ("conv", 48), ("qa", 1), ("qb", 1), ("ka", 1), ("ks", 1), ("kw", 1),
                  ("kc", 1), ("bada", 24), ("dtb", 1), ("alog", 1), ("sink", 8), ("bg", 24),
                  ("posk", 16), ("posv", 16)]:
    COLS[_name] = _n
    _n += _c
NCOLS = _n
TABS = {}
_n = 0
for _name, _c in [("ident", 128), ("ones", 128), ("bones", 128), ("cos", T1), ("sin", T1),
                  ("mA", 256), ("mB", 256), ("cneg", 4 * NCMP), ("c01", 4 * NCMP), ("i64", CH),
                  ("mincl", CH), ("mstrict", CH), ("lvl", LEVELS * CH), ("sel", 4 * 128),
                  ("oh", 383)]:
    TABS[_name] = _n
    _n += _c
NTAB = _n
GROUPS = 4 + 3 * QT


def build(nc, io):
    f32, f32r = mybir.dt.float32, mybir.dt.float32r
    ALU, ACT, AX = mybir.AluOpType, mybir.ActivationFunctionType, mybir.AxisListType
    ctx = ExitStack()

    def sem(name):
        return ctx.enter_context(nc.semaphore(name))

    top = [16512]

    def at(name, shape, dtype, off):
        return nc.alloc_sbuf_tensor_at(name, shape, dtype, offset=off)

    def size(shape):
        n = 4
        for s in shape[1:]:
            n *= s
        return (n + 31) // 32 * 32

    def place(name, shape, dtype=f32):
        off = top[0]
        top[0] += size(shape)
        assert top[0] <= 229344, (name, top[0])
        return at(name, shape, dtype, off)

    H = place("H", [P, KD, T1])
    RAW = place("RAW", [P, 2, SLOT])
    WHI = place("WHI", [P, 2, SLOT], f32r)
    WLO = place("WLO", [P, 2, SLOT], f32r)
    TAB = place("TAB", [P, NTAB])
    COL = place("COL", [P, NCOLS])
    MOD = place("MOD", [P, 24])
    CST = place("CST", [P, 4])
    RELB = place("RELB", [32, 16])
    GATE = place("GATE", [P, QT, 24])
    B31 = place("B31", [P, 16])
    NSINK = place("NSINK", [P, NH])
    SNK = place("SNK", [P, 2 * NH])
    KEEP = place("KEEP", [P, T1])
    arena = top[0]
    SIZES = {}

    def region(start, *items):
        off, out = start, []
        for name, shape, dtype in items:
            out.append(at(name, shape, dtype, off))
            off += size(shape)
            assert off <= 229344, (name, off)
        return out + [off]

    U3 = [P, NU, CH]
    UH, UL, a_u = region(arena, ("UH", [P, KD, T1], f32r), ("UL", [P, KD, T1], f32r))
    RSTD, SQ, _ = region(a_u, ("RSTD", [P, T1], f32), ("SQ", [P, KD, T1], f32))
    _, GH, GL, TANH, SILU, GF, ADA, SILUC, JUNK, SILUT, _ = region(
        a_u, ("RSTD_", [P, T1], f32), ("GH", [P, FH, T1], f32r), ("GL", [P, FH, T1], f32r),
        ("TANH", [P, 2, T1], f32), ("SILU", [P, 2, T1], f32), ("GF", [P, 2, T1], f32),
        ("ADA", [P, 2, D_MODEL], f32), ("SILUC", [P, D_MODEL], f32), ("JUNK", [P, D_MODEL], f32),
        ("SILUT", [P, D_MODEL], f32))
    PR, a_pr = region(a_u, ("PR", [P, 16, T1], f32))
    OTH, OTL, a_ot = region(a_pr, ("OTH", [P, 4, SEQ], f32r), ("OTL", [P, 4, SEQ], f32r))
    QH, KH, a_qk = region(arena, ("QH", [96, NH, SEQ], f32), ("KH", [96, NH, T1], f32))
    assert a_qk <= a_u
    VM, a_vm = region(a_ot, ("VM", [P, 5, SEQ], f32))
    CF, CHI, CLO, RQ, RK, ROT, _ = region(
        a_vm, ("CF", [P, 3, T1], f32), ("CHI", [P, 3, T1], f32r), ("CLO", [P, 3, T1], f32r),
        ("RQ", [P, T1], f32), ("RK", [P, T1], f32), ("ROT", [P, 4, SEQ], f32))
    KROT, _ = region(a_vm, ("KROT", [P, 2, T1], f32))
    PB1, PTS1, PTM, OSB1, NM1, RS1, RI1, OTF1, _ = region(
        a_vm, ("PB1", [P, 2, 640], f32), ("PTS1", [P, 2, SEQ], f32), ("PTM", [N_META, 2, P], f32),
        ("OSB1", [P, 2, SEQ], f32), ("NM1", [P, 4 * NH], f32), ("RS1", [P, 4 * NH], f32),
        ("RI1", [P, 4 * NH], f32), ("OTF1", [P, SEQ], f32))
    CV, a_cv = region(arena, ("CV", [P, 12, NCH * CH], f32))
    assert a_cv <= a_u
    IT, EU, TTT, VB, SV, SE, a_sv = region(
        a_cv, ("IT", U3, f32), ("EU", U3, f32), ("TTT", U3, f32), ("VB", U3, f32),
        ("SV", [P, 2, 4, CH], f32), ("SE", [P, 4, CH], f32))
    assert a_sv <= a_pr
    KDEC, GB, KBG, a_kb = region(a_ot, ("KDEC", U3, f32), ("GB", U3, f32), ("KBG", U3, f32))
    CT, CTT, _ = region(a_ot, ("CT", [P, 2, T1], f32), ("CTT", [P, 2, T1], f32))
    GR, GSQ, _ = region(a_ot, ("GR", [P, 8, T1], f32), ("GSQ", [P, 8, T1], f32))
    BT8, GT, _ = region(a_kb, ("BT8", [NH, NCH * CH], f32), ("GT", [32 + NH, 5, NCH * CH], f32))
    VN, _ = region(a_kb, ("VN", [P, 2, 4, CH], f32))
    TB, UMB, AB, GP, _ = region(
        a_kb, ("TB", [P, SIDE, UB, CH], f32), ("UMB", [P, SIDE, UB, CH], f32),
        ("AB", [P, SIDE, UB, CH], f32), ("GP", [P, 8, NU], f32))
    SQ2, _ = region(a_ot + 3 * size([P, 4, SEQ]), ("SQ2", [P, KD, T1], f32))
    GOH, GOL, a_go = region(a_cv + 2 * size(U3), ("GOH", [P, 4, SEQ], f32r),
                            ("GOL", [P, 4, SEQ], f32r))
    assert a_go <= a_pr
    OSQ, OR, ZT, _ = region(a_ot, ("OSQ", [P, 4, SEQ], f32), ("OR", [P, 4, SEQ], f32),
                            ("ZT", [P, 4, SEQ], f32))
    MH, ML, TG, MF, _ = region(a_ot, ("MH", [P, KD, SEQ], f32r), ("ML", [P, KD, SEQ], f32r),
                               ("TG", [P, 2, SEQ], f32), ("MF", [P, 2, SEQ], f32))
    P2, VT, DT, OC, a_oc = region(
        a_u, ("P2", [P, 21, SEQ], f32), ("VT", [P, QT, TOKEN_COLS], f32),
        ("DT", [P, 16, 256], f32), ("OC", [P, QT, SEQ], f32))
    W1K, _ = region(arena, ("W1K", [P, 16, 256], f32))
    W1V, _ = region(a_oc - size([P, QT, SEQ]) - size([P, 16, 256]), ("W1V", [P, 16, 256], f32))
    XP, _ = region(a_oc - size([P, QT, SEQ]), ("XP", [P, 2, 16, 2 * NCMP], f32))
    HTN, HCT, _ = region(a_oc, ("HTN", [P, 2, 256], f32), ("HCT", [P, 2, 256], f32))
    CPT, _ = region(a_oc, ("CPT", [NCMP, 2, NH, P], f32))
    XC, HC, W2C, KCF, VCF, M8, a_psq = region(
        a_oc, ("XC", [P, 2, 2, SEQ], f32), ("HC", [P, 4, 64], f32),
        ("W2C", [P, 2, 2, CH], f32), ("KCF", [P, 32], f32), ("VCF", [NCMP, 2, CH], f32),
        ("M8", [P, 4, 4 * NH], f32))
    PSQ, PRS, _ = region(a_psq, ("PSQ", [P, 2, SEQ], f32), ("PRS", [P, 2, SEQ], f32))
    CPB, _ = region(a_psq, ("CPB", [P, 4 * NH, NCMP], f32))
    YH, YL, _ = region(arena, ("YH", [P, KD, SEQ], f32r), ("YL", [P, KD, SEQ], f32r))
    PB2, PTS2, OSB2, OBT, OTF2, NM2, RS2, RI2, _ = region(
        a_oc, ("PB2", [P, 2, SEQ], f32), ("PTS2", [P, 2, SEQ], f32), ("OSB2", [P, 2, SEQ], f32),
        ("OBT", [P, SEQ], f32), ("OTF2", [P, SEQ], f32), ("NM2", [P, 12 * NH], f32), ("RS2", [P, 12 * NH], f32),
        ("RI2", [P, 12 * NH], f32))
    PS = ctx.enter_context(nc.psum_tensor("PS", [P, 8, 512], f32))

    def tab(name, a=0, b=None):
        b = b if b is not None else P
        return TAB[:, TABS[name] + a:TABS[name] + b]

    def col(name, k=0, n=1):
        return COL[:, COLS[name] + k:COLS[name] + k + n]

    IDENT, ONES, BONES = tab("ident"), tab("ones"), tab("bones")
    EPS_AP = CST[:, 0:1]

    def flat(t):
        return t.rearrange("p a b -> p (a b)")

    def units(t, b):
        return t[:, b * UB:(b + 1) * UB, :]

    def over(ap, n):
        return ap.unsqueeze(1).to_broadcast([P, n, CH])

    def along(ap, n, w=CH):
        return ap.unsqueeze(2).to_broadcast([P, n, w])

    def chunk_of(t, n):
        return t[:, :, :].rearrange("p (t n) c -> p t n c", n=NCH)[:, :, n, :]

    def pair_rows(t):
        return t[:, :, :].rearrange("p (t n) c -> p t (n c)", n=NCH)

    def halves(ap):
        return ap.rearrange("p (a b) -> p a b", a=2)

    h_ld = [sem("h_loaded_0"), sem("h_loaded_1")]
    ones_ld, tab_ld, col_ld, rel_ld = (sem(x) for x in ("ones_loaded", "tables_loaded", "cols_loaded",
                                                        "rel_loaded"))
    raw_ld = [sem("raw_loaded_0"), sem("raw_loaded_1")]
    hi_rdy, lo_rdy = sem("weights_hi_ready"), sem("weights_lo_ready")
    mm_done, evac = sem("chunk_multiplied"), sem("chunk_evacuated")
    eps_rdy, dve_chain, act_chain = sem("eps_ready"), sem("vector_chain"), sem("scalar_chain")
    sq_rdy, ss_done, rstd_rdy = sem("squares_ready"), sem("square_sums_done"), sem("rstd_ready")
    tsq_rdy, acc_rdy = sem("tile_squared"), sem("squares_accumulated")
    uf_rdy, uh_rdy, ul_rdy = sem("normed_ready"), sem("normed_hi_ready"), sem("normed_lo_ready")
    tanh_rdy, silu_rdy = sem("tanh_ready"), sem("silu_ready")
    gh_rdy, gl_rdy = sem("hidden_hi_ready"), sem("hidden_lo_ready")
    ada_ld = [sem("ada_loaded_0"), sem("ada_loaded_1")]
    c_ld, ct_rdy, ada_used = sem("c_loaded"), sem("c_tanh_ready"), sem("ada_used")
    rev_ps, rev_rdy, rev_st, dt_ld = sem("rev_in_psum"), sem("rev_ready"), sem("rev_stored"), sem("bias_loaded")
    dt_rdy = sem("bias_ready")
    c_sq, c_ss, c_r, c_f, c_hi, c_lo = (sem("latent_" + x) for x in
                                        ("squared", "summed", "rstd", "normed", "hi", "lo"))
    uq_ps, q_act, kn_ps, k_act, kr_dve = (sem(x) for x in (
        "q_tile_in_psum", "q_nope_copied", "k_tile_in_psum", "k_nope_copied", "k_rope_ready"))
    s_ps, max_rdy, exp_rdy = sem("scores_in_psum"), sem("max_ready"), sem("exp_ready")
    pt_ps, pt_rdy, pv_done = sem("probs_t_in_psum"), sem("probs_t_ready"), sem("values_done")
    o_free, o_rdy, ot_ps = sem("o_psum_free"), sem("o_ready"), sem("o_t_in_psum")
    ot_f, ot_hi, ot_lo, sink_e = sem("o_t_ready"), sem("o_t_hi"), sem("o_t_lo"), sem("sink_exp_ready")
    cv_m, cv_c, cv_t, cv_s = sem("conv_taps_added"), sem("conv_done"), sem("conv_tanh"), sem("conv_silu")
    l_sq, l_ss, l_r, l_n = sem("l2_squared"), sem("l2_summed"), sem("l2_rstd"), sem("l2_normed")
    gt_a, gt_d = sem("gate_scalar_steps"), sem("gate_vector_steps")
    bb_ps, bb_ev, gb_ps, gb_ev = (sem(x) for x in ("beta_bcast_psum", "beta_bcast_ready",
                                                   "decay_bcast_psum", "decay_bcast_ready"))
    hv_ps = sem("compress_v_done")
    gp_ps, gp_ev = sem("per_token_in_psum"), sem("per_token_ready")
    dc_d, dc_a, un_rdy = sem("decay_vector_steps"), sem("decay_scalar_steps"), sem("unit_operands_ready")
    pr_ps, pr_rdy = sem("products_in_psum"), sem("products_ready")
    um_rdy, a_ps, ab_rdy, d_ps, t_rdy = (sem(x) for x in (
        "masked_ready", "a_in_psum", "a_ready", "update_in_psum", "inverse_updated"))
    uw_ps, u_rdy, w_rdy = sem("uw_in_psum"), sem("u_ready"), sem("w_ready")
    st_rdy, ws_ps, vn_rdy, sa_ps, o_ps, o_ev = (sem(x) for x in (
        "state_ready", "ws_in_psum", "v_new_ready", "state_add_in_psum", "delta_o_in_psum",
        "delta_o_ready"))
    osq_rdy, oss_ps, or_rdy, zt_rdy, gof_rdy, goh_rdy, gol_rdy = (sem(x) for x in (
        "delta_squared", "delta_summed", "delta_rstd", "z_tanh", "delta_gated", "delta_hi", "delta_lo"))
    tg_rdy, mf_rdy, mh_rdy, ml_rdy = (sem(x) for x in (
        "merge_gates_ready", "merged_ready", "merged_hi", "merged_lo"))
    x2_rdy = sem("second_input_ready")
    n_sq, n_ss, n_r, n_n = sem("qk_squared"), sem("qk_summed"), sem("qk_rstd"), sem("qk_normed")
    z_t, z_s, bg_d, bg_a = sem("z2_tanh"), sem("z2_silu"), sem("branch_gate_sum"), sem("branch_gate_tanh")
    w1_ld, w1v_ld, xc_rdy, hc_ps, hc_x, hc_t, hc_tp, hc_rdy = (sem(x) for x in (
        "compress_k_loaded", "compress_v_loaded", "compress_input", "compress_psum",
        "compress_tokens", "compress_tanh", "compress_transposed", "compress_hidden"))
    kc_ps, kc_f, kc_sq, kc_ss, kc_r, kc_rdy = (sem(x) for x in (
        "cmp_kv_psum", "cmp_kv_copied", "cmp_k_squared", "cmp_k_summed", "cmp_k_rstd", "cmp_k_ready"))
    cs_ps, cs_z, cs_e, cs_p, ct_ps, ct_ev, co_ps, co_rdy = (sem(x) for x in (
        "cmp_scores", "cmp_shifted", "cmp_exp", "cmp_probs", "cmp_probs_t", "cmp_probs_t_ready",
        "cmp_o_psum", "cmp_o_ready"))
    out_st = sem("out_stored")
    sink_s, se_rdy = sem("sink_shifted"), sem("state_decayed")

    class Chain:

        def __init__(self, eng, s):
            self.eng, self.s, self.n, self.add = eng, s, 0, 0

        def __call__(self, ins):
            self.n += 1
            ins.then_inc(self.s, 1)
            self.eng.wait_ge(self.s, self.n + self.add)

    def chunk_width(name, parity):
        if name == "mg":
            return SLOT if parity == 0 else SLOT // 2
        return WIDTH[name]

    def stream(eng, name, body, straight=False):
        n0, count = START[name], COUNT[name]
        at_ = ORDER.index(name)
        after = chunk_width(ORDER[at_ + 1], 0) if at_ + 1 < len(ORDER) else 0
        head = 2 if n0 == 0 else 0

        def one(j):
            n = n0 + j
            body(n, j, n // 2, n % 2, chunk_width(name, (j + 1) % 2) if j + 1 < count else after)

        if straight:
            head = count
        for j in range(head):
            one(j)
        trips = (count - head - 1) // 2
        if trips > 1:
            with eng.Fori(0, trips) as i:
                for s in range(2):
                    n = n0 + head + s
                    body(2 * i + n, 2 * i + head + s, i + n // 2, n % 2,
                         chunk_width(name, (head + s + 1) % 2))
            done = head + 2 * trips
        else:
            done = head
        for j in range(done, count):
            one(j)

    SUMMED = {1: (0, 1), 3: (1, 2), 4: (2, 1)}
    TURN = {0: 1, 1: 2, 3: 3, 4: 4, 5: 5}
    ROUND = {0: 0, 1: 1, 2: 2, 3: 3, 5: 4}
    NORMS = [(0, T1), (0, T1), (N_META, SEQ), (N_META, SEQ), (N_META, SEQ), (N_META, SEQ)]

    def factors(v):
        return KEEP if v in (1, 2) else RSTD

    def spans(c0, w):
        return [(c0, w)] if w <= 512 else [(c0, w // 2), (c0 + w // 2, w // 2)]

    def attention_units(part):
        out = []
        if part == 0:
            for qi in range(QT):
                for h in range(NH):
                    w = P * (qi + 1)
                    out.append(dict(
                        u=len(out), g=qi, h=h, last=h == NH - 1, kind="mla", qi=qi, w=w, total=w + N_META,
                        q=QH[0:96, h, P * qi:P * (qi + 1)],
                        keys=[(0, w, KH[0:96, h, N_META:N_META + w]), (w, N_META, KH[0:96, h, 0:N_META])],
                        bias=(w - P, P, tab("mB", P, 2 * P)),
                        v=[VM[:, 1 + j, CH * h:CH * (h + 1)] for j in range(qi + 1)],
                        vm=VM[0:N_META, 0, CH * h:CH * (h + 1)], tg=qi, sink=False))
            return out
        for qi in range(QT):
            for b, kind in enumerate(("A", "sel", "win")):
                for h in range(NH):
                    j, g = h % 4, h // 4
                    rows = slice(CH * g, CH * (g + 1))
                    first = max(qi - 1, 0) if kind == "A" else 0
                    w = P * (qi + 1 - first)
                    near = min(w, 2 * P)
                    out.append(dict(
                        u=4 * NH + len(out), g=QT + 3 * qi + b, h=h, last=h == NH - 1, kind=kind, qi=qi,
                        w=w, total=w, q=P2[rows, (j if kind == "A" else 4 + j), P * qi:P * (qi + 1)],
                        keys=[(0, w, P2[rows, 8 + b, P * first:P * (qi + 1)])],
                        bias=(w - near, near, DT[:, (h if kind == "A" else 8 + h), 2 * P - near:2 * P]),
                        v=[VT[:, t, P * b + CH * g:P * b + CH * (g + 1)] for t in range(first, qi + 1)],
                        vm=None, tg=(QT + 2 * qi if kind == "A" else QT + 2 * qi + 1 if kind == "win" else None),
                        sink=kind == "A"))
        return out

    PARTS = [attention_units(0), attention_units(1)]

    def bufs(part):
        return (PB1, PTS1, OSB1, OTF1, NM1, RS1, RI1) if part == 0 else (PB2, PTS2, OSB2, OTF2, NM2, RS2, RI2)

    LAG = (0, 1)

    def scores(part, u, a, b):
        if part == 0:
            return PS[:, 2 * (u % 2):2 * (u % 2) + 2, :].rearrange("p a b -> p (a b)")[:, a:b]
        return PS[:, u % 3, a:b]

    def outputs(part, g):
        return PS[:, 3 if part == 1 and g % 2 else 6, :]

    block = ctx.enter_context(nc.Block())

    @block.sync
    def _(sp):
        for i in range(2):
            ks = slice(i * KD // 2, (i + 1) * KD // 2)
            sp.dma_start(H[:, ks, :], io["h"][ks].rearrange("k p t -> p k t")).then_inc(h_ld[i], 16)
            if i == 0:
                sp.dma_start(TAB[:, 0:TABS["cos"]], io["tabs"][:, 0:TABS["cos"]]).then_inc(ones_ld, 16)
        sp.dma_start(COL[:, :], io["cols"]).then_inc(col_ld, 16)
        sp.dma_start(RELB[:, :], io["rel"]).then_inc(rel_ld, 16)

        def load(name):
            def body(n, j, turn, slot, nxt):
                if not isinstance(n, int) or n >= 2:
                    sp.wait_ge(lo_rdy, n - 1)
                w = chunk_width(name, (n - START[name]) % 2 if isinstance(n, int) else
                                (slot - START[name]) % 2)
                src = io[name][j] if name != "mg" else io["mg"][j, :, 0:w]
                sp.dma_start(RAW[:, slot, 0:w], src).then_inc(raw_ld[slot], 16)
                if isinstance(n, int) and n == 0:
                    sp.dma_start(TAB[:, TABS["cos"]:], io["tabs"][:, TABS["cos"]:]).then_inc(tab_ld, 16)
            return body

        for name in ORDER[:-1]:
            stream(sp, name, load(name))
        n0 = START["wo2"]
        for j in range(2):
            load("wo2")(n0 + j, j, 0, (n0 + j) % 2, 0)
        sp.wait_ge(mm_done, n0)
        sp.dma_start(W1K[:, :, :], io["w1k"]).then_inc(w1_ld, 16)
        for j in range(2, 4):
            load("wo2")(n0 + j, j, 0, (n0 + j) % 2, 0)
        for j in range(4):
            sp.wait_ge(evac, n0 + j + 1)
            sp.dma_start(io["out"][2 * j:2 * j + 2].rearrange("k p t -> p k t"),
                         H[:, 2 * j:2 * j + 2, N_META:T1]).then_inc(out_st, 16)
        sp.wait_ge(out_st, 64)

    @block.gpsimd
    def _(pool):
        pool.wait_ge(h_ld[1], 16)
        pool.dma_start(SILUC[:, :], io["c"].partition_broadcast(P)).then_inc(c_ld, 16)
        for s in range(2):
            pool.dma_start(ADA[:, s, :], io["ada"][s]).then_inc(ada_ld[s], 16)
        pool.wait_ge(rev_rdy, 1)
        pool.dma_start(io["rev"][:, :, 0:383], JUNK[0:16, 0:383].unsqueeze(1).to_broadcast([16, P, 383]))\
            .then_inc(rev_st, 16)
        pool.dma_start(io["rev0"].unsqueeze(1), JUNK[0:16, 0:1]).then_inc(rev_st, 16)
        with pool.Fori(1, 12) as i:
            for s in range(2):
                pool.wait_ge(ada_used, 2 * i + s - 1)
                pool.dma_start(ADA[:, s, :], io["ada"][2 * i + s]).then_inc(ada_ld[s], 16)
        pool.wait_ge(acc_rdy, sum(1 + KD // wide for _, wide in SUMMED.values()))
        pool.dma_start(W1V[:, :, :], io["w1v"]).then_inc(w1v_ld, 16)
        pool.dma_start(W2C[:, :, :, :], io["w2"]).then_inc(w1v_ld, 16)
        pool.wait_ge(rev_st, 32)
        pool.wait_ge(hv_ps, 1)
        pool.dma_start(DT[:, :, :], bass.AP(io["rev"].tensor, 127, [[383, P], [P * 384, 16], [1, 256]]))\
            .then_inc(dt_ld, 16)
        pool.dma_start(B31[:, :], io["rev0"].partition_broadcast(P)).then_inc(dt_ld, 16)
        pool.wait_ge(dt_ld, 32)

    @block.tensor
    def _(pe):
        mm = nc.tensor.matmul

        def mm3(out, slot, c, hi, lo, first, last, w=P):
            mm(out, WHI[:, slot, c:c + w], hi, start=first, stop=False)
            mm(out, WLO[:, slot, c:c + w], hi, start=False, stop=False)
            return mm(out, WHI[:, slot, c:c + w], lo, start=False, stop=last)

        def norm(v):
            c0, w = NORMS[v]
            if v in SUMMED:
                turn, wide = SUMMED[v]
                pe.wait_ge(acc_rdy, sum(1 + KD // SUMMED[x][1] for x in (1, 3, 4)[:turn + 1]))
                for b, (a, n) in enumerate(spans(c0, w)):
                    for i in range(wide):
                        acc = TG[:, i, :] if wide == 2 else RSTD[:, a:a + n]
                        last = mm(PS[:, 6 + b, 0:n], ONES, acc, start=i == 0, stop=i == wide - 1)
            else:
                for k in range(KD):
                    pe.wait_ge(sq_rdy, KD * (v // 5) + k + 1)
                    for b, (a, n) in enumerate(spans(c0, w)):
                        last = mm(PS[:, 6 + b, 0:n], ONES, SQ[:, k, a:a + n], start=k == 0, stop=k == KD - 1)
            last.then_inc(ss_done, 1)

        def ffn(f, c0, w):
            sp_ = spans(c0, w)
            for half in range(2):
                def up(n, j, turn, slot, nxt):
                    pe.wait_ge(lo_rdy, n + 1)
                    if not isinstance(n, int) or n >= 2:
                        pe.wait_ge(evac, n - 1)
                    for k in range(KD):
                        pe.wait_ge(ul_rdy, KD * ROUND[3 * f] + k + 1)
                        for which in range(2):
                            for b, (a, m) in enumerate(sp_):
                                last = mm3(PS[:, 4 * slot + 2 * which + b, 0:m], slot,
                                           (which * KD + k) * P, UH[:, k, a:a + m], UL[:, k, a:a + m],
                                           k == 0, k == KD - 1)
                    last.then_inc(mm_done, 1)

                def down(n, j, turn, slot, nxt):
                    pe.wait_ge(lo_rdy, n + 1)
                    pe.wait_ge(evac, n - 1)
                    for b, (a, m) in enumerate(sp_):
                        for k in range(FH):
                            pe.wait_ge(gl_rdy, (2 * f + half) * FH + k + 1)
                            last = mm3(PS[:, 4 * slot + b, 0:m], slot, k * P, GH[:, k, a:a + m],
                                       GL[:, k, a:a + m], k == 0, k == FH - 1)
                    last.then_inc(mm_done, 1)

                stream(pe, f"f{f + 1}u{half}", up)
                stream(pe, f"f{f + 1}d{half}", down)

        pe.wait_ge(ones_ld, 16)
        norm(0)
        pe.wait_ge(rel_ld, 16)
        pe.wait_ge(tab_ld, 16)
        mm(PS[0:16, 0, 0:383], RELB[:, :], TAB[0:32, TABS["oh"]:TABS["oh"] + 383], start=True,
           stop=True).then_inc(rev_ps, 1)
        pe.wait_ge(rev_rdy, 1)
        ffn(0, 0, T1)
        norm(1)

        def project(v):
            c0, w = NORMS[v]

            def body(n, j, turn, slot, nxt):
                pe.wait_ge(lo_rdy, n + 1)
                pe.wait_ge(evac, n - 1)
                for k in range(KD):
                    pe.wait_ge(ul_rdy, KD * ROUND[v] + k + 1)
                    for t in range(2):
                        for b, (a, m) in enumerate(spans(c0, w)):
                            last = mm3(PS[:, 4 * slot + (2 if w > 512 else 1) * t + b, 0:m], slot,
                                       (t * KD + k) * P, UH[:, k, a:a + m], UL[:, k, a:a + m],
                                       k == 0, k == KD - 1)
                last.then_inc(mm_done, 1)
            return body

        into = project(1)

        def with_latents(n, j, turn, slot, nxt):
            if j in (3, 5):
                pe.wait_ge(c_r, j // 2)
            into(n, j, turn, slot, nxt)
            if j in (1, 3):
                pe.wait_ge(c_sq, j // 2 + 2)
                pe.wait_ge(evac, n + 1)
                for b in range(3):
                    a = b * T1 // 3
                    for k in ((0, 1) if j == 1 else (2,)):
                        last = mm(PS[:, 4 + b, 320:320 + T1 // 3], ONES, CF[:, k, a:a + T1 // 3],
                                  start=k != 1, stop=k != 0)
                last.then_inc(c_ss, 1)

        stream(pe, "w1", with_latents, straight=True)
        pe.wait_ge(evac, START["uq"])
        pe.wait_ge(lo_rdy, START["uq"] + 1)
        pe.wait_ge(c_lo, 1)
        for t in range(8):
            for k in range(2):
                last = mm3(PS[:, t, 0:SEQ], 0, (2 * t + k) * P, CHI[:, k, N_META:T1],
                           CLO[:, k, N_META:T1], k == 0, k == 1)
            last.then_inc(uq_ps, 1)
            if t == 7:
                mm_last = last
        pe.wait_ge(uq_ps, 8)
        pe.sem_inc(mm_done, 1)
        pe.wait_ge(lo_rdy, START["ukv"] + 1)
        pe.wait_ge(evac, START["ukv"])
        for t in range(4):
            for b, (a, m) in enumerate(spans(0, T1)):
                last = mm3(PS[:, 2 * t + b, 0:m], 1, t * P, CHI[:, 2, a:a + m], CLO[:, 2, a:a + m],
                           True, True)
            last.then_inc(kn_ps, 1)
        pe.wait_ge(k_act, NH)
        for t in range(5):
            a = 0 if t == 0 else N_META + P * (t - 1)
            mm(PS[:, t, 0:SEQ], CHI[:, 2, a:a + P], WHI[:, 1, SEQ:2 * SEQ], start=True, stop=False)
            mm(PS[:, t, 0:SEQ], CLO[:, 2, a:a + P], WHI[:, 1, SEQ:2 * SEQ], start=False, stop=False)
            last = mm(PS[:, t, 0:SEQ], CHI[:, 2, a:a + P], WLO[:, 1, SEQ:2 * SEQ], start=False, stop=True)
        last.then_inc(mm_done, 1)

        def attention(part):
            U = PARTS[part]
            PB, PTS, OSB = bufs(part)[:3]
            base = U[0]["u"]
            ends = {x["u"] - base: x for x in U if x["last"]}
            lag = LAG[part]
            for i in range(len(U) + 5 + lag):
                if i < len(U):
                    x = U[i]
                    if part == 0 and i >= 2:
                        pe.wait_ge(pt_rdy, x["u"] - 1)
                    elif part == 1 and i >= 3:
                        pe.wait_ge(exp_rdy, x["u"] - 2)
                    for c, n, k in x["keys"]:
                        for c1 in range(c, c + n, 512):
                            n1 = min(n, 512)
                            last = mm(scores(part, x["u"], c1, c1 + n1), x["q"], k, start=True, stop=True)
                    last.then_inc(s_ps, 1)
                if 0 <= i - 1 - lag < len(U):
                    x = U[i - 1 - lag]
                    s = x["u"] % 2
                    pe.wait_ge(exp_rdy, x["u"] + 1)
                    for t in range(x["w"] // P):
                        last = nc.tensor.transpose(PS[:, 4 + s, t * P:(t + 1) * P],
                                                   PB[:, s, t * P:(t + 1) * P], IDENT)
                    if x["vm"] is not None:
                        last = nc.tensor.transpose(PS[0:N_META, 2 * s + 1, P:2 * P],
                                                   PB[:, s, x["w"]:x["w"] + N_META], IDENT)
                    last.then_inc(pt_ps, 1)
                if 0 <= i - 2 - lag < len(U):
                    x = U[i - 2 - lag]
                    s = x["u"] % 2
                    o = outputs(part, x["g"])[:, CH * x["h"]:CH * (x["h"] + 1)]
                    pe.wait_ge(pt_rdy, x["u"] + 1)
                    if x["h"] == 0 and x["g"] > lag:
                        pe.wait_ge(o_free, x["g"] - lag)
                    n = len(x["v"])
                    for t, v in enumerate(x["v"]):
                        last = mm(o, PTS[:, s, t * P:(t + 1) * P], v, start=t == 0,
                                  stop=t == n - 1 and x["vm"] is None)
                    if x["vm"] is not None:
                        last = mm(o, PTM[:, s, :], x["vm"], start=False, stop=True)
                    last.then_inc(pv_done, 1)
                x = ends.get(i - 4 - lag)
                if x is not None and x["tg"] is not None:
                    pe.wait_ge(o_rdy, x["tg"] + 1)
                    if x["tg"] > 0:
                        pe.wait_ge(ot_f, x["tg"])
                    for f in range(4):
                        last = nc.tensor.transpose(PS[:, 7, f * P:(f + 1) * P],
                                                   OSB[:, x["tg"] % 2, f * P:(f + 1) * P], IDENT)
                    last.then_inc(ot_ps, 1)

        pe.wait_ge(evac, START["z"])
        pe.wait_ge(kr_dve, 1)
        attention(0)
        pe.wait_ge(ot_f, QT)
        for t in range(8):
            pe.wait_ge(l_sq, t + 1)
            if t == 4:
                pe.wait_ge(l_r, 1)
            for b, (a, m) in enumerate(spans(0, T1)):
                last = mm(PS[:, 2 * (t % 4) + b, 0:m], BONES, GSQ[:, t, a:a + m], start=True, stop=True)
            last.then_inc(l_ss, 1)
        W2 = NCH * CH // 2
        pe.wait_ge(l_r, 2)
        pe.wait_ge(gt_d, 9)
        for n in range(NCH):
            for p in range(2):
                for i, row, r0 in ((0, BT8[0:NH, n * CH:(n + 1) * CH], 0),
                                   (1, GT[32:32 + NH, 2, n * CH:(n + 1) * CH], 32)):
                    last = mm(PS[CH * p:CH * (p + 1), i, 4 * n:4 * n + 4], row,
                              TAB[r0:r0 + NH, TABS["ident"] + r0 + p:TABS["ident"] + r0 + NH:2],
                              start=True, stop=True)
        last.then_inc(gp_ps, 1)
        pe.wait_ge(gp_ev, 1)
        for t in range(4):
            for b in range(2):
                last = mm(PS[:, 2 * t + b, 0:W2], TAB[0:NH, TABS["sel"] + t * P:TABS["sel"] + (t + 1) * P],
                          BT8[:, b * W2:(b + 1) * W2], start=True, stop=True)
        last.then_inc(bb_ps, 1)
        pe.wait_ge(bb_ev, 1)
        for t in range(4):
            for b in range(2):
                last = mm(PS[:, 2 * t + b, 0:W2],
                          TAB[32:32 + NH, TABS["sel"] + t * P:TABS["sel"] + (t + 1) * P],
                          GT[32:32 + NH, 2, b * W2:(b + 1) * W2], start=True, stop=True)
        last.then_inc(gb_ps, 1)
        pe.wait_ge(un_rdy, 1)

        def cvu(group, u, p):
            t, n = divmod(u, NCH)
            return CV[CH * p:CH * (p + 1), 4 * group + t, n * CH:(n + 1) * CH]

        def un(t, u, p):
            return t[CH * p:CH * (p + 1), u, :]

        for b in range(NB):
            if b >= 2:
                pe.wait_ge(pr_rdy, b - 1)
            for r in range(UB):
                u = b * UB + r
                for p in range(2):
                    rows = slice(CH * p, CH * (p + 1))

                    def bank(i):
                        return PS[rows, 4 * (b % 2) + i, r * CH:(r + 1) * CH]

                    i64 = TAB[rows, TABS["i64"]:TABS["i64"] + CH]
                    mm(bank(0), cvu(1, u, p), un(TTT, u, p), start=True, stop=True)
                    mm(bank(1), cvu(1, u, p), cvu(0, u, p), start=True, stop=True)
                    mm(bank(2), cvu(1, u, p), i64, start=True, stop=True)
                    last = mm(bank(3), cvu(2, u, p), i64, start=True, stop=True)
            last.then_inc(pr_ps, 1)
        pe.wait_ge(pr_rdy, NB)
        for g in range(NB // SIDE):
            for lv in range(LEVELS):
                for x in range(SIDE):
                    i = SIDE * (LEVELS * g + lv) + x
                    pe.wait_ge(um_rdy, i + 1)
                    if lv == 0:
                        if g:
                            pe.wait_ge(u_rdy, SIDE * (g - 1) + x + 1)
                    else:
                        pe.wait_ge(t_rdy, i - SIDE + 1)
                    for r in range(UB):
                        for p in range(2):
                            rows = slice(CH * p, CH * (p + 1))
                            last = mm(PS[rows, 2 * x, r * CH:(r + 1) * CH], UMB[rows, x, r, :],
                                      TAB[rows, TABS["i64"]:TABS["i64"] + CH] if lv == 0 else
                                      TB[rows, x, r, :], start=True, stop=True)
                    last.then_inc(a_ps, 1)
                for x in range(SIDE if lv else 0):
                    b = SIDE * g + x
                    pe.wait_ge(ab_rdy, SIDE * ((LEVELS - 1) * g + lv - 1) + x + 1)
                    if lv == 1 and g:
                        pe.wait_ge(w_rdy, b - SIDE + 1)
                    for r in range(UB):
                        u = b * UB + r
                        for p in range(2):
                            rows = slice(CH * p, CH * (p + 1))
                            if lv < LEVELS - 1:
                                mm(PS[rows, 2 * x, r * CH:(r + 1) * CH], un(TTT, u, p),
                                   AB[rows, x, r, :], start=True, stop=True)
                            last = mm(PS[rows, 2 * x + 1, r * CH:(r + 1) * CH], AB[rows, x, r, :],
                                      un(TTT, u, p), start=True, stop=True)
                    last.then_inc(d_ps, 1)
            for x in range(SIDE):
                b = SIDE * g + x
                pe.wait_ge(t_rdy, SIDE * (LEVELS * (g + 1) - 1) + x + 1)
                for r in range(UB):
                    u = b * UB + r
                    for p in range(2):
                        rows = slice(CH * p, CH * (p + 1))
                        mm(PS[rows, 2 * x, r * CH:(r + 1) * CH], un(TTT, u, p), un(VB, u, p),
                           start=True, stop=True)
                        last = mm(PS[rows, 2 * x + 1, r * CH:(r + 1) * CH], un(KBG, u, p),
                                  un(TTT, u, p), start=True, stop=True)
                last.then_inc(uw_ps, 1)
        pe.wait_ge(u_rdy, NB)
        pe.wait_ge(w_rdy, NB)
        for n in range(NCH):
            pe.wait_ge(st_rdy, n + 1)

            def tiles(t, p, a):
                return slice(CH * p, CH * (p + 1)), t * NCH + n, slice(CH * a, CH * (a + 1))

            for t in range(4):
                for p in range(2):
                    rows, u, _ = tiles(t, p, 0)
                    last = mm(PS[rows, 0, t * CH:(t + 1) * CH], KBG[rows, u, :],
                              SV[rows, n % 2, t, :], start=True, stop=True)
            last.then_inc(ws_ps, 1)
            pe.wait_ge(vn_rdy, n + 1)
            if n < NCH - 1:
                for t in range(4):
                    for p in range(2):
                        rows, u, _ = tiles(t, p, 0)
                        last = mm(PS[rows, 1, t * CH:(t + 1) * CH], KDEC[rows, u, :],
                                  VN[rows, n % 2, t, :], start=True, stop=True)
                last.then_inc(sa_ps, 1)
            if n >= 2:
                pe.wait_ge(o_ev, n - 1)
            for t in range(4):
                for p in range(2):
                    rows, u, _ = tiles(t, p, 0)
                    o = PS[rows, 2 + n % 2, t * CH:(t + 1) * CH]
                    mm(o, SV[rows, n % 2, t, :], GB[rows, u, :], start=True, stop=False)
                    last = mm(o, VN[rows, n % 2, t, :], IT[rows, u, :], start=False, stop=True)
            last.then_inc(o_ps, 1)
        pe.wait_ge(osq_rdy, 1)
        for t in range(4):
            last = mm(PS[:, (2, 3, 6, 7)[t], 0:SEQ], BONES, OSQ[:, t, :], start=True, stop=True)
        last.then_inc(oss_ps, 1)
        stream(pe, "z", project(2))
        pe.wait_ge(or_rdy, 1)
        pe.wait_ge(evac, START["mg"])

        def merge(n, j, turn, slot, nxt):
            pe.wait_ge(lo_rdy, n + 1)
            if slot == 0:
                pe.wait_ge(tg_rdy, turn - (START["mg"] // 2 - 1))
                for t in range(2):
                    for k in range(KD):
                        last = mm3(PS[:, t, 0:SEQ], slot, (t * KD + k) * P, UH[:, k, N_META:T1],
                                   UL[:, k, N_META:T1], k == 0, k == KD - 1)
            else:
                pe.wait_ge(evac, n - 1)
                pe.wait_ge(gol_rdy, 1)
                for t, (hi, lo) in enumerate(((OTH, OTL), (GOH, GOL))):
                    for k in range(4):
                        last = mm3(PS[:, 4 + t, 0:SEQ], slot, (t * 4 + k) * P, hi[:, k, :], lo[:, k, :],
                                   k == 0, k == 3)
            last.then_inc(mm_done, 1)

        stream(pe, "mg", merge)

        def outward(hi, lo):
            def body(n, j, turn, slot, nxt):
                pe.wait_ge(lo_rdy, n + 1)
                pe.wait_ge(evac, n - 1)
                for t in range(2):
                    for k in range(KD):
                        last = mm3(PS[:, 4 * slot + t, 0:SEQ], slot, (t * KD + k) * P, hi[:, k, :],
                                   lo[:, k, :], k == 0, k == KD - 1)
                last.then_inc(mm_done, 1)
            return body

        pe.wait_ge(ml_rdy, KD + 1)
        pe.wait_ge(evac, START["wo"])
        stream(pe, "wo", outward(MH, ML))
        norm(3)
        ffn(1, N_META, SEQ)
        norm(4)
        norm(5)
        into = project(5)

        def head_sums(c):
            pe.wait_ge(n_sq, c + 1)
            if c >= 2:
                pe.wait_ge(n_r, c - 1)
            for t in range(2 if c < 5 else 1):
                last = mm(PS[:, 2 + 4 * (c % 2) + t, 0:SEQ], BONES, PSQ[:, t, :], start=True, stop=True)
            last.then_inc(n_ss, 1)

        def into_heads(n, j, turn, slot, nxt):
            into(n, j, turn, slot, nxt)
            if 1 <= j <= 6:
                head_sums(j - 1)

        stream(pe, "wi", into_heads, straight=True)
        n = START["wt"]
        pe.wait_ge(lo_rdy, n + 1)
        pe.wait_ge(evac, n - 1)
        for k in range(KD):
            last = mm3(PS[:, 4 * (n % 2), 0:SEQ], n % 2, k * P, UH[:, k, N_META:T1], UL[:, k, N_META:T1],
                       k == 0, k == KD - 1)
        last.then_inc(mm_done, 1)
        n = START["wv"]
        pe.wait_ge(evac, n - 1)
        pe.wait_ge(n_r, 6)
        for c in range(2):
            s = (n + c) % 2
            pe.wait_ge(lo_rdy, n + c + 1)
            for qi in range(QT):
                for kk in range(4):
                    k = 4 * c + kk
                    a = N_META + P * qi
                    out = PS[:, 4 + qi, 0:TOKEN_COLS]
                    wc = slice(kk * TOKEN_COLS, (kk + 1) * TOKEN_COLS)
                    mm(out, UH[:, k, a:a + P], WHI[:, s, wc], start=k == 0, stop=False)
                    mm(out, UL[:, k, a:a + P], WHI[:, s, wc], start=False, stop=False)
                    last = mm(out, UH[:, k, a:a + P], WLO[:, s, wc], start=False, stop=k == KD - 1)
            last.then_inc(mm_done, 1)
        B62 = 2 * NCMP
        pe.wait_ge(xc_rdy, 5)
        pe.wait_ge(w1v_ld, 32)
        for kv, w1 in ((1, W1V), (0, W1K)):
            if kv == 0:
                pe.wait_ge(w1_ld, 16)
            for lp in range(16):
                last = mm(PS[0:B62, kv, 0:256], XP[:, kv, lp, :], w1[:, lp, :], start=lp == 0, stop=lp == 15)
            if kv:
                last.then_inc(hv_ps, 1)
        last.then_inc(hc_ps, 1)
        pe.wait_ge(evac, START["wo2"])
        pe.wait_ge(hc_x, 1)
        for i in range(4):
            last = nc.tensor.transpose(PS[:, 4, 64 * i:64 * i + B62],
                                       HCT[0:B62, i // 2, P * (i % 2):P * (i % 2 + 1)], IDENT[0:B62, 0:B62])
        last.then_inc(hc_tp, 1)
        pe.wait_ge(hc_rdy, 1)
        for g in range(2):
            for m in range(2):
                mm(PS[CH * g:CH * (g + 1), 0, 0:NCMP], W2C[:, 0, m, :],
                   HC[:, m, g * NCMP:(g + 1) * NCMP], start=m == 0, stop=m == 1)
            for m in range(2):
                last = mm(PS[0:NCMP, 1, CH * g:CH * (g + 1)], HC[:, 2 + m, g * NCMP:(g + 1) * NCMP],
                          W2C[:, 1, m, :], start=m == 0, stop=m == 1)
        last.then_inc(kc_ps, 1)
        pe.wait_ge(kc_sq, 1)
        mm(PS[:, 2, 0:NCMP], BONES, PSQ[:, 0, 0:NCMP], start=True, stop=True).then_inc(kc_ss, 1)
        pe.wait_ge(kc_rdy, 1)
        pe.wait_ge(n_n, 6)
        for qi in range(QT):
            for h in range(NH):
                rows = slice(CH * (h // 4), CH * (h // 4) + CH)
                c = NCMP * (4 * qi + h % 4)
                last = mm(PS[:, h // 4, c:c + NCMP], P2[rows, 4 + h % 4, P * qi:P * (qi + 1)],
                          KCF[rows, 0:NCMP], start=True, stop=True)
        last.then_inc(cs_ps, 1)
        pe.wait_ge(cs_p, 1)
        for i in range(QT + 1):
            if i < QT:
                if i >= 2:
                    pe.wait_ge(ct_ev, i - 1)
                for h in range(NH):
                    b = (4, 2)[i % 2] + h // 4
                    last = nc.tensor.transpose(PS[0:NCMP, b, P * (h % 4):P * (h % 4 + 1)],
                                               CPB[:, 16 * (h // 4) + 4 * i + h % 4, :], IDENT)
                last.then_inc(ct_ps, 1)
            if i:
                pe.wait_ge(ct_ev, i)
                if i >= 3:
                    pe.wait_ge(co_rdy, i - 2)
                for h in range(NH):
                    last = mm(PS[:, 6 + (i - 1) % 2, CH * h:CH * (h + 1)], CPT[:, (i - 1) % 2, h, :],
                              VCF[:, h // 4, :], start=True, stop=True)
                last.then_inc(co_ps, 1)
        pe.wait_ge(co_rdy, QT)
        pe.wait_ge(dt_rdy, 1)
        attention(1)
        pe.wait_ge(ot_lo, 3 * QT)
        stream(pe, "wo2", outward(YH, YL))

    @block.scalar
    def _(act):
        A = nc.scalar.activation
        chain = Chain(act, act_chain)

        def hi_part(n, slot, turn, w):
            if w:
                act.wait_ge(raw_ld[slot], 16 * turn + 16)
                if not isinstance(n, int) or n >= 2:
                    act.wait_ge(mm_done, n - 1)
                A(WHI[:, slot, 0:w], RAW[:, slot, 0:w], ACT.Copy).then_inc(hi_rdy, 1)

        def next_hi(n, turn, slot, nxt):
            hi_part(n + 1, 1 - slot, turn + slot, nxt)

        def rstd(out, sums, d, scale=1.0):
            chain(A(out, sums, ACT.Ln, bias=CST[0:out.shape[0], 0:1], scale=scale / d))
            return A(out, out, ACT.Exp, scale=-0.5)

        def norm(v, meanwhile=None):
            c0, w = NORMS[v]
            sq = SQ2 if v == 2 else SQ
            if v in (0, 5):
                for k in range(KD):
                    if v == 5:
                        act.wait_ge(x2_rdy, k + 1)
                    else:
                        act.wait_ge(h_ld[2 * k // KD], 16)
                    A(sq[:, k, c0:c0 + w], H[:, k, c0:c0 + w], ACT.Square).then_inc(sq_rdy, 1)
            if meanwhile is not None:
                meanwhile()
            if v != 2:
                chain(A(CST[:, 3:4], EPS_AP, ACT.Ln))
                act.wait_ge(ss_done, TURN[v])
                b = len(spans(c0, w))
                out = factors(v)[:, c0:c0 + w].rearrange("p (b n) -> p b n", b=b)
                rstd(out, PS[:, 6:6 + b, 0:w // b], D_MODEL).then_inc(rstd_rdy, 1)
            if v == 4:
                return
            for k in range(KD):
                act.wait_ge(uf_rdy, KD * ROUND[v] + k + 1)
                if v == 5:
                    A(UH[:, k, c0:c0 + w], sq[:, k, c0:c0 + w], ACT.Identity, bias=MOD[:, k:k + 1])\
                        .then_inc(uh_rdy, 1)
                else:
                    A(UH[:, k, c0:c0 + w], sq[:, k, c0:c0 + w], ACT.Copy).then_inc(uh_rdy, 1)

        def ffn(f, c0, w):
            b = len(spans(c0, w))
            m = w // b
            for half in range(2):
                m0 = f * FJ + half * FH - START[f"f{f + 1}u{half}"]

                def up(n, j, turn, slot, nxt):
                    next_hi(n, turn, slot, nxt)
                    q = n + m0
                    act.wait_ge(mm_done, n + 1)
                    if not isinstance(q, int) or q >= 2:
                        act.wait_ge(silu_rdy, q - 1)
                    A(TANH[:, slot, 0:w].rearrange("p (b n) -> p b n", b=b),
                      PS[:, 4 * slot:4 * slot + b, 0:m], ACT.Tanh, scale=0.5).then_inc(tanh_rdy, 1)
                    act.wait_ge(evac, n + 1)
                    A(GH[:, j, c0:c0 + w], GF[:, slot, 0:w], ACT.Copy).then_inc(gh_rdy, 1)

                def down(n, j, turn, slot, nxt):
                    next_hi(n, turn, slot, nxt)

                stream(act, f"f{f + 1}u{half}", up)
                stream(act, f"f{f + 1}d{half}", down)

        def only_weights(n, j, turn, slot, nxt):
            next_hi(n, turn, slot, nxt)

        act.wait_ge(eps_rdy, 1)
        norm(0, lambda: hi_part(0, 0, 0, SLOT))
        act.wait_ge(c_ld, 16)
        A(SILUT[:, :], SILUC[:, :], ACT.Tanh, scale=0.5).then_inc(ct_rdy, 1)
        ffn(0, 0, T1)
        norm(1)

        def conv_tanh(c):
            for t in (2 * c - 4, 2 * c - 3):
                act.wait_ge(cv_c, t + 1)
                if t >= 2:
                    act.wait_ge(cv_s, t - 1)
                A(CTT[:, t % 2, :], CT[:, t % 2, :], ACT.Tanh, scale=0.5).then_inc(cv_t, 1)

        def latents(j):
            if j in (2, 4):
                act.wait_ge(c_ss, j // 2)
                r = (RQ if j == 2 else RK)[:, :].rearrange("p (b n) -> p b n", b=3)
                rstd(r, PS[:, 4:7, 320:320 + T1 // 3], 2 * P if j == 2 else P).then_inc(c_r, 1)
            if j in (1, 2):
                act.wait_ge(evac, START["w1"] + j)
                for k in ((0, 1) if j == 1 else (2,)):
                    A(CF[:, k, :], PR[:, k, :], ACT.Square).then_inc(c_sq, 1)
            if j == 5:
                act.wait_ge(c_f, 1)
                A(CHI[:, :, :], CF[:, :, :], ACT.Copy).then_inc(c_hi, 1)

        def with_conv(n, j, turn, slot, nxt):
            next_hi(n, turn, slot, nxt)
            latents(j)
            if j >= 3:
                conv_tanh(j - 1)

        stream(act, "w1", with_conv, straight=True)
        n = START["uq"]
        hi_part(n + 1, 1, (n + 1) // 2, WIDTH["ukv"])
        scale = float(96) ** -0.5
        for t in range(4):
            act.wait_ge(uq_ps, t + 1)
            for p in range(2):
                A(QH[0:CH, 2 * t + p, :], PS[CH * p:CH * (p + 1), t, 0:SEQ], ACT.Copy,
                  scale=scale).then_inc(q_act, 1)
        conv_tanh(7)
        hi_part(n + 2, 0, (n + 2) // 2, WIDTH["z"])
        for t in range(4):
            act.wait_ge(kn_ps, t + 1)
            for p in range(2):
                A(halves(KH[0:CH, 2 * t + p, :]), PS[CH * p:CH * (p + 1), 2 * t:2 * t + 2, 0:HT],
                  ACT.Copy).then_inc(k_act, 1)

        def attention(part):
            U = PARTS[part]
            PB, PTS, OSB, OTF, NM, RS, RI = bufs(part)
            base = U[0]["u"]
            ends = {x["u"] - base: x for x in U if x["last"]}
            lag = LAG[part]
            for i in range(len(U) + 7 + lag):
                if i < len(U):
                    x = U[i]
                    s, c = x["u"] % 2, x["u"] - base
                    act.wait_ge(max_rdy, x["u"] + 1)
                    if i >= 2:
                        act.wait_ge(pt_ps, x["u"] - 1)
                    A(PB[:, s, 0:x["total"]], scores(part, x["u"], 0, x["total"]), ACT.Exp, bias=NM[:, c:c + 1],
                      accum_out=RS[:, c:c + 1]).then_inc(exp_rdy, 1)
                if 1 <= i <= len(U):
                    x = U[i - 1]
                    s = x["u"] % 2
                    act.wait_ge(pt_ps, x["u"] + 1)
                    if i >= 3:
                        act.wait_ge(pv_done, x["u"] - 1)
                    if x["vm"] is not None:
                        A(PTM[:, s, :], PS[0:N_META, 2 * s + 1, P:2 * P], ACT.Copy)
                    A(PTS[:, s, 0:x["w"]], PS[:, 4 + s, 0:x["w"]], ACT.Copy).then_inc(pt_rdy, 1)
                x = ends.get(i - 1)
                if x is not None and x["sink"]:
                    act.wait_ge(sink_s, x["qi"] + 1)
                    A(SNK[:, 8:16], SNK[:, 0:8], ACT.Exp).then_inc(sink_e, 1)
                x = ends.get(i - 6 - lag)
                if x is not None and x["tg"] is not None:
                    act.wait_ge(ot_f, x["tg"] + 1)
                    hi, f0 = (OTH, 0) if part == 0 else (YH, 0 if x["kind"] == "A" else 4)
                    A(hi[:, f0:f0 + 4, P * x["qi"]:P * (x["qi"] + 1)],
                      OTF[:, :].rearrange("p (f q) -> p f q", f=4), ACT.Copy).then_inc(ot_hi, 1)

        attention(0)
        for i in range(2):
            act.wait_ge(l_ss, 4 * i + 4)
            rstd(GR[:, 4 * i:4 * i + 4, :].rearrange("p t (b n) -> p (t b) n", b=2), PS[:, :, 0:HT], 1.0,
                 scale=0.25).then_inc(l_r, 1)
        R8 = slice(32, 32 + NH)
        act.wait_ge(gt_d, 1)
        A(BT8[:, PAD:], PR[0:NH, 3, :], ACT.Tanh, scale=0.5).then_inc(gt_a, 1)
        A(CST[R8, 2:3], COL[R8, COLS["alog"]:COLS["alog"] + 1], ACT.Exp).then_inc(gt_a, 1)
        act.wait_ge(gt_d, 3)
        chain(A(GT[R8, 1, PAD:], GT[R8, 1, PAD:], ACT.Exp, scale=-1.0))
        A(GT[R8, 1, PAD:], GT[R8, 1, PAD:], ACT.Ln, bias=1.0).then_inc(gt_a, 1)
        act.wait_ge(gb_ps, 1)
        A(pair_rows(GB).rearrange("p t (b n) -> p (t b) n", b=2), PS[:, :, 0:NCH * CH // 2],
          ACT.Copy).then_inc(gb_ev, 1)
        act.wait_ge(dc_d, 2)
        A(EU[:, :, :], EU[:, :, :], ACT.Exp).then_inc(dc_a, 1)
        A(GP[:, 3:6, :], GP[:, 3:6, :], ACT.Exp).then_inc(dc_a, 1)
        A(GB[:, :, :], GB[:, :, :], ACT.Exp).then_inc(dc_a, 1)
        for g in range(NB // SIDE):
            for lv in range(1, LEVELS):
                for x in range(SIDE):
                    act.wait_ge(a_ps, SIDE * (LEVELS * g + lv) + x + 1)
                    if lv > 1 or g:
                        act.wait_ge(d_ps, SIDE * ((LEVELS - 1) * g + lv - 2) + x + 1)
                    A(AB[:, x, :, :], PS[:, 2 * x, 0:UB * CH].rearrange("p (r c) -> p r c", c=CH),
                      ACT.Copy).then_inc(ab_rdy, 1)
            for x in range(SIDE):
                b = SIDE * g + x
                act.wait_ge(uw_ps, b + 1)
                A(units(KBG, b), PS[:, 2 * x + 1, 0:UB * CH].rearrange("p (r c) -> p r c", c=CH),
                  ACT.Copy).then_inc(w_rdy, 1)
        for n in range(NCH):
            act.wait_ge(o_ps, n + 1)
            A(chunk_of(EU, n), PS[:, 2 + n % 2, 0:4 * CH].rearrange("p (t c) -> p t c", c=CH),
              ACT.Copy).then_inc(o_ev, 1)
        act.wait_ge(o_ev, NCH)
        A(OSQ[:, :, :], pair_rows(EU)[:, :, PAD + N_META:], ACT.Square).then_inc(osq_rdy, 1)
        norm(2)
        act.wait_ge(oss_ps, 1)
        for i, (t, b) in enumerate(((0, 2), (2, 6))):
            ins = rstd(OR[:, t:t + 2, :], PS[:, b:b + 2, 0:SEQ], CH)
        ins.then_inc(or_rdy, 1)
        stream(act, "z", only_weights)
        act.wait_ge(evac, START["mg"])
        A(OSQ[:, :, :], ZT[:, :, :], ACT.Tanh, scale=0.5).then_inc(zt_rdy, 1)
        act.wait_ge(gof_rdy, 1)
        A(GOH[:, :, :], OR[:, :, :], ACT.Copy).then_inc(goh_rdy, 1)
        act.sem_inc(tg_rdy, 1)

        def merge(n, j, turn, slot, nxt):
            next_hi(n, turn, slot, nxt)
            d1 = turn - (START["mg"] // 2 - 1)
            if slot == 0:
                act.wait_ge(mm_done, n + 1)
                act.wait_ge(evac, n)
                A(TG[:, :, :], PS[:, 0:2, 0:SEQ], ACT.Tanh, scale=0.5).then_inc(tg_rdy, 1)
            else:
                act.wait_ge(mf_rdy, d1)
                k = d1 - 1
                A(MH[:, k, :], MF[:, 1, :], ACT.Copy).then_inc(mh_rdy, 1)

        stream(act, "mg", merge)
        stream(act, "wo", only_weights)
        norm(3)
        ffn(1, N_META, SEQ)
        norm(4)
        norm(5)

        def head_squares(c):
            act.wait_ge(evac, START["wi"] + c + 1)
            if c:
                act.wait_ge(n_ss, c)
            w = 2 if c < 5 else 1
            A(PSQ[:, 0:w, :], P2[:, 2 * c:2 * c + w, :], ACT.Square).then_inc(n_sq, 1)

        def head_factors(c):
            act.wait_ge(n_ss, c + 1)
            if c:
                act.wait_ge(n_n, c)
            b, w = 2 + 4 * (c % 2), 2 if c < 5 else 1
            rstd(PRS[:, 0:w, :], PS[:, b:b + w, 0:SEQ], CH).then_inc(n_r, 1)

        def gate_tanh(c):
            act.wait_ge(evac, START["wi"] + c + 1)
            if c == 6:
                act.wait_ge(n_n, 6)
            else:
                act.wait_ge(z_s, c - 6)
            a, w = (1, 1) if c == 6 else (0, 1 if c == 10 else 2)
            A(PRS[:, a:a + w, :], P2[:, 2 * c + a:2 * c + a + w, :], ACT.Tanh, scale=0.5).then_inc(z_t, 1)

        def into_heads(n, j, turn, slot, nxt):
            next_hi(n, turn, slot, nxt)
            if 1 <= j <= 6:
                head_squares(j - 1)
            if 2 <= j <= 7:
                head_factors(j - 2)
            if j >= 8:
                gate_tanh(j - 2)

        stream(act, "wi", into_heads, straight=True)
        stream(act, "wt", only_weights)
        gate_tanh(8)
        stream(act, "wv", only_weights)
        gate_tanh(9)
        gate_tanh(10)
        act.wait_ge(bg_d, 1)
        A(GATE[:, :, :], GATE[:, :, :], ACT.Tanh, scale=0.5).then_inc(bg_a, 1)
        act.wait_ge(hc_ps, 1)
        A(HTN[0:2 * NCMP, :, :], PS[0:2 * NCMP, 0:2, 0:256], ACT.Tanh, scale=0.5).then_inc(hc_t, 1)
        act.wait_ge(kc_f, 1)
        A(PSQ[:, 0, 0:NCMP], KCF[:, 0:NCMP], ACT.Square).then_inc(kc_sq, 1)
        act.wait_ge(kc_ss, 1)
        rstd(PRS[:, 0, 0:NCMP], PS[:, 2, 0:NCMP], CH).then_inc(kc_r, 1)
        act.wait_ge(cs_z, 1)
        A(CPB[:, :, :], CPB[:, :, :], ACT.Exp).then_inc(cs_e, 1)
        for qi in range(QT):
            act.wait_ge(ct_ps, qi + 1)
            if qi >= 2:
                act.wait_ge(co_ps, qi - 1)
            b = (4, 2)[qi % 2]
            A(CPT[:, qi % 2, :, :].rearrange("p (a h) q -> p a (h q)", a=2), PS[0:NCMP, b:b + 2, 0:512],
              ACT.Copy).then_inc(ct_ev, 1)
        attention(1)
        stream(act, "wo2", only_weights)

    @block.vector
    def _(dve):
        V = nc.vector
        chain = Chain(dve, dve_chain)
        TT, STT, TS = V.tensor_tensor, V.scalar_tensor_tensor, V.tensor_scalar

        def lo_part(n, slot, w):
            if w:
                dve.wait_ge(hi_rdy, n + 1)
                if not isinstance(n, int) or n >= 2:
                    dve.wait_ge(mm_done, n - 1)
                TT(WLO[:, slot, 0:w], RAW[:, slot, 0:w], WHI[:, slot, 0:w].bitcast(f32),
                   ALU.subtract).then_inc(lo_rdy, 1)

        def next_lo(n, slot, nxt):
            lo_part(n + 1, 1 - slot, nxt)

        def norm(v, gain, gain_of=None):
            c0, w = NORMS[v]
            cs = slice(c0, c0 + w)
            sq = SQ2 if v == 2 else SQ
            r = factors(v)
            if v != 2:
                dve.wait_ge(rstd_rdy, TURN[v])
            if v == 4:
                for k in range(KD):
                    STT(H[:, k, cs], H[:, k, cs], col(gain, k), r[:, cs], ALU.mult, ALU.mult)\
                        .then_inc(x2_rdy, 1)
                return

            def low(k):
                dve.wait_ge(uh_rdy, KD * ROUND[v] + k + 1)
                uh = UH[:, k, cs].bitcast(f32)
                if v == 5:
                    STT(UL[:, k, cs], sq[:, k, cs], MOD[:, k:k + 1], uh, ALU.add, ALU.subtract)\
                        .then_inc(ul_rdy, 1)
                else:
                    TT(UL[:, k, cs], sq[:, k, cs], uh, ALU.subtract).then_inc(ul_rdy, 1)

            for k in range(KD):
                STT(sq[:, k, cs], H[:, k, cs], col(gain, k), r[:, cs], ALU.mult, ALU.mult)\
                    .then_inc(uf_rdy, 1)
                if k:
                    low(k - 1)
            low(KD - 1)

        def start_sum(v, acc):
            V.memset(acc, 0.0).then_inc(acc_rdy, 1)

        def add_squares(v, j, h, tmp, acc):
            turn, wide = SUMMED[v]
            base = sum(KD // SUMMED[x][1] for x in (1, 3, 4)[:turn])
            dve.wait_ge(acc_rdy, j + base + turn + 1)
            TT(tmp, h, h, ALU.mult).then_inc(tsq_rdy, 1)
            dve.wait_ge(tsq_rdy, j + base + 1)
            TT(acc, acc, tmp, ALU.add).then_inc(acc_rdy, 1)

        def ada(m, slot, turn):
            dve.wait_ge(ada_ld[slot], 16 * turn + 16)
            if not isinstance(m, int) or m >= 1:
                dve.wait_ge(ada_used, m)
            STT(JUNK[:, :], ADA[:, slot, :], 0.5, SILUC[:, :], ALU.mult, ALU.mult,
                accum_out=MOD[:, bass.ds(m, 1)] if not isinstance(m, int) else MOD[:, m:m + 1])\
                .then_inc(ada_used, 1)

        def ffn(f, c0, w):
            b = len(spans(c0, w))
            m = w // b
            wide = lambda t: t.rearrange("p (b n) -> p b n", b=b)
            for half in range(2):
                n0 = START[f"f{f + 1}u{half}"]
                m0 = f * FJ + half * FH - n0

                def up(n, j, turn, slot, nxt):
                    next_lo(n, slot, nxt)
                    q = n + m0
                    if f == 0:
                        ada(q, (slot + m0) % 2, turn + (slot + m0) // 2)
                    ps = PS[:, 4 * slot:4 * slot + 4, 0:m]
                    dve.wait_ge(tanh_rdy, q + 1)
                    STT(wide(SILU[:, slot, 0:w]), wide(TANH[:, slot, 0:w]), 1.0, ps[:, 0:b, :], ALU.add,
                        ALU.mult).then_inc(silu_rdy, 1)
                    dve.wait_ge(silu_rdy, q + 1)
                    if not isinstance(q, int) or q >= 2:
                        dve.wait_ge(gl_rdy, q - 1)
                    TT(wide(GF[:, slot, 0:w]), wide(SILU[:, slot, 0:w]), ps[:, 2:2 + b, :],
                       ALU.mult).then_inc(evac, 1)
                    dve.wait_ge(gh_rdy, q + 1)
                    TT(GL[:, j, c0:c0 + w], GF[:, slot, 0:w], GH[:, j, c0:c0 + w].bitcast(f32),
                       ALU.subtract).then_inc(gl_rdy, 1)

                def down(n, j, turn, slot, nxt):
                    next_lo(n, slot, nxt)
                    dve.wait_ge(mm_done, n + 1)
                    h = wide(H[:, j, c0:c0 + w])
                    STT(h, PS[:, 4 * slot:4 * slot + b, 0:m], 0.25, h, ALU.mult, ALU.add)\
                        .then_inc(evac, 1)
                    if half == 1:
                        dve.wait_ge(evac, n + 1)
                        add_squares((1, 4)[f], j, h, wide(SILU[:, 0, 0:w]), wide(RSTD[:, c0:c0 + w]))

                stream(dve, f"f{f + 1}u{half}", up)
                if half == 1:
                    start_sum((1, 4)[f], RSTD[:, c0:c0 + w])
                stream(dve, f"f{f + 1}d{half}", down)

        V.memset(CST[:, 0:1], EPS).then_inc(eps_rdy, 1)
        dve.wait_ge(rev_ps, 1)
        V.tensor_copy(JUNK[0:16, 0:383], PS[0:16, 0, 0:383]).then_inc(rev_rdy, 1)
        dve.wait_ge(col_ld, 16)
        lo_part(0, 0, SLOT)
        norm(0, "ffn1")
        dve.wait_ge(ct_rdy, 1)
        dve.wait_ge(rev_st, 32)
        chain(STT(SILUC[:, :], SILUT[:, :], 1.0, SILUC[:, :], ALU.add, ALU.mult))
        ffn(0, 0, T1)
        for m in range(FJ, 24):
            ada(m, m % 2, m // 2)
        dve.wait_ge(ada_used, 24)
        chain(TT(MOD[:, :], MOD[:, :], col("bada", 0, 24), ALU.add))
        chain(STT(col("ng2", 0, 8), MOD[:, 8:16], 1.0, col("ng2", 0, 8), ALU.add, ALU.mult))
        chain(TS(col("qa", 0, 2), col("qa", 0, 2), 0.125, None, ALU.mult))
        norm(1, "mix")

        def project(dst, w, per):
            def body(n, j, turn, slot, nxt):
                next_lo(n, slot, nxt)
                dve.wait_ge(mm_done, n + 1)
                if w > 512:
                    for t in range(2):
                        last = V.tensor_copy(halves(dst[:, 2 * j + t, :]),
                                             PS[:, 4 * slot + 2 * t:4 * slot + 2 * t + 2, 0:HT])
                        if t == 0:
                            last.then_inc(dve_chain, 1)
                else:
                    last = V.tensor_copy(dst[:, bass.ds(2 * j, 2), :], PS[:, 4 * slot:4 * slot + 2, 0:SEQ])
                last.then_inc(evac, 1)
            return body

        into = project(PR, T1, 2)

        def conv_taps(c):
            dve.wait_ge(evac, START["w1"] + c + 1)
            for d in (3, 2, 1, 0):
                for t in (2 * c - 4, 2 * c - 3):
                    y, x, w = CT[:, t % 2, :], PR[:, 4 + t, :], col("conv", 4 * t + d)
                    if d == 3:
                        if t >= 2:
                            dve.wait_ge(cv_s, t - 1)
                        TS(y, x, w, None, ALU.mult).then_inc(cv_m, 1)
                    else:
                        e = 3 - d
                        dve.wait_ge(cv_m, 3 * (t - t % 2) + 2 * e + t % 2 - 1)
                        STT(y[:, e:T1], x[:, 0:T1 - e], w, y[:, e:T1], ALU.mult, ALU.add)\
                            .then_inc(cv_m if d else cv_c, 1)

        def conv_silu(c):
            for t in (2 * c - 4, 2 * c - 3):
                dve.wait_ge(cv_t, t + 1)
                dve.wait_ge(cv_c, t + 1)
                STT(PR[:, 4 + t, :], CTT[:, t % 2, :], 1.0, CT[:, t % 2, :], ALU.add, ALU.mult)\
                    .then_inc(cv_s, 1)

        def with_conv(n, j, turn, slot, nxt):
            into(n, j, turn, slot, nxt)
            chain.n += 1
            if j == 4:
                dve.wait_ge(dve_chain, chain.n)
                dve.wait_ge(c_r, 2)
                for k in range(3):
                    last = STT(CF[:, k, :], PR[:, k, :], col("qn", k) if k < 2 else col("kvn"),
                               RQ[:, :] if k < 2 else RK[:, :], ALU.mult, ALU.mult)
                last.then_inc(c_f, 1)
            if j == 5:
                dve.wait_ge(c_hi, 1)
                TT(CLO[:, :, :], CF[:, :, :], CHI[:, :, :].bitcast(f32), ALU.subtract).then_inc(c_lo, 1)
            if j >= 4:
                conv_silu(j - 2)
            if j >= 3:
                conv_taps(j - 1)

        stream(dve, "w1", with_conv, straight=True)
        dve.wait_ge(dve_chain, chain.n)
        dve.wait_ge(evac, START["uq"])
        n = START["uq"]
        lo_part(n + 1, 1, WIDTH["ukv"])
        conv_silu(6)
        conv_taps(7)
        scale = float(96) ** -0.5
        cos, sin = tab("cos", 0, T1), tab("sin", 0, T1)
        dve.wait_ge(uq_ps, 8)
        for r in range(2):
            STT(ROT[:, r, :], PS[:, 4 + r, 0:SEQ], scale, cos[:, N_META:T1], ALU.mult, ALU.mult)
            last = STT(ROT[:, 2 + r, :], PS[:, 6 + r, 0:SEQ], scale, sin[:, N_META:T1], ALU.mult, ALU.mult)
        chain(last)
        for h in range(NH):
            rows = slice(32 * (h % 4), 32 * (h % 4) + 32)
            last = TT(QH[CH:96, h, :], ROT[rows, h // 4, :], ROT[rows, 2 + h // 4, :], ALU.add)
        chain(last)
        dve.wait_ge(q_act, NH)
        dve.sem_inc(evac, 1)
        conv_silu(7)
        lo_part(n + 2, 0, WIDTH["z"])
        dve.wait_ge(mm_done, n + 2)
        TT(KROT[CH:96, 0, :], PR[CH:96, 3, :], cos[CH:96, :], ALU.mult)
        chain(TT(KROT[CH:96, 1, :], PR[96:128, 3, :], sin[96:128, :], ALU.mult))
        for h in range(NH):
            last = TT(KH[CH:96, h, :], KROT[CH:96, 0, :], KROT[CH:96, 1, :], ALU.add)
        last.then_inc(kr_dve, 1)
        chain(V.tensor_copy(VM[0:N_META, 0, :], PS[0:N_META, 0, 0:SEQ]))
        for t in range(1, 5):
            last = V.tensor_copy(VM[:, t, :], PS[:, t, 0:SEQ])
        chain(last)
        dve.wait_ge(kr_dve, 1)
        dve.sem_inc(evac, 1)

        def attention(part):
            U = PARTS[part]
            PB, PTS, OSB, OTF, NM, RS, RI = bufs(part)
            base, gbase = U[0]["u"], U[0]["g"]
            ends = {x["u"] - base: x for x in U if x["last"]}
            lag = LAG[part]
            for i in range(len(U) + 8 + lag):
                if i < len(U):
                    x = U[i]
                    c = x["u"] - base
                    a, n, bias = x["bias"]
                    dve.wait_ge(s_ps, x["u"] + 1)
                    near = scores(part, x["u"], a, a + n)
                    chain(TT(near, near, bias, ALU.add))
                    red = V.tensor_reduce(NM[:, c:c + 1], scores(part, x["u"], 0, x["total"]), AX.X, ALU.max,
                                          negate=True)
                    if x["sink"]:
                        chain(red)
                        red = TT(NM[:, c:c + 1], NM[:, c:c + 1], NSINK[:, x["h"]:x["h"] + 1], ALU.min)
                    red.then_inc(max_rdy, 1)
                x = ends.get(i - 1)
                if x is not None and x["sink"]:
                    c = x["u"] - base
                    dve.wait_ge(max_rdy, x["u"] + 1)
                    if x["qi"] > 0:
                        dve.wait_ge(sink_e, x["qi"])
                    TT(SNK[:, 0:8], NM[:, c - 7:c + 1], col("sink", 0, 8), ALU.add).then_inc(sink_s, 1)
                x = ends.get(i - 2 - lag)
                if x is not None:
                    c, g, qi = x["u"] - base, x["g"], x["qi"]
                    rs, ri = RS[:, c - 7:c + 1], RI[:, c - 7:c + 1]
                    dve.wait_ge(pv_done, x["u"] + 1)
                    if x["sink"]:
                        dve.wait_ge(sink_e, qi + 1)
                        chain(TT(rs, rs, SNK[:, 8:16], ALU.add))
                    chain(V.reciprocal(ri, rs))
                    o = outputs(part, g).rearrange("p (h d) -> p h d", h=NH)
                    if x["kind"] in ("sel", "win"):
                        g_col = GATE[:, qi, :].rearrange("p (h b) -> p b h", b=3)[:, 1 if x["kind"] == "sel" else 2, :]
                        chain(TT(ri, ri, g_col, ALU.mult))
                    tg = x["tg"] if x["tg"] is not None else U[c + NH]["tg"]
                    osb = OSB[:, tg % 2, :]
                    wide = lambda t: t.rearrange("p (h d) -> p h d", h=NH)
                    norm8 = ri.unsqueeze(2).to_broadcast([P, NH, CH])
                    if x["kind"] == "win":
                        TT(wide(OBT[:, :]), o, norm8, ALU.mult).then_inc(o_free, 1)
                        dve.wait_ge(o_free, g + 1)
                        chain(TT(osb, osb, OBT[:, :], ALU.add))
                        TT(osb, osb, OC[:, qi, :], ALU.add).then_inc(o_rdy, 1)
                    else:
                        if tg >= 2:
                            dve.wait_ge(ot_ps, tg - 1)
                        TT(wide(osb), o, norm8, ALU.mult).then_inc(o_free, 1)
                        dve.wait_ge(o_free, g + 1)
                        if x["kind"] != "sel":
                            dve.sem_inc(o_rdy, 1)
                x = ends.get(i - 5 - lag)
                if x is not None and x["tg"] is not None:
                    dve.wait_ge(ot_ps, x["tg"] + 1)
                    if x["tg"] > 0:
                        dve.wait_ge(ot_lo, x["tg"])
                    ps = PS[:, 7, :].rearrange("p (f q) -> p f q", f=4)
                    otf = OTF[:, :].rearrange("p (f q) -> p f q", f=4)
                    if part == 0:
                        V.tensor_copy(otf, ps).then_inc(ot_f, 1)
                    else:
                        f0 = 13 if x["kind"] == "A" else 17
                        STT(otf, ps, 0.5, P2[:, f0:f0 + 4, P * x["qi"]:P * (x["qi"] + 1)], ALU.mult,
                            ALU.mult).then_inc(ot_f, 1)
                x = ends.get(i - 7 - lag)
                if x is not None and x["tg"] is not None:
                    dve.wait_ge(ot_hi, x["tg"] + 1)
                    hi, lo, f0 = (OTH, OTL, 0) if part == 0 else (YH, YL, 0 if x["kind"] == "A" else 4)
                    sl = slice(P * x["qi"], P * (x["qi"] + 1))
                    TT(lo[:, f0:f0 + 4, sl], OTF[:, :].rearrange("p (f q) -> p f q", f=4),
                       hi[:, f0:f0 + 4, sl].bitcast(f32), ALU.subtract).then_inc(ot_lo, 1)

        attention(0)
        dve.wait_ge(ot_lo, QT)
        for t in range(8):
            TT(GSQ[:, t, :], PR[:, 4 + t, :], PR[:, 4 + t, :], ALU.mult).then_inc(l_sq, 1)
        V.memset(CV[:, :, 0:PAD], 0.0).then_inc(dve_chain, 1)
        chain.n += 1
        V.tensor_copy(CV[:, 8:12, PAD:], PR[:, 12:16, :])
        for t in range(8):
            dve.wait_ge(l_r, t // 4 + 1)
            STT(CV[:, t, PAD:], PR[:, 4 + t, :], 0.0625 if t < 4 else 0.5, GR[:, t, :], ALU.mult,
                ALU.mult).then_inc(l_n, 1)
        dve.wait_ge(l_n, 8)
        R8 = slice(32, 32 + NH)
        V.memset(GT[R8, 3, 0:PAD], 0.0)
        V.memset(GT[R8, 4, :], 1.0).then_inc(dve_chain, 1)
        chain.n += 1
        V.memset(BT8[:, 0:PAD], 0.0).then_inc(gt_d, 1)
        dve.wait_ge(dve_chain, chain.n)
        chain(V.memset(GT[R8, 4, :].rearrange("p (n c) -> p n c", c=CH)[:, :, 0:1], 0.0))
        x = GT[R8, 0, PAD:]
        TS(x, PR[R8, 3, :], COL[R8, COLS["dtb"]:COLS["dtb"] + 1], None, ALU.add).then_inc(gt_d, 1)
        dve.wait_ge(gt_d, 2)
        chain(TS(GT[R8, 1, PAD:], x, -1.0, None, ALU.mult))
        TT(GT[R8, 1, PAD:], x, GT[R8, 1, PAD:], ALU.max).then_inc(gt_d, 1)
        dve.wait_ge(gt_a, 1)
        TS(BT8[:, PAD:], BT8[:, PAD:], 1.0, 0.5, ALU.add, ALU.mult).then_inc(gt_d, 1)
        dve.wait_ge(gt_a, 3)
        STT(GT[R8, 3, PAD:], x, 0.0, GT[R8, 1, PAD:], ALU.max, ALU.add).then_inc(gt_d, 1)
        dve.wait_ge(gt_d, 5)
        TS(GT[R8, 3, PAD:], GT[R8, 3, PAD:], CST[R8, 2:3], -1.0, ALU.mult, ALU.mult).then_inc(gt_d, 1)
        dve.wait_ge(gt_d, 6)
        V.tensor_tensor_scan(GT[R8, 2, :], GT[R8, 4, :], GT[R8, 3, :], 0.0, ALU.mult, ALU.add)\
            .then_inc(gt_d, 3)
        dve.wait_ge(gp_ps, 1)
        V.tensor_copy(GP[:, 0:2, :].rearrange("p i (t n) -> p i n t", t=4),
                      PS[:, 0:2, 0:NU].rearrange("p i (n t) -> p i n t", t=4)).then_inc(gp_ev, 1)
        dve.wait_ge(gp_ev, 1)
        dve.wait_ge(bb_ps, 1)
        W2 = NCH * CH // 2
        V.tensor_copy(pair_rows(TTT).rearrange("p t (b n) -> p (t b) n", b=2), PS[:, :, 0:W2])\
            .then_inc(bb_ev, 1)
        dve.wait_ge(bb_ev, 1)
        dve.wait_ge(gb_ev, 1)
        chain(TT(EU[:, :, :], GB[:, :, :], along(GP[:, 1, :], NU), ALU.subtract))
        TS(EU[:, :, :], EU[:, :, :], 0.0, None, ALU.min).then_inc(dc_d, 1)
        chain(V.tensor_copy(GP[:, 2, :], GB[:, :, CH - 1]))
        V.tensor_copy(GP[:, 3, :], GP[:, 1, :])
        V.tensor_copy(GP[:, 4, :], GP[:, 2, :])
        chain(TT(GP[:, 5, :], GP[:, 2, :], GP[:, 1, :], ALU.subtract))
        chain(TS(GP[:, 6, :], GP[:, 0, :], 0.5, None, ALU.mult))
        dve.sem_inc(dc_d, 1)
        chain(TT(pair_rows(TTT), CV[:, 4:8, :], pair_rows(TTT), ALU.mult))
        dve.wait_ge(dc_a, 2)
        TT(GP[:, 7, :], GP[:, 0, :], GP[:, 3, :], ALU.mult)
        chain(TT(EU[:, :, :], EU[:, :, :], over(tab("mincl", 0, CH), NU), ALU.mult))
        dve.wait_ge(dc_a, 3)
        chain(TT(pair_rows(GB), CV[:, 0:4, :], pair_rows(GB), ALU.mult))
        dve.sem_inc(un_rdy, 1)
        for b in range(NB):
            dve.wait_ge(pr_ps, b + 1)

            def bank(i):
                return PS[:, 4 * (b % 2) + i, 0:UB * CH].rearrange("p (r c) -> p r c", c=CH)

            def value(i):
                return along(GP[:, i, b * UB:(b + 1) * UB], UB)

            chain(TT(units(IT, b), bank(1), units(EU, b), ALU.mult))
            chain(TT(units(EU, b), bank(0), units(EU, b), ALU.mult))
            TT(units(EU, b), units(EU, b), over(tab("mstrict", 0, CH), UB), ALU.mult)
            TT(units(KBG, b), bank(2), value(7), ALU.mult)
            TT(units(KDEC, b), bank(2), value(5), ALU.mult)
            chain(TT(units(VB, b), bank(3), value(6), ALU.mult))
            dve.sem_inc(pr_rdy, 1)
        LVL = TAB[:, TABS["lvl"]:TABS["lvl"] + LEVELS * CH].rearrange("p (l c) -> p l c", c=CH)
        dve.wait_ge(gt_d, 9)
        identity = over(tab("i64", 0, CH), UB)
        for g in range(NB // SIDE):

            def mask_level(lv, x):
                if lv:
                    dve.wait_ge(a_ps, SIDE * (LEVELS * g + lv - 1) + x + 1)
                TT(UMB[:, x, :, :], units(EU, SIDE * g + x),
                   LVL[:, lv:lv + 1, :].to_broadcast([P, UB, CH]), ALU.mult).then_inc(um_rdy, 1)

            for x in range(SIDE):
                mask_level(0, x)
            for x in range(SIDE):
                i = SIDE * LEVELS * g + x
                dve.wait_ge(um_rdy, i + 1)
                V.tensor_tensor(units(TTT, SIDE * g + x), identity, UMB[:, x, :, :], ALU.subtract)
                dve.wait_ge(a_ps, i + 1)
                TT(TB[:, x, :, :], identity, PS[:, 2 * x, 0:UB * CH].rearrange("p (r c) -> p r c", c=CH),
                   ALU.subtract).then_inc(t_rdy, 1)
                dve.wait_ge(t_rdy, i + 1)
                mask_level(1, x)
            for lv in range(1, LEVELS):
                for x in range(SIDE):
                    b = SIDE * g + x
                    dve.wait_ge(d_ps, SIDE * ((LEVELS - 1) * g + lv - 1) + x + 1)
                    dve.wait_ge(t_rdy, SIDE * (LEVELS * g + lv - 1) + x + 1)

                    def bank(k):
                        return PS[:, 2 * x + k, 0:UB * CH].rearrange("p (r c) -> p r c", c=CH)

                    if lv < LEVELS - 1:
                        TT(TB[:, x, :, :], TB[:, x, :, :], bank(0), ALU.subtract)
                    TT(units(TTT, b), units(TTT, b), bank(1), ALU.subtract).then_inc(t_rdy, 1)
                    if lv < LEVELS - 1:
                        mask_level(lv + 1, x)
            for x in range(SIDE):
                b = SIDE * g + x
                dve.wait_ge(uw_ps, b + 1)
                V.tensor_copy(units(VB, b), PS[:, 2 * x, 0:UB * CH].rearrange("p (r c) -> p r c", c=CH))\
                    .then_inc(u_rdy, 1)
        chain(V.memset(SV[:, 0, :, :], 0.0))
        dve.sem_inc(st_rdy, 1)
        for n in range(NCH):
            ws = PS[:, 0, 0:4 * CH].rearrange("p (t c) -> p t c", c=CH)
            sa = PS[:, 1, 0:4 * CH].rearrange("p (t c) -> p t c", c=CH)
            if n < NCH - 1:
                egl = GP[:, 4, :].rearrange("p (t n) -> p t n", n=NCH)[:, :, n:n + 1].to_broadcast([P, 4, CH])
                TT(SE[:, :, :], SV[:, n % 2, :, :], egl, ALU.mult).then_inc(se_rdy, 1)
            if n >= 2:
                dve.wait_ge(o_ps, n - 1)
            dve.wait_ge(ws_ps, n + 1)
            TT(VN[:, n % 2, :, :], chunk_of(VB, n), ws, ALU.subtract).then_inc(vn_rdy, 1)
            if n < NCH - 1:
                dve.wait_ge(se_rdy, n + 1)
                dve.wait_ge(sa_ps, n + 1)
                if n >= 1:
                    dve.wait_ge(o_ps, n)
                TT(SV[:, (n + 1) % 2, :, :], SE[:, :, :], sa, ALU.add).then_inc(st_rdy, 1)
                dve.wait_ge(st_rdy, n + 2)
        dve.wait_ge(o_ev, NCH)
        norm(2, "mix")
        dve.wait_ge(or_rdy, 1)
        STT(OR[:, :, :], pair_rows(EU)[:, :, PAD + N_META:], col("gdn"), OR[:, :, :], ALU.mult, ALU.mult)\
            .then_inc(dve_chain, 1)
        chain.n += 1
        stream(dve, "z", project(ZT, SEQ, 2))
        dve.wait_ge(dve_chain, chain.n)
        dve.wait_ge(zt_rdy, 1)
        chain(STT(ZT[:, :, :], OSQ[:, :, :], 1.0, ZT[:, :, :], ALU.add, ALU.mult))
        STT(OR[:, :, :], OR[:, :, :], 0.5, ZT[:, :, :], ALU.mult, ALU.mult).then_inc(gof_rdy, 1)
        dve.wait_ge(goh_rdy, 1)
        TT(GOL[:, :, :], OR[:, :, :], GOH[:, :, :].bitcast(f32), ALU.subtract).then_inc(gol_rdy, 1)

        def merge(n, j, turn, slot, nxt):
            next_lo(n, slot, nxt)
            if slot == 0:
                return
            d1 = turn - (START["mg"] // 2 - 1)
            dve.wait_ge(mm_done, n + 1)
            dve.wait_ge(tg_rdy, d1 + 1)
            dve.wait_ge(ml_rdy, d1)
            TT_ = STT(MF[:, 0, :], TG[:, 0, :], 1.0, PS[:, 4, 0:SEQ], ALU.add, ALU.mult)
            STT(MF[:, 1, :], TG[:, 1, :], 1.0, PS[:, 5, 0:SEQ], ALU.add, ALU.mult).then_inc(evac, 2)
            dve.wait_ge(evac, n + 1)
            TT(MF[:, 1, :], MF[:, 0, :], MF[:, 1, :], ALU.add).then_inc(mf_rdy, 1)
            dve.wait_ge(mh_rdy, d1)
            TT(ML[:, d1 - 1, :], MF[:, 1, :], MH[:, d1 - 1, :].bitcast(f32), ALU.subtract)\
                .then_inc(ml_rdy, 1)

        dve.sem_inc(ml_rdy, 1)
        stream(dve, "mg", merge)

        def outward(n, j, turn, slot, nxt):
            next_lo(n, slot, nxt)
            dve.wait_ge(mm_done, n + 1)
            h = H[:, bass.ds(2 * j, 2), N_META:T1]
            STT(h, PS[:, 4 * slot:4 * slot + 2, 0:SEQ], 0.5, h, ALU.mult, ALU.add).then_inc(evac, 1)
            dve.wait_ge(evac, n + 1)
            add_squares(3, j, h, MF[:, :, :], TG[:, :, :])

        dve.wait_ge(ml_rdy, KD + 1)
        start_sum(3, TG[:, :, :])
        stream(dve, "wo", outward)
        norm(3, "ffn2")
        ffn(1, N_META, SEQ)
        norm(4, "fin")
        dve.wait_ge(x2_rdy, KD)
        norm(5, "ng2")
        into = project(P2, SEQ, 2)
        gains = ["qa"] * 4 + ["qb"] * 4 + ["ka", "ks", "kw"]

        def head_norms(c):
            dve.wait_ge(n_r, c + 1)
            for t in range(2 if c < 5 else 1):
                last = STT(P2[:, 2 * c + t, :], P2[:, 2 * c + t, :], col(gains[2 * c + t]), PRS[:, t, :],
                           ALU.mult, ALU.mult)
            last.then_inc(n_n, 1)

        def gate_silu(c):
            dve.wait_ge(z_t, c - 5)
            a, w = (1, 1) if c == 6 else (0, 1 if c == 10 else 2)
            z = P2[:, 2 * c + a:2 * c + a + w, :]
            STT(z, PRS[:, a:a + w, :], 1.0, z, ALU.add, ALU.mult).then_inc(z_s, 1)

        def places(kv):
            src = P2[:, 11 + kv, :]
            for g in range(2):
                rows = slice(CH * g, CH * (g + 1))
                V.tensor_copy(XC[0:CH, kv, g, :], src[rows, :])
                last = V.tensor_copy(XC[CH:P, kv, g, 0:SEQ - 1], src[rows, 1:SEQ])
            last.then_inc(xc_rdy, 1)

        def blocks(kv):
            dve.wait_ge(xc_rdy, kv + 1)
            pos = col(("posk", "posv")[kv], 0, 16).unsqueeze(2).to_broadcast([P, 16, NCMP])
            for g in range(2):
                x = XC[:, kv, g, :].rearrange("p (m l t) -> p t l m", l=8, t=2)[:, 0, :, :]
                for far in range(2):
                    last = TT(XP[:, kv, 8 * far:8 * far + 8, NCMP * g:NCMP * (g + 1)],
                              x[:, :, far:far + NCMP], pos[:, 8 * far:8 * far + 8, :], ALU.add)
            last.then_inc(xc_rdy, 1 if kv == 0 else 2)

        def into_heads(n, j, turn, slot, nxt):
            into(n, j, turn, slot, nxt)
            if 2 <= j <= 7:
                head_norms(j - 2)
            if j >= 8:
                gate_silu(j - 2)
            if j == 8:
                dve.wait_ge(evac, START["wi"] + 7)
                places(0)
                places(1)
            if j == 9:
                blocks(0)
                dve.wait_ge(xc_rdy, 3)
                blocks(1)

        stream(dve, "wi", into_heads, straight=True)
        n = START["wt"]
        next_lo(n, n % 2, WIDTH["wv"])
        dve.wait_ge(mm_done, n + 1)
        V.tensor_copy(P2[:, 20, :], PS[:, 4 * (n % 2), 0:SEQ]).then_inc(evac, 1)
        gate_silu(8)
        n = START["wv"]
        next_lo(n, n % 2, WIDTH["wv"])
        next_lo(n + 1, (n + 1) % 2, WIDTH["wo2"])
        gate_silu(9)
        gate_silu(10)
        dve.wait_ge(mm_done, n + 2)
        V.tensor_copy(VT[:, :, :], PS[:, 4:8, 0:TOKEN_COLS]).then_inc(evac, 2)
        dve.wait_ge(evac, START["wo2"])
        TT(GATE[:, :, :], VT[:, :, 384:408], col("bg", 0, 24).unsqueeze(1).to_broadcast([P, QT, 24]),
           ALU.add).then_inc(bg_d, 1)
        dve.wait_ge(bg_a, 1)
        chain(TS(GATE[:, :, :], GATE[:, :, :], 1.0, 0.5, ALU.add, ALU.mult))
        chain(TS(NSINK[:, :], col("sink", 0, 8), -1.0, None, ALU.mult))
        dve.wait_ge(hc_ps, 1)
        dve.wait_ge(hc_t, 1)
        B62 = 2 * NCMP
        STT(HCT[0:B62, :, :], HTN[0:B62, :, :], 1.0, PS[0:B62, 0:2, 0:256], ALU.add, ALU.mult).then_inc(hc_x, 1)
        dve.wait_ge(hc_tp, 1)
        V.tensor_copy(HC[:, :, 0:B62], PS[:, 4, 0:256].rearrange("p (i n) -> p i n", i=4)[:, :, 0:B62])\
            .then_inc(hc_rdy, 1)
        dve.wait_ge(kc_ps, 1)
        TS(KCF[:, 0:NCMP], PS[:, 0, 0:NCMP], 0.5, None, ALU.mult).then_inc(kc_f, 1)
        TS(VCF[:, :, :], PS[0:NCMP, 1, 0:P].rearrange("p (g d) -> p g d", g=2), 0.5, None, ALU.mult)\
            .then_inc(dve_chain, 1)
        chain.n += 1
        dve.wait_ge(dve_chain, chain.n)
        dve.wait_ge(kc_r, 1)
        dve.wait_ge(kc_f, 1)
        STT(KCF[:, 0:NCMP], KCF[:, 0:NCMP], col("kc"), PRS[:, 0, 0:NCMP], ALU.mult, ALU.mult)\
            .then_inc(kc_rdy, 1)
        def masks(name):
            m = tab(name, 0, QT * NCMP).rearrange("p (q n) -> p q n", q=QT)
            return m.unsqueeze(2).to_broadcast([P, QT, 4, NCMP])

        def tiles(ap):
            return ap.rearrange("p (q h) n -> p q h n", q=QT)

        def heads(ap):
            return ap.unsqueeze(2).to_broadcast([P, 4 * NH, NCMP])

        dve.wait_ge(dt_ld, 32)
        for h in range(NH):
            TT(DT[:, h, :], DT[:, h, :], tab("mA", 0, 256), ALU.add)
            last = STT(DT[:, 8 + h, :], DT[:, 8 + h, :], B31[:, 8 + h:9 + h], tab("mB", 0, 256),
                       ALU.subtract, ALU.add)
        chain(last)
        dve.sem_inc(dt_rdy, 1)
        dve.wait_ge(cs_ps, 1)
        for g in range(2):
            last = TT(tiles(CPB[:, 16 * g:16 * g + 16, :]),
                      PS[:, g, 0:16 * NCMP].rearrange("p (q h n) -> p q h n", q=QT, h=4), masks("cneg"), ALU.add)
        chain(last)
        chain(V.tensor_reduce(M8[:, 0, :], CPB[:, :, :], AX.X, ALU.max))
        TT(CPB[:, :, :], CPB[:, :, :], heads(M8[:, 0, :]), ALU.subtract).then_inc(cs_z, 1)
        dve.wait_ge(cs_e, 1)
        for g in range(2):
            last = TT(tiles(CPB[:, 16 * g:16 * g + 16, :]), tiles(CPB[:, 16 * g:16 * g + 16, :]),
                      masks("c01"), ALU.mult)
        last.then_inc(cs_p, 1)
        dve.wait_ge(cs_p, 1)
        chain(V.tensor_reduce(M8[:, 1, :], CPB[:, :, :], AX.X, ALU.add))
        chain(TS(M8[:, 1, :], M8[:, 1, :], 1e-30, None, ALU.max))
        chain(V.reciprocal(M8[:, 2, :], M8[:, 1, :]))
        for g in range(2):
            rows = slice(16 * g, 16 * g + 16)
            last = TT(M8[:, 3, rows].rearrange("p (q h) -> p q h", q=QT),
                      M8[:, 2, rows].rearrange("p (q h) -> p q h", q=QT),
                      GATE[:, :, :].rearrange("p q (h b) -> p b q h", b=3)[:, 0, :, 4 * g:4 * g + 4], ALU.mult)
        chain(last)
        for qi in range(QT):
            dve.wait_ge(co_ps, qi + 1)
            for g in range(2):
                last = TT(OC[:, qi, 256 * g:256 * (g + 1)].rearrange("p (h d) -> p h d", h=4),
                          PS[:, 6 + qi % 2, 256 * g:256 * (g + 1)].rearrange("p (h d) -> p h d", h=4),
                          M8[:, 3, 16 * g + 4 * qi:16 * g + 4 * qi + 4].unsqueeze(2).to_broadcast([P, 4, CH]),
                          ALU.mult)
            last.then_inc(co_rdy, 1)
        dve.wait_ge(co_rdy, QT)
        attention(1)

        def last_product(n, j, turn, slot, nxt):
            next_lo(n, slot, nxt)
            dve.wait_ge(mm_done, n + 1)
            for t in range(2):
                h = H[:, bass.ds(2 * j + t, 1), N_META:T1] if not isinstance(j, int) else \
                    H[:, 2 * j + t:2 * j + t + 1, N_META:T1]
                m = MOD[:, bass.ds(2 * j + 16 + t, 1)] if not isinstance(j, int) else \
                    MOD[:, 2 * j + 16 + t:2 * j + 17 + t]
                last = STT(h, PS[:, 4 * slot + t:4 * slot + t + 1, 0:SEQ], m, h, ALU.mult, ALU.add)
                if t == 0:
                    last.then_inc(dve_chain, 1)
            last.then_inc(evac, 1)

        stream(dve, "wo2", last_product)

    ctx.close()


def tables():
    t = np.zeros((P, NTAB), np.float32)

    def put(name, a):
        t[:a.shape[0], TABS[name]:TABS[name] + a.shape[1]] = a

    p = np.arange(P)
    put("ident", np.eye(P))
    put("ones", np.ones((P, P)))
    put("bones", (p[:, None] // CH == p[None] // CH).astype(np.float32))
    pos = np.arange(T1, dtype=np.float32)
    inv = np.float32(10000.0) ** (-np.arange(0, 32, 2, dtype=np.float32) / np.float32(32))
    ang = (pos[:, None] * inv[None, :]).astype(np.float32)
    put("cos", np.cos(ang).T[p % 16])
    put("sin", np.sin(ang).T[p % 16] * np.where(p % 32 < 16, -1, 1)[:, None])
    k = np.arange(256)
    dist = P + p[:, None] - k[None]
    put("mA", np.where((dist >= 0) & (dist < P), 0, NEG))
    put("mB", np.where(dist >= 0, 0, NEG))
    n = np.arange(NCMP)
    ok = np.stack([(16 * n[None] + 31) <= (P * q + p[:, None]) for q in range(QT)], 1).reshape(P, -1)
    put("cneg", np.where(ok, 0, NEG))
    put("c01", ok.astype(np.float32))
    s, c = (p % CH)[:, None], np.arange(CH)[None]
    put("i64", (s == c).astype(np.float32))
    put("mincl", (c >= s).astype(np.float32))
    put("mstrict", (c > s).astype(np.float32))
    put("lvl", np.concatenate([((s // (2 << l) == c // (2 << l)) & (s // (1 << l) % 2 == 0)
                                & (c // (1 << l) % 2 == 1)).astype(np.float32) for l in range(LEVELS)], 1))
    sel = np.zeros((40, 4 * P), np.float32)
    for h in range(NH):
        sel[h, P * (h // 2) + CH * (h % 2):P * (h // 2) + CH * (h % 2 + 1)] = 1
    sel[32:40] = sel[0:8]
    put("sel", sel)
    d = 255 - np.arange(383)
    nn = np.maximum(d, 0)
    nf = np.maximum(nn, 1).astype(np.float32)
    large = 16 + (np.log(nf / np.float32(16)) / np.float32(np.log(8.0)) * np.float32(16)).astype(np.int32)
    bucket = np.where(nn < 16, nn, np.minimum(large, 31))
    put("oh", (np.arange(32)[:, None] == bucket[None]).astype(np.float32))
    return t


def tiled(w):
    k, n = w.shape
    return np.ascontiguousarray(w.reshape(k // P, P, n // P, P).transpose(2, 1, 0, 3).reshape(n // P, P, k))


def pairs(t):
    n, p, k = t.shape
    return np.ascontiguousarray(t.reshape(n // 2, 2, p, k).transpose(0, 2, 1, 3).reshape(n // 2, p, 2 * k))


def lay_out(x):
    a = {}
    h = np.concatenate([x["meta_tokens"], x["x"][0]], axis=0)
    a["h"] = np.ascontiguousarray(h.T.reshape(KD, P, T1))
    a["tabs"] = tables()
    for f in (1, 2):
        g, u, d = (tiled(x[f"ffn{f}_w_{n}"][0]) for n in ("gate", "up", "down"))
        for half in range(2):
            js = slice(half * FH, (half + 1) * FH)
            a[f"f{f}u{half}"] = np.ascontiguousarray(np.concatenate([g[js], u[js]], axis=2))
            a[f"f{f}d{half}"] = np.ascontiguousarray(d[:, :, half * FH * P:(half + 1) * FH * P])
    w = x["w_in"][0]
    misc = np.zeros((D_MODEL, P), np.float32)
    kr = w[:, 384:416]
    misc[:, 0:8], misc[:, 32:40], misc[:, 64:96] = w[:, 1952:1960], w[:, 1960:1968], kr
    misc[:, 96:112], misc[:, 112:128] = kr[:, 16:32], kr[:, 0:16]
    a["w1"] = pairs(tiled(np.concatenate([w[:, 0:384], misc, w[:, 416:1952]], axis=1)))
    a["z"] = pairs(tiled(w[:, 1968:2480]))
    gm, gg = tiled(w[:, 2480:3504]), tiled(w[:, 3504:4528])
    mo, go = tiled(x["w_mla_o"][0]), tiled(x["w_gdn_o"][0])
    mg = np.zeros((16, P, SLOT), np.float32)
    mg[0::2] = np.concatenate([gm, gg], axis=2)
    mg[1::2, :, 0:SLOT // 2] = np.concatenate([mo, go], axis=2)
    a["mg"] = mg
    uq = x["w_uq"][0].reshape(256, NH, 96)
    rope = uq[:, :, 64:96]
    swap = np.concatenate([rope[:, :, 16:32], rope[:, :, 0:16]], axis=2)
    a["uq"] = tiled(np.concatenate([uq[:, :, 0:64].reshape(256, 512), rope.reshape(256, 256),
                                    swap.reshape(256, 256)], axis=1)).transpose(1, 0, 2).reshape(1, P, SLOT)
    ukv = x["w_ukv"][0].reshape(P, NH, 128)
    a["ukv"] = np.concatenate([ukv[:, :, 0:64].reshape(P, 512), ukv[:, :, 64:128].reshape(P, 512)], axis=1)[None]
    a["wo"] = pairs(tiled(x["w_out"][0]))
    w = x["w_in_2"][0]
    at = np.cumsum([0, 512, 128, 128, 512, 512, 128, 128, 128, 128, 128, 128, 512, 24])
    qa, ka, va, za, qb, kc, vc, ks, vs, kw, vw, zb, gb = (w[:, at[i]:at[i + 1]] for i in range(13))

    def heads(q):
        return q.reshape(D_MODEL, 2, 4, CH).transpose(0, 2, 1, 3).reshape(D_MODEL, 512)

    t = tiled(np.concatenate([heads(qa), heads(qb), ka, ks, kw, kc, vc, za, zb], axis=1))
    a["wi"], a["wt"] = pairs(t[:20]), t[20:21]
    wv = np.concatenate([va, vs, vw, gb], axis=1)
    a["wv"] = wv.reshape(2, 4, P, TOKEN_COLS).transpose(0, 2, 1, 3).reshape(2, P, 4 * TOKEN_COLS)
    a["wo2"] = pairs(tiled(x["w_out_2"][0]))
    for n in ("k", "v"):
        a["w1" + n] = x[f"w_cmp_{n}1_2"][0].reshape(16, P, 256).transpose(1, 0, 2)
    a["w2"] = np.stack([x[f"w_cmp_{n}2_2"][0].reshape(2, P, CH).transpose(1, 0, 2) for n in ("k", "v")], axis=1)
    a["ada"] = x["w_ada_2"][0].T.reshape(24, P, D_MODEL)
    a["c"] = x["c_2"][0]
    a["rel"] = x["rel_bias_2"]
    c = np.zeros((P, NCOLS), np.float32)

    def put(name, v):
        c[:, COLS[name]:COLS[name] + v.shape[1]] = v

    for name, key in (("ffn1", "ffn1_norm"), ("mix", "mix_norm"), ("ffn2", "ffn2_norm"),
                      ("fin", "final_norm"), ("ng2", "norm_gain_2"), ("qn", "q_norm"),
                      ("kvn", "kv_norm"), ("bada", "b_ada_2")):
        put(name, x[key].reshape(-1, P).T)
    for name, key in (("gdn", "gdn_norm"), ("qa", "q_gain_a_2"), ("qb", "q_gain_b_2"), ("ka", "k_gain_a_2"),
                      ("ks", "k_gain_sel_2"), ("kw", "k_gain_win_2"), ("kc", "k_gain_cmp_2")):
        put(name, np.tile(x[key][0], 2)[:, None])
    put("conv", x["conv_w"][0].reshape(4, 12, P).transpose(2, 1, 0).reshape(P, 48))
    c[32:40, COLS["dtb"]], c[32:40, COLS["alog"]] = x["dt_bias"][0], x["a_log"][0]
    put("sink", np.broadcast_to(x["sinks_2"][0], (P, 8)))
    put("bg", np.broadcast_to(x["b_nsa_gate_2"][0], (P, 24)))
    put("posk", x["cmp_pos_k_2"][0].reshape(16, P).T)
    put("posv", x["cmp_pos_v_2"][0].reshape(16, P).T)
    a["cols"] = c
    return {k: np.ascontiguousarray(v) for k, v in a.items()}


def program(nc, shapes):
    io = {n: nc.dram_tensor("in_" + n, s, mybir.dt.float32, kind="ExternalInput").ap()
          for n, s in shapes.items()}
    io["rev"] = nc.dram_tensor("rev", [16, P, 384], mybir.dt.float32).ap()
    io["rev0"] = nc.dram_tensor("rev0", [16], mybir.dt.float32).ap()
    io["out"] = nc.dram_tensor("out", [KD, P, SEQ], mybir.dt.float32, kind="ExternalOutput").ap()
    build(nc, io)


def kernel(**inputs):
    import concourse.bacc as bacc
    from concourse.bass_utils import run_bass_kernel_spmd

    arrays = lay_out({k: np.asarray(v) for k, v in inputs.items()})
    nc = bacc.Bacc("TRN2", target_bir_lowering=False, num_devices=1)
    program(nc, {k: list(v.shape) for k, v in arrays.items()})
    r = run_bass_kernel_spmd(nc, [{"in_" + k: v for k, v in arrays.items()}], core_ids=[0])
    out = r.results[0]["out"]
    return np.ascontiguousarray(out.reshape(D_MODEL, SEQ).T)[None]
```
